# Optimizing a Trainium2 kernel written in Bass

```python
import jax, jax.numpy as jnp
from jax import lax
import numpy as np

D_MODEL = 1024
BATCH = 1
SEQ = 512
DEPTH = 2

N_MIXERS = 2
HEAD_DIM = 64
N_HEADS = D_MODEL // HEAD_DIM
FOX_HEADS = N_HEADS
DSA_Q_HEADS = N_HEADS
DSA_KV_HEADS = 4
GROUP = DSA_Q_HEADS // DSA_KV_HEADS
IDX_HEADS = 8
IDX_DIM = 64
TOPK_MAX = 256
Q_BLOCK = 128
D_FF = 2816
CONV_WIDTH = 3
EPS = 1e-6
FORGET_BIAS = 3.0
N_FOX_LAYERS = (DEPTH + 1) // 2
N_DSA_LAYERS = DEPTH // 2

FOX_IN = 3 * FOX_HEADS * HEAD_DIM + FOX_HEADS
DSA_QW = DSA_Q_HEADS * HEAD_DIM
DSA_KVW = DSA_KV_HEADS * HEAD_DIM
DSA_SPLITS = [DSA_QW, DSA_QW + DSA_KVW, DSA_QW + 2 * DSA_KVW,
              DSA_QW + 2 * DSA_KVW + IDX_HEADS * IDX_DIM,
              DSA_QW + 2 * DSA_KVW + IDX_HEADS * IDX_DIM + IDX_DIM]
DSA_IN = DSA_SPLITS[-1] + IDX_HEADS

kernel_name = 'hybrid_fox_dsa_convffn'

def rms_norm(x, g):
    xf = x.astype(jnp.float32)
    y = xf * lax.rsqrt(jnp.mean(xf * xf, axis=-1, keepdims=True) + EPS)
    return (y * g.astype(jnp.float32)).astype(x.dtype)

def modulate(x, g, shift, scale):
    return rms_norm(x, g) * (1 + scale[:, None, :]) + shift[:, None, :]

def alibi_slopes(n):
    return jnp.exp2(-8.0 * jnp.arange(1, n + 1, dtype=jnp.float32) / n)

def to_blocks(a):
    b, l = a.shape[:2]
    return jnp.moveaxis(a.reshape(b, l // Q_BLOCK, Q_BLOCK, *a.shape[2:]), 1, 0)

def from_blocks(a):
    nb, b, q = a.shape[:3]
    return jnp.moveaxis(a, 0, 1).reshape(b, nb * q, *a.shape[3:])

def forgetting_attention(h, w_in, b_f, g_q, g_k, w_out):
    b, l, _ = h.shape
    dq = FOX_HEADS * HEAD_DIM
    q, k, v, f_logit = jnp.split(h @ w_in, [dq, 2 * dq, 3 * dq], axis=-1)
    q = rms_norm(q.reshape(b, l, FOX_HEADS, HEAD_DIM), g_q)
    k = rms_norm(k.reshape(b, l, FOX_HEADS, HEAD_DIM), g_k).astype(jnp.float32)
    v = v.reshape(b, l, FOX_HEADS, HEAD_DIM)
    log_f = jax.nn.log_sigmoid((f_logit + b_f).astype(jnp.float32))
    cum = jnp.cumsum(log_f, axis=1)
    cum_k = jnp.transpose(cum, (0, 2, 1))
    pos = jnp.arange(l)
    scale = HEAD_DIM ** -0.5

    def block(args):
        qb, cqb, pb = args
        s = jnp.einsum('bqhd,bkhd->bhqk', qb.astype(jnp.float32), k) * scale
        s = s + jnp.transpose(cqb, (0, 2, 1))[..., None] - cum_k[:, :, None, :]
        s = jnp.where(pos[None, :] <= pb[:, None], s, -jnp.inf)
        p = jax.nn.softmax(s, axis=-1)
        return jnp.einsum('bhqk,bkhd->bqhd', p.astype(v.dtype), v)

    o = lax.map(block, (to_blocks(q), to_blocks(cum), pos.reshape(-1, Q_BLOCK)))
    o = from_blocks(o).reshape(b, l, dq)
    return o @ w_out

def sparse_indexed_attention(h, w_in, g_q, g_k, g_kidx, w_out):
    b, l, _ = h.shape
    top_k = min(TOPK_MAX, l // 4)
    q, k, v, q_idx, k_idx, w_idx = jnp.split(h @ w_in, DSA_SPLITS, axis=-1)
    q = rms_norm(q.reshape(b, l, DSA_KV_HEADS, GROUP, HEAD_DIM), g_q)
    k = rms_norm(k.reshape(b, l, DSA_KV_HEADS, HEAD_DIM), g_k)
    v = v.reshape(b, l, DSA_KV_HEADS, HEAD_DIM)
    q_idx = q_idx.reshape(b, l, IDX_HEADS, IDX_DIM)
    k_idx = rms_norm(k_idx, g_kidx).astype(jnp.float32)
    w_idx = w_idx.astype(jnp.float32) * (IDX_HEADS ** -0.5 * IDX_DIM ** -0.5)
    slopes = alibi_slopes(DSA_Q_HEADS).reshape(DSA_KV_HEADS, GROUP)
    pos = jnp.arange(l)
    scale = HEAD_DIM ** -0.5
    gather = jax.vmap(lambda a, i: a[i])

    def block(args):
        qb, qib, wib, pb = args
        rel = jax.nn.relu(jnp.einsum('bqhd,bkd->bqhk', qib.astype(jnp.float32), k_idx))
        score = jnp.einsum('bqhk,bqh->bqk', rel, wib)
        score = jnp.where(pos[None, None, :] <= pb[None, :, None], score, -jnp.inf)
        _, idx = lax.top_k(score, top_k)
        valid = idx <= pb[None, :, None]
        k_sel = gather(k, idx).astype(jnp.float32)
        v_sel = gather(v, idx)
        s = jnp.einsum('bqgrd,bqkgd->bqgrk', qb.astype(jnp.float32), k_sel) * scale
        dist = (pb[None, :, None] - idx).astype(jnp.float32)
        s = s - slopes[None, None, :, :, None] * dist[:, :, None, None, :]
        s = jnp.where(valid[:, :, None, None, :], s, -jnp.inf)
        p = jax.nn.softmax(s, axis=-1)
        return jnp.einsum('bqgrk,bqkgd->bqgrd', p.astype(v_sel.dtype), v_sel)

    o = lax.map(block, (to_blocks(q), to_blocks(q_idx), to_blocks(w_idx),
                        pos.reshape(-1, Q_BLOCK)))
    o = from_blocks(o).reshape(b, l, DSA_QW)
    return o @ w_out

def conv_gated_mlp(h, w_up, conv_w, conv_b, w_down):
    a, g = jnp.split(h @ w_up, 2, axis=-1)
    a = lax.conv_general_dilated(a, conv_w[:, None, :], window_strides=(1,),
                                 padding=[(CONV_WIDTH - 1, 0)],
                                 dimension_numbers=('NWC', 'WIO', 'NWC'),
                                 feature_group_count=D_FF) + conv_b
    return (jax.nn.silu(a) * g) @ w_down

def setup_inputs(seed: int = 0) -> dict:
    key = jax.random.key(seed)
    ks = jax.random.split(key, 24)
    f32 = jnp.float32

    def dense(k, shape, fan_in, mult=1.0):
        return jax.random.normal(k, shape, f32) * (mult * fan_in ** -0.5)

    def gain(k, shape):
        return 1.0 + 0.02 * jax.random.normal(k, shape, f32)

    return {
        'x': jax.random.normal(ks[0], (BATCH, SEQ, D_MODEL), f32),
        'c': jax.random.normal(ks[1], (BATCH, D_MODEL), f32),
        'w_ada': dense(ks[2], (DEPTH, D_MODEL, 6 * D_MODEL), D_MODEL, 0.5),
        'b_ada': 0.01 * jax.random.normal(ks[3], (DEPTH, 6 * D_MODEL), f32),
        'g_norm_mix': gain(ks[4], (DEPTH, D_MODEL)),
        'g_norm_ffn': gain(ks[5], (DEPTH, D_MODEL)),
        'fox_w_in': dense(ks[6], (N_FOX_LAYERS, D_MODEL, FOX_IN), D_MODEL),
        'fox_b_f': FORGET_BIAS + 0.1 * jax.random.normal(ks[7], (N_FOX_LAYERS, FOX_HEADS), f32),
        'fox_g_q': gain(ks[8], (N_FOX_LAYERS, HEAD_DIM)),
        'fox_g_k': gain(ks[9], (N_FOX_LAYERS, HEAD_DIM)),
        'fox_w_out': dense(ks[10], (N_FOX_LAYERS, FOX_HEADS * HEAD_DIM, D_MODEL), FOX_HEADS * HEAD_DIM),
        'dsa_w_in': dense(ks[11], (N_DSA_LAYERS, D_MODEL, DSA_IN), D_MODEL),
        'dsa_g_q': gain(ks[12], (N_DSA_LAYERS, HEAD_DIM)),
        'dsa_g_k': gain(ks[13], (N_DSA_LAYERS, HEAD_DIM)),
        'dsa_g_kidx': gain(ks[14], (N_DSA_LAYERS, IDX_DIM)),
        'dsa_w_out': dense(ks[15], (N_DSA_LAYERS, DSA_QW, D_MODEL), DSA_QW),
        'ffn_w_up': dense(ks[16], (DEPTH, D_MODEL, 2 * D_FF), D_MODEL),
        'ffn_conv_w': dense(ks[17], (DEPTH, CONV_WIDTH, D_FF), CONV_WIDTH),
        'ffn_conv_b': 0.01 * jax.random.normal(ks[18], (DEPTH, D_FF), f32),
        'ffn_w_down': dense(ks[19], (DEPTH, D_FF, D_MODEL), D_FF),
    }

def reference(x, c, w_ada, b_ada, g_norm_mix, g_norm_ffn, fox_w_in, fox_b_f, fox_g_q,
              fox_g_k, fox_w_out, dsa_w_in, dsa_g_q, dsa_g_k, dsa_g_kidx, dsa_w_out,
              ffn_w_up, ffn_conv_w, ffn_conv_b, ffn_w_down):
    c_act = jax.nn.silu(c)
    for i in range(DEPTH):
        mod = c_act @ w_ada[i] + b_ada[i]
        sh1, sc1, gt1, sh2, sc2, gt2 = jnp.split(mod, 6, axis=-1)
        h = modulate(x, g_norm_mix[i], sh1, sc1)
        j = i // N_MIXERS
        if i % N_MIXERS == 0:
            y = forgetting_attention(h, fox_w_in[j], fox_b_f[j], fox_g_q[j], fox_g_k[j], fox_w_out[j])
        else:
            y = sparse_indexed_attention(h, dsa_w_in[j], dsa_g_q[j], dsa_g_k[j], dsa_g_kidx[j], dsa_w_out[j])
        x = x + gt1[:, None, :] * y
        h = modulate(x, g_norm_ffn[i], sh2, sc2)
        x = x + gt2[:, None, :] * conv_gated_mlp(h, ffn_w_up[i], ffn_conv_w[i], ffn_conv_b[i], ffn_w_down[i])
    return x


_drawn_inputs = setup_inputs


def setup_inputs(seed=0):
    import zlib

    import numpy as np

    out = dict(_drawn_inputs(seed))
    spreads = {}
    factors = {'g_norm_ffn': 3.821,
     'fox_b_f': 28.328,
     'fox_g_q': 7.79,
     'fox_g_k': 6.145,
     'dsa_g_q': 33.493,
     'dsa_g_k': 31.774,
     'dsa_g_kidx': 10.534,
     'ffn_conv_b': 5.371}
    for name, (base, spread) in spreads.items():
        noise = np.random.default_rng([zlib.crc32(name.encode()), seed]).standard_normal(out[name].shape)
        drawn = base * np.exp(spread * noise) if base else spread * noise
        out[name] = __import__('jax').numpy.asarray(drawn.astype(out[name].dtype))
    for name, factor in factors.items():
        out[name] = (out[name] * factor).astype(out[name].dtype)
    return out
```

```python
from contextlib import ExitStack

import concourse.bass as bass
from concourse import mybir

F32 = mybir.dt.float32
F32R = mybir.dt.float32r
ALU = mybir.AluOpType
ACT = mybir.ActivationFunctionType
AX_X = mybir.AxisListType.X
ds = bass.ds

P = 128
D = 1024
L = 512
FT = D // P
TT = L // P
HD = 64
NH = D // HD
NKV = 4
IH = 8
TOPK = L // 4
FF = 2816
UT = FF // P
EPS = 1e-6
MASKED = -3.0e38
TAKEN = -3.4028235e38

C_ID, C_CAUSAL, C_BLOCK, C_EVEN, C_ODD, C_HEAD, C_ONE, C_EPS, C_N = 0, 128, 256, 258, 259, 260, 276, 277, 278

FOX_IN, FOX_OUT, FOX_UP, FOX_DOWN = 0, 12, 16, 38
DSA_IDX, DSA_K, DSA_Q, DSA_V, DSA_OUT, DSA_UP, DSA_DOWN = 49, 51, 52, 56, 57, 61, 83
LOADS = 94
UNIT = 1024

V_CONVW, V_CONVB, V_GMIX, V_GFFN, V_ROWS = 0, 66, 88, 96, 104
V_BADA, V_C = 0, 96
G_FOXQ, G_FOXK, G_DSAQ, G_DSAK, G_KIDX, G_BF, G_ROWS = 0, 1, 2, 3, 4, 5, 6
GAIN = [0, 16]


def two_layers(nc, x, c, w_ada, b_ada, g_norm_mix, g_norm_ffn, fox_w_in, fox_b_f, fox_g_q, fox_g_k,
               fox_w_out, dsa_w_in, dsa_g_q, dsa_g_k, dsa_g_kidx, dsa_w_out, ffn_w_up, ffn_conv_w,
               ffn_conv_b, ffn_w_down, consts, alibi, out):
    ctx = ExitStack()
    with ctx:
        def sem(name):
            return ctx.enter_context(nc.semaphore(name))

        def sems(name, n):
            return [sem(f"{name}{i}") for i in range(n)]

        def sb(name, shape, dt=F32, stack=ctx):
            return stack.enter_context(nc.sbuf_tensor(name, shape, dt))

        xT = sb("xT", [P, FT, L])
        hh = sb("hh", [P, FT, L], F32R)
        hl = sb("hl", [P, FT, L], F32R)
        raw = sb("raw", [P, 2, 2 * UNIT])
        wh = sb("wh", [P, 4, UNIT], F32R)
        wl = sb("wl", [P, 4, UNIT], F32R)
        ada_raw = sb("ada_raw", [P, 2, D])
        ada_acc = sb("ada_acc", [P, D])
        nt = sb("nt", [P, 4, L])
        rbs = sb("rbs", [P, L])
        cst = sb("cst", [P, C_N])
        ident_r = sb("ident_r", [P, P], F32R)
        causal_r = sb("causal_r", [P, P], F32R)
        vec = sb("vec", [P, 4, P])
        csil = sb("csil", [P, FT])
        mod = sb("mod", [P, 12, FT])
        mulA = sb("mulA", [P, 4, FT])
        gains = sb("gains", [P, 32])
        rv = sb("rv", [P, 8])
        rln = sb("rln", [P, 8])
        ry = sb("ry", [P, 8])
        ra = sb("ra", [P, 8])
        rb2 = sb("rb2", [P, 8])
        nmax = sb("nmax", [P, 16])
        rowsum = sb("rowsum", [P, 16])
        rrec = sb("rrec", [P, 16])
        widx = sb("widx", [P, TT * IH])
        top8 = sb("top8", [P, 3, 8])
        ident = cst[:, C_ID:C_ID + P]

        with ExitStack() as att:
            qk = sb("qk", [P, 16, L], stack=att)
            probs = sb("probs", [P, 2, L], stack=att)
            probsT = sb("probsT", [P, 2, L], stack=att)
            oP = sb("oP", [P, 2, TT, P], stack=att)
            biasq = sb("biasq", [P, L], F32R, stack=att)
            biask = sb("biask", [P, L], stack=att)
            biaskh = sb("biaskh", [P, 2, L], F32R, stack=att)
            cum = sb("cum", [P, L], stack=att)
            cumh = sb("cumh", [P, L], F32R, stack=att)
            with ExitStack() as proj:
                sqb = sb("sqb", [P, 2, L], stack=proj)
                qg = sb("qg", [P, 2, L], stack=proj)
                smr0 = sb("smr0", [P, FT, 16], stack=proj)
                smh0 = sb("smh0", [P, FT, P], F32R, stack=proj)
                sml0 = sb("sml0", [P, FT, P], F32R, stack=proj)
            with ExitStack() as proj:
                sb("sqb_qg", [P, 4, L], stack=proj)
                smr1 = sb("smr1", [P, FT, 72], stack=proj)
                smh1 = sb("smh1", [P, FT, 136], F32R, stack=proj)
                sml1 = sb("sml1", [P, FT, 136], F32R, stack=proj)
            with ExitStack() as heads:
                qSh = sb("qSh", [P, 2, L], F32R, stack=heads)
                qSl = sb("qSl", [P, 2, L], F32R, stack=heads)
                kSh = sb("kSh", [P, 2, L], F32R, stack=heads)
                kSl = sb("kSl", [P, 2, L], F32R, stack=heads)
            sb("below_values", [P, 5 * 1024], stack=att)
            with ExitStack() as fox:
                v0 = sb("v0", [P, TT, D], stack=fox)
            with ExitStack() as dsa:
                v1 = sb("v1", [P, TT, NKV * HD], stack=dsa)
                score = sb("score", [P, 3, L], stack=dsa)
                masked = sb("masked", [P, TT, L], F32R, stack=dsa)
        qidx = qk[:, 12:16, :]
        kidx = oP[:, 0, :, :].rearrange("p t d -> p (t d)")
        with ExitStack() as mlp:
            uh = sb("uh", [P, UT, L], F32R, stack=mlp)
            ul = sb("ul", [P, UT, L], F32R, stack=mlp)
            cv = sb("cv", [P, 2, L], stack=mlp)
        with ExitStack() as ends:
            xtok = sb("xtok", [P, TT, D], stack=ends)
            vrows = sb("vrows", [P, 4, P], stack=ends)
        with ExitStack() as ends2:
            outs = sb("outs", [P, TT, D], stack=ends2)

        bank = [ctx.enter_context(nc.psum_tensor(f"bank{i}", [P, 512], F32)) for i in range(8)]
        ST, RB, MISC, ADA = bank[4], bank[5], bank[6], bank[7]

        cst_in, vec_in, x_in, alibi_in, out_done = (sem(n) for n in ("cst_in", "vec_in", "x_in", "alibi_in", "out_done"))
        raw_in = sems("raw_in", 2)
        w_hi = sem("w_hi")
        w_split = sem("w_split")
        unit_used = sem("unit_used")
        ada_in = sems("ada_in", 2)
        ada_used = sem("ada_used")
        ada_sum = sem("ada_sum")
        ada_done = sem("ada_done")
        vecT_ready, vec_done, csil_done = sem("vecT_ready"), sem("vec_done"), sem("csil_done")
        cst_done, xT_ready = sem("cst_done"), sem("xT_ready")
        x_done = sems("x_done", 5)
        sq_ready = sem("sq_ready")
        sq_added = sem("sq_added")
        ms_ready = sem("ms_ready")
        nD = sem("nD")
        nA = sem("nA")
        rms_ready = sem("rms_ready")
        t_ready, hf_ready, h_ready = sem("t_ready"), sem("hf_ready"), sem("h_ready")
        mul_ready = sem("mul_ready")
        sm_in, sm_hi, sm_ready = sems("sm_in", 2), sems("sm_hi", 2), sems("sm_ready", 2)
        tile_ready = sems("tile_ready", 2)
        kidx_ready = sem("kidx_ready")
        taken = sems("taken", 2)
        hsq_ready = sems("hsq_ready", 2)
        hms_ready = sems("hms_ready", 2)
        hD, hA = sems("hD", 2), sems("hA", 2)
        hrs_ready = sems("hrs_ready", 2)
        hrb_ready = sems("hrb_ready", 2)
        normed = sems("normed", 2)
        v_ready = sems("v_ready", 2)
        f_ready, f_act, f_dve = sem("f_ready"), sem("f_act"), sem("f_dve")
        bias_step = sems("bias_step", 2)
        bias_ready = sems("bias_ready", 2)
        w_ready, w_taken = sem("w_ready"), sem("w_taken")
        is_ready, relu_done, weighed, tk, mask_ready = (sem(n) for n in ("is_ready", "relu_done", "weighed", "tk", "mask_ready"))
        qk_high, qs_ready, kb_ready = sem("qk_high"), sem("qs_ready"), sem("kb_ready")
        s_ready, max_done, p_ready = sem("s_ready"), sem("max_done"), sem("p_ready")
        pt_ready, ptd_done, pta_done = sem("pt_ready"), sem("ptd_done"), sem("pta_done")
        pv_done, rec_done, o_done = sem("pv_done"), sem("rec_done"), sem("o_done")
        ot_ready, oh_done, ol_done = sem("ot_ready"), sem("oh_done"), sem("ol_done")
        y_ready = sems("y_ready", 4)
        a_ready, g_ready = sems("a_ready", 2), sems("g_ready", 2)
        tap2, tap1, conv_done, silu_done = sems("tap2_", 2), sems("tap1_", 2), sems("conv_done", 2), sems("silu_done", 2)
        uf_done, uh_done, u_done = sems("uf_done", 2), sems("uh_done", 2), sems("u_done", 2)
        oT_ready, oT_done = sem("oT_ready"), sem("oT_done")
        waits_passed = sem("waits_passed")

        block = ctx.enter_context(nc.Block())

        def wait_alone(eng, semaphore, count):
            eng.wait_ge(semaphore, count)
            eng.sem_inc(waits_passed, 1)

        def half(tensor, h):
            return tensor[64 * (h % 2):64 * (h % 2) + 64]

        def pair_tiles(l, g, p):
            return qk[:, ds(2 * g + p, 1), :], qk[:, ds(8 + (2 * g + p if l == 0 else g), 1), :]

        @block.sync
        def _(sp):
            def load(n, slot, src, first=False):
                if not first:
                    sp.wait_ge(w_split, 2 * n - 2)
                dst = raw[:, slot, :]
                sp.dma_start(dst.rearrange("p (k c) -> p k c", k=src.shape[1]), src).then_inc(raw_in[slot], 16)

            def load_cols(n, slot, w, col, first=False):
                load(n, slot, w.rearrange("(k p) c -> p k c", p=P)[:, :, ds(col, 256)], first)

            def load_rows(n, slot, w, k):
                load(n, slot, w.rearrange("(k p) c -> p k c", p=P)[:, ds(k, 2), :])

            def ada_chunk(layer, q, part, first=False):
                for k in range(FT):
                    if not (first and k < 2):
                        sp.wait_ge(ada_used, 8 * q + k - 1)
                    sp.dma_start(ada_raw[:, k % 2, :], w_ada[layer, k * P:(k + 1) * P, ds(part * D, D)]).then_inc(ada_in[k % 2], 16)

            sp.dma_start(cst[:], consts).then_inc(cst_in, 16)
            for l in range(2):
                sp.dma_start(vrows[V_CONVW:V_CONVB, l, :], ffn_conv_w[l].rearrange("w (m p) -> (w m) p", p=P)).then_inc(vec_in, 16)
                sp.dma_start(vrows[V_CONVB:V_GMIX, l, :], ffn_conv_b[l].rearrange("(m p) -> m p", p=P)).then_inc(vec_in, 16)
                sp.dma_start(vrows[V_GMIX:V_GFFN, l, :], g_norm_mix[l].rearrange("(m p) -> m p", p=P)).then_inc(vec_in, 16)
                sp.dma_start(vrows[V_GFFN:V_ROWS, l, :], g_norm_ffn[l].rearrange("(m p) -> m p", p=P)).then_inc(vec_in, 16)
            sp.dma_start(vrows[V_BADA:V_C, 2, :], b_ada.rearrange("l (m p) -> (l m) p", p=P)).then_inc(vec_in, 16)
            sp.dma_start(vrows[V_C:V_ROWS, 2, :], c.rearrange("a (m p) -> (a m) p", p=P)).then_inc(vec_in, 16)
            for r, g in ((G_FOXQ, fox_g_q), (G_FOXK, fox_g_k), (G_DSAQ, dsa_g_q), (G_DSAK, dsa_g_k), (G_KIDX, dsa_g_kidx)):
                for e in range(2):
                    sp.dma_start(vrows[r:r + 1, 3, e * HD:(e + 1) * HD], g).then_inc(vec_in, 16)
            for e in range(8):
                sp.dma_start(vrows[G_BF:G_BF + 1, 3, e * NH:(e + 1) * NH], fox_b_f).then_inc(vec_in, 16)
            for t in range(TT):
                sp.dma_start(xtok[:, t, :], x[0, t * P:(t + 1) * P, :]).then_inc(x_in, 16)
            load_cols(0, 0, fox_w_in[0], 0, first=True)
            sp.dma_start(smr0[:], fox_w_in[0].rearrange("(k p) c -> p k c", p=P)[:, :, 3 * D:3 * D + NH]).then_inc(sm_in[0], 16)
            ada_chunk(0, 0, 0, first=True)
            load_cols(1, 1, fox_w_in[0], 256, first=True)
            ada_chunk(0, 1, 1)
            for s in range(2):
                load_cols(2 + s, s, fox_w_in[0], (2 + s) * 256)
            ada_chunk(0, 2, 2)
            with sp.Fori(1, 4) as i:
                for s in range(2):
                    load_cols(2 * i + 2 + s, s, fox_w_in[0], 512 * i + 512 + 256 * s)
                ada_chunk(0, 2 + i, 2 + i)
            for s in range(2):
                load_cols(10 + s, s, fox_w_in[0], (10 + s) * 256)
            for j in range(4):
                load_rows(FOX_OUT + j, j % 2, fox_w_out[0], 2 * j)

            def mlp_loads(l, up, down):
                def columns(i):
                    load_cols(up + 2 * i, up % 2, ffn_w_up[l], 256 * i)
                    load_cols(up + 2 * i + 1, (up + 1) % 2, ffn_w_up[l], FF + 256 * i)
                if l == 0:
                    with sp.Fori(0, 6) as i:
                        columns(i)
                        ada_chunk(1, 6 + i, i)
                    with sp.Fori(6, 11) as i:
                        columns(i)
                else:
                    with sp.Fori(0, 11) as i:
                        columns(i)
                load_rows(down, down % 2, ffn_w_down[l], 0)
                with sp.Fori(0, 5) as i:
                    for s in range(2):
                        load_rows(down + 1 + 2 * i + s, (down + 1 + s) % 2, ffn_w_down[l], 2 + 4 * i + 2 * s)

            mlp_loads(0, FOX_UP, FOX_DOWN)
            for j in range(2):
                load_cols(DSA_IDX + j, (DSA_IDX + j) % 2, dsa_w_in[0], 1536 + 256 * j)
            sp.wait_ge(x_done[2], FT)
            sp.dma_start(smr1[:], dsa_w_in[0].rearrange("(k p) c -> p k c", p=P)[:, :, 2048:2120]).then_inc(sm_in[1], 16)
            sp.dma_start(cum[:], alibi).then_inc(alibi_in, 16)
            load_cols(DSA_K, DSA_K % 2, dsa_w_in[0], 1024)
            for j in range(4):
                load_cols(DSA_Q + j, (DSA_Q + j) % 2, dsa_w_in[0], 256 * j)
            load_cols(DSA_V, DSA_V % 2, dsa_w_in[0], 1280)
            for j in range(4):
                load_rows(DSA_OUT + j, (DSA_OUT + j) % 2, dsa_w_out[0], 2 * j)
            mlp_loads(1, DSA_UP, DSA_DOWN)
            for e in range(2):
                sp.wait_ge(oT_done, 4 * e + 4)
                sp.dma_start(out[0].rearrange("(t p) d -> p t d", p=P)[:, :, 512 * e:512 * e + 512],
                             outs[:, :, 512 * e:512 * e + 512]).then_inc(out_done, 16)
            sp.wait_ge(out_done, 32)

        @block.gpsimd
        def _(pool):
            def split(i, s, u, first):
                n = 2 * s + u
                src = raw[:, s, u * UNIT:(u + 1) * UNIT]
                if not first:
                    wait_alone(pool, unit_used, 4 * i + n - 3)
                pool.tensor_scalar(wh[:, n, :], src, 1.0, 1.0, ALU.mult, ALU.mult).then_inc(w_hi, 1)
                pool.wait_ge(w_hi, 4 * i + n + 1)
                pool.tensor_tensor(wl[:, n, :], src, wh[:, n, :].bitcast(F32), ALU.subtract).then_inc(w_split, 1)

            def split_loads(first, end):
                with pool.Fori(first // 2, end // 2) as i:
                    for s in range(2):
                        pool.wait_ge(raw_in[s], 16 * i + 16)
                        for u in range(2):
                            split(i, s, u, False)

            def split_heads(l):
                with pool.Fori(4 * l, 4 * l + 4) as i:
                    for p in range(2):
                        q, k = pair_tiles(l, i - 4 * l, p)
                        wait_alone(pool, qk_high, 4 * i + 2 * p + 2)
                        pool.tensor_tensor(qSl[:, p:p + 1, :], q, qSh[:, p:p + 1, :].bitcast(F32), ALU.subtract).then_inc(qs_ready, 1)
                        pool.tensor_tensor(kSl[:, p:p + 1, :], k, kSh[:, p:p + 1, :].bitcast(F32), ALU.subtract).then_inc(qs_ready, 1)

            for s in range(2):
                pool.wait_ge(raw_in[s], 16)
                for u in range(2):
                    split(0, s, u, True)
            split_loads(2, FOX_OUT + 2)
            split_heads(0)
            split_loads(FOX_OUT + 2, DSA_OUT + 1)
            split_heads(1)
            split_loads(DSA_OUT + 1, LOADS)

        @block.tensor
        def _(pe):
            def mm3(dst, wa, wb, xa, xb, start, stop):
                pe.matmul(dst, wa, xa, start=start, stop=False)
                pe.matmul(dst, wa, xb, start=False, stop=False)
                return pe.matmul(dst, wb, xa, start=False, stop=stop)

            def unit_cols(load, u):
                n = (2 * load + u) % 4
                return (wh[:, n, :].rearrange("p (k c) -> p k c", k=4), wl[:, n, :].rearrange("p (k c) -> p k c", k=4))

            def proj_tile(load, load_e, c, dst, ready):
                for u in range(2):
                    a, b = unit_cols(load, u)
                    if c == 0:
                        pe.wait_ge(w_split, 2 * load_e + u + 1)
                    cols = slice(c * P, (c + 1) * P)
                    for k in range(4):
                        mm = mm3(dst, a[:, k, cols], b[:, k, cols], hh[:, 4 * u + k, :], hl[:, 4 * u + k, :],
                                 start=(u == 0 and k == 0), stop=(u == 1 and k == 3))
                    if c == 1:
                        mm.then_inc(unit_used, 1)
                if c == 0:
                    mm.then_inc(ready, 1)

            def rows_load(n, load, load_e, xs, first, last, order=range(FT), before=None):
                for m in order:
                    if before:
                        before(m)
                    for u in range(2):
                        if m == order[0]:
                            pe.wait_ge(w_split, 2 * load_e + u + 1)
                        s = (2 * load + u) % 4
                        xa, xb = xs(u)
                        mm = mm3(bank[m][:], wh[:, s, m * P:(m + 1) * P], wl[:, s, m * P:(m + 1) * P], xa, xb,
                                 start=(first and u == 0), stop=(last and u == 1))
                        if m == order[-1]:
                            mm.then_inc(unit_used, 1)
                    if last and m != order[-1]:
                        mm.then_inc(y_ready[n], 1)

            def ada(q):
                pe.wait_ge(ada_used, 8 * q + 8)
                for m in range(FT):
                    mm = pe.matmul(ADA[:, m:m + 1], ada_acc[:, m * P:(m + 1) * P], cst[:, C_ONE:C_ONE + 1], start=True, stop=True)
                mm.then_inc(ada_sum, 1)

            def norm(n):
                pe.wait_ge(sq_added, (FT - 1) * n + FT - 1)
                for t in range(TT):
                    mm = pe.matmul(ST[:, t:t + 1], nt[:, 0, t * P:(t + 1) * P], cst[:, C_ONE:C_ONE + 1], start=True, stop=True)
                mm.then_inc(ms_ready, 1)
                pe.wait_ge(nD, 4 * n + 4)
                for t in range(TT):
                    mm = pe.transpose(RB[:, t * P:(t + 1) * P], rbs[:, t * P:(t + 1) * P], ident)
                mm.then_inc(rms_ready, 1)

            def stat(l, te, t):
                pe.wait_ge(hsq_ready[l], te + 1)
                if t > 0:
                    pe.wait_ge(hD[l], 3 * te - 2)
                for j in range(TT):
                    mm = pe.matmul(ST[:, 2 * j:2 * j + 2], sqb[:, t % 2, j * P:(j + 1) * P], cst[:, C_BLOCK:C_BLOCK + 2], start=True, stop=True)
                mm.then_inc(hms_ready[l], 1)

            def spread(l, te):
                pe.wait_ge(hrs_ready[l], te + 1)
                pe.wait_ge(normed[l], te)
                for j in range(TT):
                    mm = pe.transpose(RB[:, j * P:(j + 1) * P], rbs[:, j * P:(j + 1) * P], ident)
                mm.then_inc(hrb_ready[l], 1)

            def v_load(l, load, load_e, emptied):
                for u in range(2):
                    a, b = unit_cols(load, u)
                    pe.wait_ge(w_split, 2 * load_e + u + 1)
                    for t in range(TT):
                        if u == 0:
                            pe.wait_ge(taken[l], emptied(t))
                        tok = slice(t * P, (t + 1) * P)
                        for k in range(4):
                            kk = 4 * u + k
                            mm = mm3(bank[t][:, 0:256], hh[:, kk, tok], hl[:, kk, tok], a[:, k, :], b[:, k, :],
                                     start=(kk == 0), stop=(kk == 7))
                        if u == 1 and t < TT - 1:
                            mm.then_inc(v_ready[l], 1)
                    mm.then_inc(unit_used, 1)

            def attention(l):
                def scores(i, s):
                    h, t = divmod(s, TT)
                    n = (t + 1) * P
                    if t == 0:
                        pe.wait_ge(qs_ready, 4 * i + 2 * (h // 2) + 2)
                        pe.wait_ge(kb_ready, 4 * i + h + 1)
                    S = bank[s % 2]
                    tok = slice(t * P, (t + 1) * P)
                    mm3(S[:, 0:n], half(qSh, h)[:, h // 2, tok], half(qSl, h)[:, h // 2, tok],
                        half(kSh, h)[:, h // 2, 0:n], half(kSl, h)[:, h // 2, 0:n], True, False)
                    pe.matmul(S[:, 0:n], half(biasq, h)[:, tok], half(biaskh, h)[:, h % 2, 0:n], start=False, stop=False)
                    if l == 0:
                        mm = pe.matmul(S[:, t * P:n], ident_r[:], causal_r[:], start=False, stop=True)
                    else:
                        mm = pe.matmul(S[:, 0:n], ident_r[:], masked[:, t, 0:n], start=False, stop=True)
                    mm.then_inc(s_ready, 1)

                def turn(i, s):
                    pe.wait_ge(p_ready, 16 * i + s + 1)
                    for j in range(s % TT + 1):
                        mm = pe.transpose(bank[2 + s % 2][:, j * P:(j + 1) * P], probs[:, s % 2, j * P:(j + 1) * P], ident)
                    mm.then_inc(pt_ready, 1)

                def values(i, s):
                    h, t = divmod(s, TT)
                    pe.wait_ge(pta_done if s % 2 else ptd_done, 8 * i + s // 2 + 1)
                    if t == 0 and h >= 2:
                        pe.wait_ge(o_done, 4 * i + h - 1)
                    for j in range(t + 1):
                        vj = v0[:, j, ds(256 * i + HD * h, HD)] if l == 0 else v1[:, j, ds(HD * (i - 4), HD)]
                        mm = pe.matmul(bank[4 + h % 2][:, t * HD:(t + 1) * HD], probsT[:, s % 2, j * P:(j + 1) * P], vj,
                                       start=(j == 0), stop=(j == t))
                    mm.then_inc(pv_done, 1)

                def turn_pair(i, p):
                    pe.wait_ge(o_done, 4 * i + 2 * p + 2)
                    pe.wait_ge(ol_done, 2 * i + p + 1)
                    for t in range(TT):
                        mm = pe.transpose(MISC[:, t * P:(t + 1) * P], oP[:, p, t, :], ident)
                    mm.then_inc(ot_ready, 1)

                with pe.Fori(4 * l, 4 * l + 4) as i:
                    scores(i, 0)
                    scores(i, 1)
                    for s in range(16):
                        turn(i, s)
                        if s + 2 < 16:
                            scores(i, s + 2)
                        if s >= 1:
                            values(i, s - 1)
                        if s == 11:
                            turn_pair(i, 0)
                    values(i, 15)
                    turn_pair(i, 1)

            def out_proj(l, load):
                pe.wait_ge(ol_done, 8 * l + 9)
                pe.wait_ge(ada_done, 6 if l == 0 else 12)
                for j in range(4):
                    rows_load(2 * l, load + j, load + j, lambda u: (hh[:, 2 * j + u, :], hl[:, 2 * j + u, :]), j == 0, j == 3)

            def mlp_layer(l, up, dn):
                n = 2 * l + 1
                norm(n)
                pe.wait_ge(h_ready, FT * n + FT)

                def up_body(i, with_ada):
                    proj_tile(up, up + 2 * i, 0, bank[0][:], a_ready[l])
                    pe.wait_ge(uf_done[l], 2 * i + 1)
                    proj_tile(up, up + 2 * i, 1, bank[1][:], None)
                    proj_tile(up + 1, up + 2 * i + 1, 0, bank[2][:], g_ready[l])
                    pe.wait_ge(conv_done[l], 2 * i + 2)
                    proj_tile(up + 1, up + 2 * i + 1, 1, bank[3][:], None)
                    if with_ada:
                        ada(6 + i)

                if l == 0:
                    with pe.Fori(0, 6) as i:
                        up_body(i, True)
                    with pe.Fori(6, 11) as i:
                        up_body(i, False)
                else:
                    with pe.Fori(0, 11) as i:
                        up_body(i, False)

                def hidden(k):
                    return (uh[:, ds(k, 1), :].rearrange("p a n -> p (a n)"), ul[:, ds(k, 1), :].rearrange("p a n -> p (a n)"))

                def before(m):
                    if m == 0:
                        pe.wait_ge(uf_done[l], UT + 1)

                if l == 0:
                    pe.wait_ge(ada_done, 12)
                pe.wait_ge(u_done[l], UT - 1)
                rows_load(n, dn, dn, lambda u: (uh[:, u, :], ul[:, u, :]), True, False, order=[4, 5, 6, 7, 0, 1, 2, 3], before=before)
                with pe.Fori(0, 4) as i:
                    for s in range(2):
                        rows_load(n, dn + 1 + s, dn + 1 + s + 2 * i, lambda u: hidden(4 * i + 2 + 2 * s + u), False, False)
                pe.wait_ge(u_done[l], UT + 1)
                for j in (9, 10):
                    rows_load(n, dn + j, dn + j, lambda u: (uh[:, 2 * j + u, :], ul[:, 2 * j + u, :]), False, j == 10)

            for s_ in (ol_done, uf_done[0], uf_done[1], u_done[0], u_done[1]):
                pe.sem_inc(s_, 1)

            pe.wait_ge(cst_in, 16)
            pe.wait_ge(vec_in, 16 * (8 + 2 + 10 + 8))
            for j, rows in enumerate((V_ROWS, V_ROWS, V_ROWS, G_ROWS)):
                mm = pe.transpose(MISC[:, j * P:j * P + rows], vrows[0:rows, j, :], cst[0:rows, C_ID:C_ID + rows])
            mm.then_inc(vecT_ready, 1)
            pe.wait_ge(x_in, 16 * TT)
            for m in range(FT):
                if m >= 4:
                    pe.wait_ge(x_done[0], m - 3)
                for t in range(TT):
                    mm = pe.transpose(bank[m % 4][:, t * P:(t + 1) * P], xtok[:, t, m * P:(m + 1) * P], ident)
                mm.then_inc(xT_ready, 1)
            ada(0)
            ada(1)

            norm(0)
            pe.wait_ge(sm_ready[0], 8)
            for k in range(FT):
                pe.wait_ge(h_ready, FT * 0 + k + 1)
                mm = mm3(MISC[:], smh0[:, k, :], sml0[:, k, :], hh[:, k, :], hl[:, k, :], k == 0, k == FT - 1)
            mm.then_inc(f_ready, 1)

            def fox_body(i, first):
                for c_ in range(4):
                    if not first:
                        pe.wait_ge(taken[0], 4 * i + c_ - 3)
                    proj_tile(c_ // 2, 2 * i + c_ // 2, c_ % 2, bank[c_][:], tile_ready[0])
                    if not (first and c_ == 0):
                        stat(0, 4 * i + c_ - 1, c_ - 1 if first else c_ + 3)
                    if not (first and c_ < 2):
                        spread(0, 4 * i + c_ - 2)
                ada(2 + i)

            fox_body(0, True)
            with pe.Fori(1, 4) as i:
                fox_body(i, False)
            stat(0, 15, 15)
            spread(0, 14)
            with pe.Fori(0, 2) as i:
                for s in range(2):
                    v_load(0, s, 8 + 2 * i + s, lambda t: 8 * i + 4 * s + 13 + t)
            spread(0, 15)
            pe.wait_ge(taken[0], 32)
            pe.wait_ge(normed[0], 16)
            attention(0)
            out_proj(0, FOX_OUT)
            mlp_layer(0, FOX_UP, FOX_DOWN)

            norm(2)
            pe.wait_ge(sm_ready[1], 3)
            for k in range(FT):
                pe.wait_ge(h_ready, FT * 2 + k + 1)
                mm = mm3(bank[0][:], smh1[:, k, 0:P], sml1[:, k, 0:P], hh[:, k, :], hl[:, k, :], k == 0, k == FT - 1)
            mm.then_inc(kidx_ready, 1)
            for t in range(TT):
                for k in range(FT):
                    tok = slice(t * P, (t + 1) * P)
                    mm = mm3(MISC[:, IH * t:IH * t + IH], hh[:, k, tok], hl[:, k, tok], smh1[:, k, P:P + IH], sml1[:, k, P:P + IH],
                             k == 0, k == FT - 1)
            mm.then_inc(w_ready, 1)
            for j in range(2):
                for c_ in range(2):
                    if j == 1 and c_ == 1:
                        pe.wait_ge(taken[1], 1)
                    proj_tile(DSA_IDX + j, DSA_IDX + j, c_, bank[(1 + 2 * j + c_) % 4][:], tile_ready[1])
                    if (j, c_) == (0, 0):
                        stat(1, 0, 0)
                    if (j, c_) == (0, 1):
                        spread(1, 0)
            pe.wait_ge(taken[1], 5)
            pe.wait_ge(normed[1], 1)
            pe.wait_ge(w_taken, 1)
            for e in range(3 * IH):
                h, t = e // 3, 1 + e % 3
                n = (t + 1) * P
                if e >= 2:
                    pe.wait_ge(relu_done, e - 1)
                pe.matmul(bank[6 + e % 2][:, 0:n], half(qidx, h)[:, h // 2, t * P:(t + 1) * P], half(kidx, h)[:, 0:n],
                          start=True, stop=True).then_inc(is_ready, 1)
            for c_ in range(2):
                proj_tile(DSA_K, DSA_K, c_, bank[1 + c_][:], tile_ready[1])
            stat(1, 1, 1)
            with pe.Fori(0, 2) as i:
                for c_ in range(4):
                    pe.wait_ge(taken[1], 4 * i + c_ + 4)
                    proj_tile(DSA_Q + c_ // 2, DSA_Q + c_ // 2 + 2 * i, c_ % 2, bank[(3 + c_) % 4][:], tile_ready[1])
                    stat(1, 4 * i + c_ + 2, c_ + 2)
                    spread(1, 4 * i + c_ + 1)
            stat(1, 10, 10)
            spread(1, 9)
            v_load(1, DSA_V, DSA_V, lambda t: 15)
            spread(1, 10)
            pe.wait_ge(taken[1], 19)
            pe.wait_ge(normed[1], 11)
            pe.wait_ge(relu_done, 3 * IH)
            pe.wait_ge(mask_ready, 4)
            attention(1)
            out_proj(1, DSA_OUT)
            mlp_layer(1, DSA_UP, DSA_DOWN)

            for m in range(FT):
                pe.wait_ge(x_done[4], m + 1)
                if m >= 4:
                    pe.wait_ge(oT_done, m - 3)
                for t in range(TT):
                    mm = pe.transpose(bank[m % 4][:, t * P:(t + 1) * P], xT[:, m, t * P:(t + 1) * P], ident)
                mm.then_inc(oT_ready, 1)

        @block.scalar
        def _(act):
            one = cst[:, C_ONE:C_ONE + 1]

            def squares(n, m):
                act.wait_ge(x_done[n], m + 1)
                if m >= 3:
                    act.wait_ge(sq_added, (FT - 1) * n + m - 2)
                act.activation(nt[:, 0 if m == 0 else 1 + m % 2, :], xT[:, m, :], ACT.Square).then_inc(sq_ready, 1)

            def guess(steps_d, steps_a, d0, a0, cols):
                act.wait_ge(steps_d, d0 + 1)
                act.activation(rln[:, 0:cols], rv[:, 0:cols], ACT.Ln).then_inc(steps_a, 1)
                act.wait_ge(steps_a, a0 + 1)
                act.activation(ry[:, 0:cols], rln[:, 0:cols], ACT.Exp, scale=-0.5).then_inc(steps_a, 1)

            def modulate(n):
                guess(nD, nA, 4 * n, 2 * n, TT)
                act.wait_ge(mul_ready, n + 1)
                shift = 3 * n
                for k in range(FT):
                    act.wait_ge(t_ready, FT * n + k + 1)
                    args = dict(scale=mulA[:, n, k:k + 1], bias=mod[:, shift, k:k + 1])
                    act.activation(hh[:, k, :], nt[:, k % 2, :], ACT.Identity, **args)
                    if k >= 2:
                        act.wait_ge(h_ready, FT * n + k - 1)
                    act.activation(nt[:, 2 + k % 2, :], nt[:, k % 2, :], ACT.Identity, **args).then_inc(hf_ready, 1)

            def take(l, te, t, b, gain, sem_, count):
                act.wait_ge(sem_, count)
                if t >= 2:
                    act.wait_ge(hms_ready[l], te - 1)
                act.activation(sqb[:, t % 2, :], bank[b][:], ACT.Square).then_inc(hsq_ready[l], 1)
                if t >= 2:
                    act.wait_ge(normed[l], te - 1)
                act.activation(qg[:, t % 2, :], bank[b][:], ACT.Identity, scale=gain).then_inc(taken[l], 1)

            def attention(l):
                def probabilities(i, s):
                    n = (s % TT + 1) * P
                    act.wait_ge(max_done, 16 * i + s + 1)
                    act.activation(probs[:, s % 2, 0:n], bank[s % 2][:, 0:n], ACT.Exp, bias=nmax[:, s:s + 1],
                                   accum_out=rowsum[:, s:s + 1]).then_inc(p_ready, 1)

                def turned(i, s):
                    n = (s % TT + 1) * P
                    act.wait_ge(pt_ready, 16 * i + s + 1)
                    act.copy(probsT[:, s % 2, 0:n], bank[2 + s % 2][:, 0:n]).then_inc(pta_done, 1)

                def out_high(i, p):
                    act.wait_ge(ot_ready, 2 * i + p + 1)
                    act.copy(hh[:, ds(2 * (i - 4 * l) + p, 1), :], MISC[:].rearrange("p (a n) -> p a n", a=1)).then_inc(oh_done, 1)

                def pair_high(g, p):
                    q, k = pair_tiles(l, g, p)
                    act.copy(qSh[:, p:p + 1, :], q).then_inc(qk_high, 1)
                    act.copy(kSh[:, p:p + 1, :], k).then_inc(qk_high, 1)

                def round_(i, last):
                    for s in range(16):
                        probabilities(i, s)
                        if s >= 2 and s % 2 == 0:
                            turned(i, s - 1)
                        if s == 9 and not last:
                            pair_high(i - 4 * l + 1, 0)
                        if s == 13:
                            out_high(i, 0)
                    if not last:
                        pair_high(i - 4 * l + 1, 1)
                    turned(i, 15)
                    out_high(i, 1)

                act.wait_ge(normed[l], 16 if l == 0 else 11)
                pair_high(0, 0)
                pair_high(0, 1)
                with act.Fori(4 * l, 4 * l + 3) as i:
                    round_(i, False)
                round_(4 * l + 3, True)

            def mlp_layer(l, up):
                n = 2 * l + 1
                modulate(n)
                col = vec[:, l, :]

                def up_body(i):
                    for c_ in range(2):
                        if c_ == 0:
                            act.wait_ge(a_ready[l], i + 1)
                            act.wait_ge(u_done[l], 2 * i + 1)
                        else:
                            act.wait_ge(unit_used, 2 * (up + 2 * i) + 2)
                        tau = 2 * i + c_
                        act.activation(cv[:, c_, :], bank[c_][:], ACT.Identity, scale=col[:, ds(V_CONVW + 2 * UT + tau, 1)],
                                       bias=col[:, ds(V_CONVB + tau, 1)]).then_inc(tap2[l], 1)
                    for c_ in range(2):
                        act.wait_ge(conv_done[l], 2 * i + c_ + 1)
                        act.activation(cv[:, c_, :], cv[:, c_, :], ACT.Silu).then_inc(silu_done[l], 1)
                    for c_ in range(2):
                        act.wait_ge(uf_done[l], 2 * i + c_ + 2)
                        act.copy(uh[:, ds(2 * i + c_, 1), :], cv[:, c_:c_ + 1, :]).then_inc(uh_done[l], 1)

                with act.Fori(0, 11) as i:
                    up_body(i)

            act.wait_ge(vec_done, 4)
            act.activation(csil[:], vec[:, 2, V_C:V_ROWS], ACT.Silu).then_inc(csil_done, 1)
            for m in range(FT):
                act.wait_ge(xT_ready, m + 1)
                act.copy(xT[:, m, :], bank[m % 4][:]).then_inc(x_done[0], 1)
                squares(0, m)

            modulate(0)
            act.wait_ge(f_ready, 1)
            act.activation(probs[:, 0, :], MISC[:], ACT.Identity, bias=vec[:, 3, G_BF:G_BF + 1]).then_inc(f_act, 1)
            act.wait_ge(f_act, 1)
            act.activation(probs[:, 1, :], probs[:, 0, :], ACT.Abs).then_inc(f_act, 1)
            act.wait_ge(f_act, 2)
            act.activation(probsT[:, 0, :], probs[:, 1, :], ACT.Exp, scale=-1.0).then_inc(f_act, 1)
            act.wait_ge(f_act, 3)
            act.activation(probsT[:, 1, :], probsT[:, 0, :], ACT.Ln, bias=one).then_inc(f_act, 1)

            def fox_tile(i, c_, first):
                tau = 4 * i + c_
                sem_, count = (tile_ready[0], 2 * i + c_ // 2 + 1) if c_ % 2 == 0 else (unit_used, 2 * (2 * i + c_ // 2) + 2)
                take(0, tau, c_ if first else c_ + 4, c_, gains[:, ds(GAIN[0] + tau, 1)], sem_, count)
                if not (first and c_ == 0):
                    guess(hD[0], hA[0], 3 * (tau - 1), 2 * (tau - 1), 8)

            for c_ in range(4):
                fox_tile(0, c_, True)
            with act.Fori(1, 4) as i:
                for c_ in range(4):
                    fox_tile(i, c_, False)
            guess(hD[0], hA[0], 3 * 15, 2 * 15, 8)

            def take_v(l, je, load_e, dst, t):
                if t < TT - 1:
                    act.wait_ge(v_ready[l], 3 * je + t + 1)
                else:
                    act.wait_ge(unit_used, 2 * load_e + 2)
                act.copy(dst, bank[t][:, 0:256]).then_inc(taken[l], 1)

            with act.Fori(0, 4) as j:
                for t in range(TT):
                    take_v(0, j, 8 + j, v0[:, t, ds(256 * j, 256)], t)
            attention(0)
            for m in range(FT):
                squares(1, m)
            mlp_layer(0, FOX_UP)
            for m in range(FT):
                squares(2, m)

            modulate(2)
            take(1, 0, 0, 0, gains[:, GAIN[1]:GAIN[1] + 1], kidx_ready, 1)
            for j in range(2):
                for c_ in range(2):
                    if c_ == 0:
                        act.wait_ge(tile_ready[1], j + 1)
                    else:
                        act.wait_ge(unit_used, 2 * (DSA_IDX + j) + 2)
                    act.copy(qidx[:, 2 * j + c_, :], bank[(1 + 2 * j + c_) % 4][:]).then_inc(taken[1], 1)
                    if (j, c_) == (0, 0):
                        guess(hD[1], hA[1], 0, 0, 8)
            for e in range(3 * IH):
                n = (2 + e % 3) * P
                act.wait_ge(is_ready, e + 1)
                if e >= 2:
                    act.wait_ge(weighed, e - 1)
                act.activation(probs[:, e % 2, 0:n], bank[6 + e % 2][:, 0:n], ACT.Relu).then_inc(relu_done, 1)
            take(1, 1, 1, 1, gains[:, GAIN[1] + 1:GAIN[1] + 2], tile_ready[1], 3)
            take(1, 2, 2, 2, gains[:, GAIN[1] + 2:GAIN[1] + 3], unit_used, 2 * DSA_K + 2)
            guess(hD[1], hA[1], 3, 2, 8)
            with act.Fori(0, 2) as i:
                for c_ in range(4):
                    tau = 4 * i + c_ + 3
                    sem_, count = (tile_ready[1], 2 * i + c_ // 2 + 4) if c_ % 2 == 0 else (unit_used, 2 * (DSA_Q + c_ // 2 + 2 * i) + 2)
                    take(1, tau, c_ + 3, (3 + c_) % 4, gains[:, ds(GAIN[1] + tau, 1)], sem_, count)
                    guess(hD[1], hA[1], 3 * (tau - 1), 2 * (tau - 1), 8)
            guess(hD[1], hA[1], 3 * 10, 2 * 10, 8)
            for t in range(TT):
                take_v(1, 0, DSA_V, v1[:, t, :], t)
            attention(1)
            for m in range(FT):
                squares(3, m)
            mlp_layer(1, DSA_UP)

        @block.vector
        def _(dve):
            def add_squares(n, m):
                dve.wait_ge(sq_ready, FT * n + m + 1)
                if m >= 2:
                    dve.wait_ge(sq_added, (FT - 1) * n + m - 1)
                dve.tensor_tensor(nt[:, 0, :], nt[:, 0, :], nt[:, 1 + m % 2, :], ALU.add).then_inc(sq_added, 1)

            def mean_square(ready, count, steps, cols, width):
                dve.wait_ge(ready, count)
                dve.tensor_scalar(rv[:, 0:cols], ST[:, 0:cols], 1.0 / width, EPS, ALU.mult, ALU.add).then_inc(steps, 1)

            def newton(steps_d, steps_a, d0, a0, cols, last):
                dve.wait_ge(steps_a, a0 + 2)
                dve.tensor_tensor(ra[:, 0:cols], ry[:, 0:cols], ry[:, 0:cols], ALU.mult).then_inc(steps_d, 1)
                dve.wait_ge(steps_d, d0 + 2)
                dve.scalar_tensor_tensor(out=rb2[:, 0:cols], in0=ra[:, 0:cols], scalar=-0.5, in1=rv[:, 0:cols],
                                         op0=ALU.mult, op1=ALU.mult).then_inc(steps_d, 1)
                dve.wait_ge(steps_d, d0 + 3)
                wide = [P, cols, L // cols]
                dve.scalar_tensor_tensor(out=rbs[:].rearrange("p (a b) -> p a b", a=cols),
                                         in0=rb2[:, 0:cols].unsqueeze(2).to_broadcast(wide), scalar=1.5,
                                         in1=ry[:, 0:cols].unsqueeze(2).to_broadcast(wide),
                                         op0=ALU.add, op1=ALU.mult).then_inc(last, 1)

            def modulate(n):
                l, scale = n // 2, 3 * n + 1
                gain = vec[:, l, V_GMIX:V_GFFN] if n % 2 == 0 else vec[:, l, V_GFFN:V_ROWS]
                dve.wait_ge(ada_done, scale + 1)
                dve.scalar_tensor_tensor(out=mulA[:, n, :], in0=mod[:, scale, :], scalar=1.0, in1=gain,
                                         op0=ALU.add, op1=ALU.mult).then_inc(mul_ready, 1)
                mean_square(ms_ready, n + 1, nD, TT, float(D))
                newton(nD, nA, 4 * n, 2 * n, TT, nD)
                dve.wait_ge(rms_ready, n + 1)
                for k in range(FT + 1):
                    if k < FT:
                        if k >= 2:
                            dve.wait_ge(hf_ready, FT * n + k - 1)
                        dve.tensor_tensor(nt[:, k % 2, :], xT[:, k, :], RB[:], ALU.mult).then_inc(t_ready, 1)
                    if k >= 1:
                        dve.wait_ge(hf_ready, FT * n + k)
                        dve.tensor_tensor(hl[:, k - 1, :], nt[:, 2 + (k - 1) % 2, :], hh[:, k - 1, :].bitcast(F32),
                                          ALU.subtract).then_inc(h_ready, 1)

            def residual(n, last_unit):
                gate = 6 * (n // 2) + (2 if n % 2 == 0 else 5)
                dve.wait_ge(ada_done, gate + 1)
                for m in range(FT):
                    if m < FT - 1:
                        dve.wait_ge(y_ready[n], m + 1)
                    else:
                        dve.wait_ge(unit_used, last_unit)
                    dve.scalar_tensor_tensor(out=xT[:, m, :], in0=bank[m][:], scalar=mod[:, gate, m:m + 1], in1=xT[:, m, :],
                                             op0=ALU.mult, op1=ALU.add).then_inc(x_done[n + 1], 1)
                    if n < 3 and m >= 2:
                        add_squares(n + 1, m - 1)
                if n < 3:
                    add_squares(n + 1, FT - 1)

            def ada_slice(q, k):
                dve.wait_ge(ada_in[k % 2], 16 * (4 * q + k // 2 + 1))
                if k == 0:
                    dve.tensor_scalar(ada_acc[:], ada_raw[:, 0, :], csil[:, 0:1], None, ALU.mult).then_inc(ada_used, 1)
                else:
                    dve.wait_ge(ada_used, 8 * q + k)
                    dve.scalar_tensor_tensor(out=ada_acc[:], in0=ada_raw[:, k % 2, :], scalar=csil[:, k:k + 1], in1=ada_acc[:],
                                             op0=ALU.mult, op1=ALU.add).then_inc(ada_used, 1)

            def ada_out(l, q, part):
                dve.wait_ge(ada_sum, q + 1)
                bias = vec[:, 2, V_BADA + 48 * l:V_BADA + 48 * l + 48].rearrange("p (q m) -> p q m", q=6)[:, ds(part, 1), :]
                dve.tensor_tensor(mod[:, ds(q, 1), :], ADA[:, 0:FT].rearrange("p (a m) -> p a m", a=1), bias, ALU.add).then_inc(ada_done, 1)

            def finish_tile(l, te, t, dst):
                dve.wait_ge(hrb_ready[l], te + 1)
                return dve.tensor_tensor(dst, qg[:, t % 2:t % 2 + 1, :], RB[:].rearrange("p (a n) -> p a n", a=1), ALU.mult).then_inc(normed[l], 1)

            def head_stats(l, te):
                mean_square(hms_ready[l], te + 1, hD[l], 8, float(HD))

            def head_newton(l, te):
                newton(hD[l], hA[l], 3 * te, 2 * te, 8, hrs_ready[l])

            def bias_rows(l):
                b = bias_step[l]
                dve.tensor_copy(cumh[:], cum[:]).then_inc(b, 1)
                dve.wait_ge(b, 1)
                dve.tensor_tensor(probs[:, 0, :], cum[:], cumh[:].bitcast(F32), ALU.subtract).then_inc(b, 1)
                dve.wait_ge(b, 2)
                dve.tensor_scalar(probs[:, 1, :], probs[:, 0, :], cst[:, C_ODD:C_ODD + 1], None, ALU.mult).then_inc(b, 1)
                dve.wait_ge(b, 3)
                dve.scalar_tensor_tensor(out=probs[:, 0, :], in0=cumh[:].bitcast(F32), scalar=cst[:, C_EVEN:C_EVEN + 1],
                                         in1=probs[:, 1, :], op0=ALU.mult, op1=ALU.add).then_inc(b, 1)
                dve.wait_ge(b, 4)
                for r in (0, 64):
                    dve.tensor_copy(biasq[r:r + 32, :], probs[r:r + 32, 0, :])
                    dve.tensor_scalar(biasq[r + 32:r + 64, :], cst[r + 32:r + 64, C_ONE:C_ONE + 1].to_broadcast([32, L]), 1.0, None, ALU.mult)
                    dve.memset(biask[r:r + 32, :], 1.0)
                    op = dve.tensor_scalar(biask[r + 32:r + 64, :], probs[r + 32:r + 64, 0, :], -1.0, None, ALU.mult)
                op.then_inc(b, 1)
                dve.wait_ge(b, 5)

            def attention(l):
                def bias_head(i, h):
                    dve.tensor_scalar(half(biaskh, h)[:, h % 2, :], half(biask, h), half(cst, h)[:, ds(C_HEAD + 4 * (i - 4 * l) + h, 1)], None,
                                      ALU.mult).then_inc(kb_ready, 1)

                def row_max(i, s):
                    n = (s % TT + 1) * P
                    dve.wait_ge(s_ready, 16 * i + s + 1)
                    dve.tensor_reduce(nmax[:, s:s + 1], bank[s % 2][:, 0:n], AX_X, ALU.max, negate=True).then_inc(max_done, 1)

                def turned(i, s):
                    n = (s % TT + 1) * P
                    dve.wait_ge(pt_ready, 16 * i + s + 1)
                    dve.tensor_copy(probsT[:, s % 2, 0:n], bank[2 + s % 2][:, 0:n]).then_inc(ptd_done, 1)

                def head_out(i, h):
                    dve.wait_ge(pv_done, 16 * i + 4 * h + 4)
                    dve.reciprocal(rrec[:, 4 * h:4 * h + 4], rowsum[:, 4 * h:4 * h + 4]).then_inc(rec_done, 1)
                    dve.wait_ge(rec_done, 4 * i + h + 1)
                    dve.tensor_tensor(oP[:, h // 2, :, HD * (h % 2):HD * (h % 2) + HD],
                                      bank[4 + h % 2][:, 0:4 * HD].rearrange("p (t d) -> p t d", t=TT),
                                      rrec[:, 4 * h:4 * h + 4].unsqueeze(2).to_broadcast([P, TT, HD]), ALU.mult).then_inc(o_done, 1)

                def out_low(i, p):
                    dve.wait_ge(oh_done, 2 * i + p + 1)
                    dve.tensor_tensor(hl[:, ds(2 * (i - 4 * l) + p, 1), :], MISC[:].rearrange("p (a n) -> p a n", a=1),
                                      hh[:, ds(2 * (i - 4 * l) + p, 1), :].bitcast(F32), ALU.subtract).then_inc(ol_done, 1)

                with dve.Fori(4 * l, 4 * l + 4) as i:
                    bias_head(i, 0)
                    bias_head(i, 1)
                    row_max(i, 0)
                    row_max(i, 1)
                    for s in range(16):
                        if s % 2 == 0:
                            turned(i, s)
                        if s in (3, 7):
                            bias_head(i, s // 4 + 2)
                        if s + 2 < 16:
                            row_max(i, s + 2)
                        if s >= 5 and s % 4 == 1:
                            head_out(i, s // 4 - 1)
                        if s == 14:
                            out_low(i, 0)
                    head_out(i, 3)
                    out_low(i, 1)

            def mlp_layer(l, up, last_unit):
                n = 2 * l + 1
                modulate(n)
                col = vec[:, l, :]

                def up_body(i, with_ada):
                    for c_ in range(2):
                        tau = 2 * i + c_
                        dve.wait_ge(tap2[l], tau + 1)
                        dve.scalar_tensor_tensor(out=cv[:, c_, 1:L], in0=bank[c_][:, 0:L - 1], scalar=col[:, ds(V_CONVW + UT + tau, 1)],
                                                 in1=cv[:, c_, 1:L], op0=ALU.mult, op1=ALU.add).then_inc(tap1[l], 1)
                        dve.wait_ge(tap1[l], tau + 1)
                        dve.scalar_tensor_tensor(out=cv[:, c_, 2:L], in0=bank[c_][:, 0:L - 2], scalar=col[:, ds(V_CONVW + tau, 1)],
                                                 in1=cv[:, c_, 2:L], op0=ALU.mult, op1=ALU.add).then_inc(conv_done[l], 1)
                    if with_ada:
                        for k in range(FT):
                            ada_slice(6 + i, k)
                    for c_ in range(2):
                        tau = 2 * i + c_
                        dve.wait_ge(silu_done[l], tau + 1)
                        if c_ == 0:
                            dve.wait_ge(g_ready[l], i + 1)
                        else:
                            dve.wait_ge(unit_used, 2 * (up + 2 * i + 1) + 2)
                        dve.tensor_tensor(cv[:, c_, :], cv[:, c_, :], bank[2 + c_][:], ALU.mult).then_inc(uf_done[l], 1)
                        dve.wait_ge(uh_done[l], tau + 1)
                        dve.tensor_tensor(ul[:, ds(tau, 1), :], cv[:, c_:c_ + 1, :], uh[:, ds(tau, 1), :].bitcast(F32),
                                          ALU.subtract).then_inc(u_done[l], 1)
                    if with_ada:
                        ada_out(1, 6 + i, i)

                if l == 0:
                    with dve.Fori(0, 6) as i:
                        up_body(i, True)
                    with dve.Fori(6, 11) as i:
                        up_body(i, False)
                else:
                    with dve.Fori(0, 11) as i:
                        up_body(i, False)
                residual(n, last_unit)

            dve.wait_ge(cst_in, 16)
            dve.tensor_copy(ident_r[:], ident)
            dve.tensor_copy(causal_r[:], cst[:, C_CAUSAL:C_CAUSAL + P]).then_inc(cst_done, 1)
            dve.wait_ge(vecT_ready, 1)
            for j, rows in enumerate((V_ROWS, V_ROWS, V_ROWS, G_ROWS)):
                dve.tensor_copy(vec[:, j, 0:rows], MISC[:, j * P:j * P + rows]).then_inc(vec_done, 1)
            dve.wait_ge(vec_done, 4)

            def gain_cols(at, n, row, scale):
                return dve.tensor_scalar(gains[:, at:at + n], vec[:, 3, row:row + 1].to_broadcast([P, n]), scale, None, ALU.mult)
            gain_cols(GAIN[0], 8, G_FOXQ, HD ** -0.5)
            gain_cols(GAIN[0] + 8, 8, G_FOXK, 1.0)
            gain_cols(GAIN[1], 1, G_KIDX, 1.0)
            gain_cols(GAIN[1] + 1, 2, G_DSAK, 1.0)
            gain_cols(GAIN[1] + 3, 8, G_DSAQ, HD ** -0.5).then_inc(cst_done, 1)
            for m in range(1, FT):
                add_squares(0, m)
            dve.wait_ge(csil_done, 1)
            for q in range(2):
                for k in range(FT):
                    ada_slice(q, k)
                ada_out(0, q, q)
            dve.wait_ge(sm_in[0], 16)
            for r in range(8):
                dve.tensor_copy(smh0[:, :, r * NH:(r + 1) * NH], smr0[:]).then_inc(sm_hi[0], 1)
            dve.wait_ge(sm_hi[0], 8)
            for r in range(8):
                dve.tensor_tensor(sml0[:, :, r * NH:(r + 1) * NH], smr0[:], smh0[:, :, r * NH:(r + 1) * NH].bitcast(F32),
                                  ALU.subtract).then_inc(sm_ready[0], 1)

            modulate(0)
            dve.wait_ge(f_act, 4)
            dve.tensor_scalar(probs[:, 0, :], probs[:, 0, :], 0.0, None, ALU.min).then_inc(f_dve, 1)
            dve.wait_ge(f_dve, 1)
            dve.tensor_tensor(probs[:, 1, :], probs[:, 0, :], probsT[:, 1, :], ALU.subtract).then_inc(f_dve, 1)
            dve.memset(probsT[:, 0, :], 1.0).then_inc(f_dve, 1)
            dve.wait_ge(f_dve, 3)
            dve.tensor_tensor_scan(cum[:], probsT[:, 0, :], probs[:, 1, :], 0.0, ALU.mult, ALU.add).then_inc(f_dve, 1)
            dve.wait_ge(f_dve, 4)
            bias_rows(0)

            def fox_body(i, first):
                for c_ in range(4):
                    tau = 4 * i + c_
                    if not (first and c_ == 0):
                        head_stats(0, tau - 1)
                    if not (first and c_ < 2):
                        finish_tile(0, tau - 2, c_, qk[:, ds(tau - 2, 1), :])
                    if not (first and c_ == 0):
                        head_newton(0, tau - 1)
                    ada_slice(2 + i, 2 * c_)
                    ada_slice(2 + i, 2 * c_ + 1)
                ada_out(0, 2 + i, 2 + i)

            fox_body(0, True)
            with dve.Fori(1, 4) as i:
                fox_body(i, False)
            head_stats(0, 15)
            finish_tile(0, 14, 14, qk[:, 14:15, :])
            head_newton(0, 15)
            finish_tile(0, 15, 15, qk[:, 15:16, :])
            attention(0)
            residual(0, 2 * (FOX_OUT + 3) + 2)
            mlp_layer(0, FOX_UP, 2 * (FOX_DOWN + 10) + 2)

            modulate(2)
            dve.wait_ge(sm_in[1], 16)
            parts = ((0, HD, 0), (HD, HD, 0), (P, IH, HD))
            for at, n, src in parts:
                dve.tensor_copy(smh1[:, :, at:at + n], smr1[:, :, src:src + n]).then_inc(sm_hi[1], 1)
            dve.wait_ge(sm_hi[1], 3)
            for at, n, src in parts:
                dve.tensor_tensor(sml1[:, :, at:at + n], smr1[:, :, src:src + n], smh1[:, :, at:at + n].bitcast(F32),
                                  ALU.subtract).then_inc(sm_ready[1], 1)
            dve.wait_ge(alibi_in, 16)
            bias_rows(1)
            dve.wait_ge(w_ready, 1)
            dve.tensor_scalar(widx[:], MISC[:, 0:TT * IH], IH ** -0.5 * HD ** -0.5, None, ALU.mult).then_inc(w_taken, 1)
            dve.wait_ge(w_taken, 1)
            head_stats(1, 0)
            head_newton(1, 0)
            finish_tile(1, 0, 0, kidx.rearrange("p (a n) -> p a n", a=1))
            for e in range(3 * IH):
                h, t = e // 3, 1 + e % 3
                n = (t + 1) * P
                w_col = widx[:, IH * t + h:IH * t + h + 1]
                dve.wait_ge(relu_done, e + 1)
                if h == 0:
                    dve.tensor_scalar(score[:, t - 1, 0:n], probs[:, e % 2, 0:n], w_col, 0.0, ALU.mult, ALU.add).then_inc(weighed, 1)
                else:
                    dve.wait_ge(weighed, e - 2)
                    dve.scalar_tensor_tensor(out=score[:, t - 1, 0:n], in0=probs[:, e % 2, 0:n], scalar=w_col,
                                             in1=score[:, t - 1, 0:n], op0=ALU.mult, op1=ALU.add).then_inc(weighed, 1)
            dve.wait_ge(weighed, 3 * IH)
            for t in range(1, TT):
                dve.tensor_tensor(score[:, t - 1, t * P:(t + 1) * P], score[:, t - 1, t * P:(t + 1) * P],
                                  cst[:, C_CAUSAL:C_CAUSAL + P], ALU.add).then_inc(tk, 1)

            def top_round(r):
                for t in range(3):
                    n = (t + 2) * P
                    dve.wait_ge(tk, 6 * r + 1 + t)
                    dve.max(top8[:, t, :], score[:, t, 0:n]).then_inc(tk, 1)
                for t in range(3):
                    n = (t + 2) * P
                    dve.wait_ge(tk, 6 * r + 4 + t)
                    dve.match_replace(score[:, t, 0:n], top8[:, t, :], score[:, t, 0:n], TAKEN).then_inc(tk, 1)

            head_stats(1, 1)
            head_newton(1, 1)

            def key_heads(te, p):
                dve.wait_ge(hrb_ready[1], te + 1)
                for g in range(2):
                    src = slice(g * HD, (g + 1) * HD)
                    for e in range(2):
                        op = dve.tensor_tensor(qk[e * HD:(e + 1) * HD, 8 + 2 * p + g, :], qg[src, te % 2, :], RB[src, :], ALU.mult)
                op.then_inc(normed[1], 1)

            def dsa_slot(i, c_, first):
                tau = 4 * i + c_ + 3
                head_stats(1, tau - 1)
                if first and c_ < 2:
                    key_heads(tau - 2, tau - 3)
                else:
                    finish_tile(1, tau - 2, c_ + 1, qk[:, ds(tau - 5, 1), :])
                head_newton(1, tau - 1)
                top_round(2 * (4 * i + c_))
                top_round(2 * (4 * i + c_) + 1)

            for c_ in range(4):
                dsa_slot(0, c_, True)
            with dve.Fori(1, 2) as i:
                for c_ in range(4):
                    dsa_slot(i, c_, False)
            head_stats(1, 10)
            finish_tile(1, 9, 9, qk[:, 6:7, :])
            head_newton(1, 10)
            finish_tile(1, 10, 10, qk[:, 7:8, :])
            dve.tensor_copy(masked[:, 0, 0:P], cst[:, C_CAUSAL:C_CAUSAL + P]).then_inc(mask_ready, 1)
            dve.wait_ge(tk, 3 + 6 * (TOPK // 8))
            for t in range(1, TT):
                n = (t + 1) * P
                dve.tensor_scalar(masked[:, t, 0:n], score[:, t - 1, 0:n], TAKEN, MASKED, ALU.not_equal, ALU.mult).then_inc(mask_ready, 1)
            attention(1)
            residual(2, 2 * (DSA_OUT + 3) + 2)
            mlp_layer(1, DSA_UP, 2 * (DSA_DOWN + 10) + 2)

            for m in range(FT):
                dve.wait_ge(oT_ready, m + 1)
                dve.tensor_copy(outs[:, :, m * P:(m + 1) * P], bank[m % 4][:].rearrange("p (t d) -> p t d", t=TT)).then_inc(oT_done, 1)


_INS = ["x", "c", "w_ada", "b_ada", "g_norm_mix", "g_norm_ffn", "fox_w_in", "fox_b_f", "fox_g_q", "fox_g_k",
        "fox_w_out", "dsa_w_in", "dsa_g_q", "dsa_g_k", "dsa_g_kidx", "dsa_w_out", "ffn_w_up", "ffn_conv_w",
        "ffn_conv_b", "ffn_w_down"]


def shape_constants():
    import numpy as np
    t = np.zeros((P, C_N), np.float32)
    p = np.arange(P)
    t[:, C_ID:C_ID + P] = np.eye(P)
    t[:, C_CAUSAL:C_CAUSAL + P] = np.where(p[None, :] > p[:, None], MASKED, 0.0)
    t[:, C_BLOCK] = p < HD
    t[:, C_BLOCK + 1] = p >= HD
    t[:, C_EVEN] = p % 32 < NH
    t[:, C_ODD] = p % 32 >= NH
    t[:, C_HEAD:C_HEAD + NH] = p[:, None] % NH == np.arange(NH)[None, :]
    t[:, C_ONE] = 1.0
    t[:, C_EPS] = EPS
    slopes = np.exp2(-8.0 * np.arange(1, NH + 1, dtype=np.float32) / np.float32(NH)).astype(np.float32)
    alibi = -slopes[p % NH][:, None] * np.arange(L, dtype=np.float32)[None, :]
    return t, alibi.astype(np.float32)


def kernel(**inputs):
    import numpy as _np
    import concourse.bacc as _bacc
    from concourse import mybir as _mybir
    from concourse.bass_utils import run_bass_kernel_spmd as _run

    nc = _bacc.Bacc("TRN2", target_bir_lowering=False, num_devices=1, dynamic_dma_scratch_size=2048)
    arrays, args = {}, []
    for name, a in [(n, inputs[n]) for n in _INS] + list(zip(("consts", "alibi"), shape_constants())):
        a = _np.ascontiguousarray(a)
        arrays[f"in_{name}_dram"] = a
        args.append(nc.dram_tensor(f"in_{name}_dram", a.shape, _mybir.dt.from_np(a.dtype), kind="ExternalInput").ap())
    args.append(nc.dram_tensor("out_dram", (1, L, D), _mybir.dt.float32, kind="ExternalOutput").ap())
    two_layers(nc, *args)
    r = _run(nc, [arrays], core_ids=[0])
    return r.results[0]["out_dram"]
```

```python
from contextlib import ExitStack

import concourse.bass as bass
from concourse import mybir

F32 = mybir.dt.float32
F32R = mybir.dt.float32r
ALU = mybir.AluOpType
ACT = mybir.ActivationFunctionType
AX_X = mybir.AxisListType.X
ds = bass.ds

P = 128
D = 1024
L = 512
FT = D // P
TT = L // P
HD = 64
NH = D // HD
NKV = 4
IH = 8
TOPK = L // 4
FF = 2816
UT = FF // P
EPS = 1e-6
MASKED = -3.0e38
TAKEN = -3.4028235e38

C_ID, C_CAUSAL, C_BLOCK, C_EVEN, C_ODD, C_HEAD, C_ONE, C_EPS, C_N = 0, 128, 256, 258, 259, 260, 276, 277, 278

FOX_IN, FOX_OUT, FOX_UP, FOX_DOWN = 0, 12, 16, 38
DSA_IDX, DSA_K, DSA_Q, DSA_V, DSA_OUT, DSA_UP, DSA_DOWN = 49, 51, 52, 56, 57, 61, 83
LOADS = 94
UNIT = 1024

V_CONVW, V_CONVB, V_GMIX, V_GFFN, V_ROWS = 0, 66, 88, 96, 104
V_BADA, V_C = 0, 96
G_FOXQ, G_FOXK, G_DSAQ, G_DSAK, G_KIDX, G_BF, G_ROWS = 0, 1, 2, 3, 4, 5, 6
GAIN = [0, 16]


def two_layers(nc, x, c, w_ada, b_ada, g_norm_mix, g_norm_ffn, fox_w_in, fox_b_f, fox_g_q, fox_g_k,
               fox_w_out, dsa_w_in, dsa_g_q, dsa_g_k, dsa_g_kidx, dsa_w_out, ffn_w_up, ffn_conv_w,
               ffn_conv_b, ffn_w_down, consts, alibi, out):
    ctx = ExitStack()
    with ctx:
        def sem(name):
            return ctx.enter_context(nc.semaphore(name))

        def sems(name, n):
            return [sem(f"{name}{i}") for i in range(n)]

        def sb(name, shape, dt=F32, stack=ctx):
            return stack.enter_context(nc.sbuf_tensor(name, shape, dt))

        xT = sb("xT", [P, FT, L])
        hh = sb("hh", [P, FT, L], F32R)
        hl = sb("hl", [P, FT, L], F32R)
        raw = sb("raw", [P, 2, 2 * UNIT])
        wh = sb("wh", [P, 4, UNIT], F32R)
        wl = sb("wl", [P, 4, UNIT], F32R)
        ada_raw = sb("ada_raw", [P, 2, D])
        ada_acc = sb("ada_acc", [P, D])
        nt = sb("nt", [P, 4, L])
        rbs = sb("rbs", [P, L])
        cst = sb("cst", [P, C_N])
        ident_r = sb("ident_r", [P, P], F32R)
        causal_r = sb("causal_r", [P, P], F32R)
        vec = sb("vec", [P, 4, P])
        csil = sb("csil", [P, FT])
        mod = sb("mod", [P, 12, FT])
        mulA = sb("mulA", [P, 4, FT])
        gains = sb("gains", [P, 32])
        rv = sb("rv", [P, 8])
        rt = sb("rt", [P, 8])
        ry = sb("ry", [P, 8])
        ra = sb("ra", [P, 8])
        rb2 = sb("rb2", [P, 8])
        nmax = sb("nmax", [P, 16])
        rowsum = sb("rowsum", [P, 16])
        rrec = sb("rrec", [P, 16])
        widx = sb("widx", [P, TT * IH])
        top8 = sb("top8", [P, 3, 8])
        ident = cst[:, C_ID:C_ID + P]

        with ExitStack() as att:
            qk = sb("qk", [P, 16, L], stack=att)
            probsT = sb("probsT", [P, 4, L], stack=att)
            oP = sb("oP", [P, 2, TT, P], stack=att)
            biasq = sb("biasq", [P, L], F32R, stack=att)
            biask = sb("biask", [P, L], stack=att)
            biaskh = sb("biaskh", [P, 2, L], F32R, stack=att)
            cum = sb("cum", [P, L], stack=att)
            cumh = sb("cumh", [P, L], F32R, stack=att)
            with ExitStack() as proj:
                sqb = sb("sqb", [P, 2, L], stack=proj)
                qg = sb("qg", [P, 2, L], stack=proj)
                smr0 = sb("smr0", [P, FT, 16], stack=proj)
                smh0 = sb("smh0", [P, FT, P], F32R, stack=proj)
                sml0 = sb("sml0", [P, FT, P], F32R, stack=proj)
            with ExitStack() as proj:
                sb("sqb_qg", [P, 4, L], stack=proj)
                smr1 = sb("smr1", [P, FT, HD + IH], stack=proj)
                smh1 = sb("smh1", [P, FT, HD + IH], F32R, stack=proj)
                sml1 = sb("sml1", [P, FT, HD + IH], F32R, stack=proj)
                wT = sb("wT", [P, L], stack=proj)
            with ExitStack() as heads:
                qSh = sb("qSh", [P, 2, L], F32R, stack=heads)
                qSl = sb("qSl", [P, 2, L], F32R, stack=heads)
                kSh = sb("kSh", [P, 2, L], F32R, stack=heads)
                kSl = sb("kSl", [P, 2, L], F32R, stack=heads)
            sb("below_values", [P, 5 * 1024], stack=att)
            with ExitStack() as fox:
                v0 = sb("v0", [P, TT, D], stack=fox)
            with ExitStack() as dsa:
                v1 = sb("v1", [P, TT, NKV * HD], stack=dsa)
                score = sb("score", [P, 3, L], stack=dsa)
                masked = sb("masked", [P, TT, L], F32R, stack=dsa)
        probs = nt
        scr = probsT
        qidx = qk[:, 12:16, :]
        kidx = oP[:, 0, :, :].rearrange("p t d -> p (t d)")
        with ExitStack() as mlp:
            uh = sb("uh", [P, UT, L], F32R, stack=mlp)
            ul = sb("ul", [P, UT, L], F32R, stack=mlp)
            cv = sb("cv", [P, 2, L], stack=mlp)
        with ExitStack() as ends:
            xtok = sb("xtok", [P, TT, D], stack=ends)
            vrows = sb("vrows", [P, 4, P], stack=ends)
        with ExitStack() as ends2:
            outs = sb("outs", [P, TT, D], stack=ends2)

        bank = [ctx.enter_context(nc.psum_tensor(f"bank{i}", [P, 512], F32)) for i in range(8)]
        ST, RB, MISC, ADA = bank[4], bank[5], bank[6], bank[7]

        cst_in, c_in, vec_in, x_in, alibi_in, out_done = (sem(n) for n in ("cst_in", "c_in", "vec_in", "x_in", "alibi_in", "out_done"))
        raw_in = sems("raw_in", 2)
        w_hi = sem("w_hi")
        w_split = sem("w_split")
        unit_used = sem("unit_used")
        ada_in = sems("ada_in", 4)
        ada_used = sem("ada_used")
        ada_sum = sem("ada_sum")
        ada_done = sem("ada_done")
        vecT_ready, vec_done, csil_done = sem("vecT_ready"), sem("vec_done"), sem("csil_done")
        cst_done, xT_ready = sem("cst_done"), sem("xT_ready")
        x_done = sems("x_done", 5)
        sq_ready = sem("sq_ready")
        sq_added = sem("sq_added")
        ms_ready = sem("ms_ready")
        nD = sem("nD")
        nA = sem("nA")
        rms_ready = sem("rms_ready")
        t_ready, hf_ready, h_ready = sem("t_ready"), sem("hf_ready"), sem("h_ready")
        mul_ready = sem("mul_ready")
        sm_in, sm_hi, sm_ready = sems("sm_in", 2), sems("sm_hi", 2), sems("sm_ready", 2)
        tile_ready = sems("tile_ready", 2)
        kidx_ready = sem("kidx_ready")
        taken = sems("taken", 2)
        hsq_ready = sems("hsq_ready", 2)
        hms_ready = sems("hms_ready", 2)
        hD, hA = sems("hD", 2), sems("hA", 2)
        hrs_ready = sems("hrs_ready", 2)
        hrb_ready = sems("hrb_ready", 2)
        normed = sems("normed", 2)
        v_ready = sems("v_ready", 2)
        f_ready, f_act, f_dve = sem("f_ready"), sem("f_act"), sem("f_dve")
        bias_step = sems("bias_step", 2)
        bias_ready = sems("bias_ready", 2)
        wT_ready, w_ready, w_taken = sem("wT_ready"), sem("w_ready"), sem("w_taken")
        is_ready, relu_done, weighed, tk, mask_ready = (sem(n) for n in ("is_ready", "relu_done", "weighed", "tk", "mask_ready"))
        qk_high, qs_ready, kb_ready = sem("qk_high"), sem("qs_ready"), sem("kb_ready")
        s_ready, max_done, p_ready = sem("s_ready"), sem("max_done"), sem("p_ready")
        pt_ready, ptd_done, pta_done = sem("pt_ready"), sem("ptd_done"), sem("pta_done")
        pv_done, rec_done, o_done = sem("pv_done"), sem("rec_done"), sem("o_done")
        ot_ready, oh_done, ol_done = sem("ot_ready"), sem("oh_done"), sem("ol_done")
        y_ready = sems("y_ready", 4)
        a_ready, g_ready = sems("a_ready", 2), sems("g_ready", 2)
        tap2, tap1, conv_done, silu_done = sems("tap2_", 2), sems("tap1_", 2), sems("conv_done", 2), sems("silu_done", 2)
        uf_done, uh_done, u_done = sems("uf_done", 2), sems("uh_done", 2), sems("u_done", 2)
        oT_ready, oT_done = sem("oT_ready"), sem("oT_done")
        waits_passed = sem("waits_passed")

        block = ctx.enter_context(nc.Block())

        def wait_alone(eng, semaphore, count):
            eng.wait_ge(semaphore, count)
            eng.sem_inc(waits_passed, 1)

        def half(tensor, h):
            return tensor[64 * (h % 2):64 * (h % 2) + 64]

        def pair_tiles(l, g, p):
            return qk[:, ds(2 * g + p, 1), :], qk[:, ds(8 + (2 * g + p if l == 0 else g), 1), :]

        def turned_bank(s):
            return bank[4 + (s + (s >= 4) + (s >= 12)) % 2]

        def pair_bank(p):
            return bank[5 - p]

        @block.sync
        def _(sp):
            def load(n, slot, src, first=False):
                if not first:
                    sp.wait_ge(w_split, 2 * n - 2)
                dst = raw[:, slot, :]
                sp.dma_start(dst.rearrange("p (k c) -> p k c", k=src.shape[1]), src).then_inc(raw_in[slot], 16)

            def load_cols(n, slot, w, col, first=False):
                load(n, slot, w.rearrange("(k p) c -> p k c", p=P)[:, :, ds(col, 256)], first)

            def load_rows(n, slot, w, k):
                load(n, slot, w.rearrange("(k p) c -> p k c", p=P)[:, ds(k, 2), :])

            def ada_slices(layer, q, part, ks=range(FT)):
                for k in ks:
                    sp.wait_ge(ada_used, 8 * q + k - 1)
                    sp.dma_start(ada_raw[:, k % 2, :], w_ada[layer, k * P:(k + 1) * P, ds(part * D, D)]).then_inc(ada_in[k % 2], 16)

            def ada_start(q):
                for k in range(FT):
                    if 8 * q + k >= 4:
                        sp.wait_ge(ada_used, 8 * q + k - 3)
                    sp.dma_start(v0[:, k % 4, :], w_ada[0, k * P:(k + 1) * P, q * D:(q + 1) * D]).then_inc(ada_in[k % 4], 16)

            sp.dma_start(cst[:], consts).then_inc(cst_in, 16)
            sp.dma_start(vrows[V_BADA:V_C, 2, :], b_ada.rearrange("l (m p) -> (l m) p", p=P)).then_inc(c_in, 16)
            sp.dma_start(vrows[V_C:V_ROWS, 2, :], c.rearrange("a (m p) -> (a m) p", p=P)).then_inc(c_in, 16)
            for t in range(TT):
                sp.dma_start(xtok[:, t, :], x[0, t * P:(t + 1) * P, :]).then_inc(x_in, 16)
            ada_start(0)
            load_cols(0, 0, fox_w_in[0], 0, first=True)
            for l in range(2):
                sp.dma_start(vrows[V_CONVW:V_CONVB, l, :], ffn_conv_w[l].rearrange("w (m p) -> (w m) p", p=P)).then_inc(vec_in, 16)
                sp.dma_start(vrows[V_CONVB:V_GMIX, l, :], ffn_conv_b[l].rearrange("(m p) -> m p", p=P)).then_inc(vec_in, 16)
                sp.dma_start(vrows[V_GMIX:V_GFFN, l, :], g_norm_mix[l].rearrange("(m p) -> m p", p=P)).then_inc(vec_in, 16)
                sp.dma_start(vrows[V_GFFN:V_ROWS, l, :], g_norm_ffn[l].rearrange("(m p) -> m p", p=P)).then_inc(vec_in, 16)
            for row, g, n in ((G_FOXQ, fox_g_q, 2), (G_FOXK, fox_g_k, 2), (G_DSAQ, dsa_g_q, 2), (G_DSAK, dsa_g_k, 2),
                              (G_KIDX, dsa_g_kidx, 2), (G_BF, fox_b_f, 8)):
                sp.dma_start(vrows[row:row + 1, 3, :].rearrange("a (e d) -> a e d", e=n),
                             g.unsqueeze(1).to_broadcast([1, n, P // n])).then_inc(vec_in, 16)
            sp.dma_start(smr0[:], fox_w_in[0].rearrange("(k p) c -> p k c", p=P)[:, :, 3 * D:3 * D + NH]).then_inc(sm_in[0], 16)
            ada_start(1)
            load_cols(1, 1, fox_w_in[0], 256, first=True)
            for s in range(2):
                load_cols(2 + s, s, fox_w_in[0], 512 + 256 * s)
            with sp.Fori(1, 4) as i:
                for s in range(2):
                    load_cols(2 * i + 2 + s, s, fox_w_in[0], 512 * i + 512 + 256 * s)
                    ada_slices(0, 1 + i, 1 + i, range(4 * s, 4 * s + 4))
            for i in range(2):
                for s in range(2):
                    if i == 0:
                        load_cols(10 + s, s, fox_w_in[0], 2560 + 256 * s)
                    else:
                        load_rows(FOX_OUT + s, s, fox_w_out[0], 2 * s)
                    ada_slices(i, 5 + i, 5 * (1 - i), range(4 * s, 4 * s + 4))
            for j in (2, 3):
                load_rows(FOX_OUT + j, j % 2, fox_w_out[0], 2 * j)

            def mlp_loads(l, up, down):
                def columns(i, between=lambda e: None):
                    load_cols(up + 2 * i, up % 2, ffn_w_up[l], 256 * i)
                    between(0)
                    load_cols(up + 2 * i + 1, (up + 1) % 2, ffn_w_up[l], FF + 256 * i)
                    between(2)
                if l == 0:
                    columns(0)
                    with sp.Fori(0, 5) as j:
                        for e in range(2):
                            columns(2 * j + e + 1, lambda k: ada_slices(1, 7 + j, 1 + j, range(4 * e + k, 4 * e + k + 2)))
                else:
                    with sp.Fori(0, 11) as i:
                        columns(i)
                load_rows(down, down % 2, ffn_w_down[l], 0)
                with sp.Fori(0, 5) as i:
                    for s in range(2):
                        load_rows(down + 1 + 2 * i + s, (down + 1 + s) % 2, ffn_w_down[l], 2 + 4 * i + 2 * s)

            mlp_loads(0, FOX_UP, FOX_DOWN)
            for j in range(2):
                load_cols(DSA_IDX + j, (DSA_IDX + j) % 2, dsa_w_in[0], 1536 + 256 * j)
            sp.wait_ge(x_done[2], FT)
            sp.dma_start(smr1[:], dsa_w_in[0].rearrange("(k p) c -> p k c", p=P)[:, :, 2048:2120]).then_inc(sm_in[1], 16)
            sp.dma_start(cum[:], alibi).then_inc(alibi_in, 16)
            load_cols(DSA_K, DSA_K % 2, dsa_w_in[0], 1024)
            for j in range(4):
                load_cols(DSA_Q + j, (DSA_Q + j) % 2, dsa_w_in[0], 256 * j)
            load_cols(DSA_V, DSA_V % 2, dsa_w_in[0], 1280)
            for j in range(4):
                load_rows(DSA_OUT + j, (DSA_OUT + j) % 2, dsa_w_out[0], 2 * j)
            mlp_loads(1, DSA_UP, DSA_DOWN)
            for e in range(2):
                sp.wait_ge(oT_done, 4 * e + 4)
                sp.dma_start(out[0].rearrange("(t p) d -> p t d", p=P)[:, :, 512 * e:512 * e + 512],
                             outs[:, :, 512 * e:512 * e + 512]).then_inc(out_done, 16)
            sp.wait_ge(out_done, 32)

        @block.gpsimd
        def _(pool):
            def split(i, s, u, first):
                n = 2 * s + u
                src = raw[:, s, u * UNIT:(u + 1) * UNIT]
                if not first:
                    wait_alone(pool, unit_used, 4 * i + n - 3)
                pool.tensor_scalar(wh[:, n, :], src, 1.0, 1.0, ALU.mult, ALU.mult).then_inc(w_hi, 1)
                pool.wait_ge(w_hi, 4 * i + n + 1)
                pool.tensor_tensor(wl[:, n, :], src, wh[:, n, :].bitcast(F32), ALU.subtract).then_inc(w_split, 1)

            def split_loads(first, end):
                with pool.Fori(first // 2, end // 2) as i:
                    for s in range(2):
                        pool.wait_ge(raw_in[s], 16 * i + 16)
                        for u in range(2):
                            split(i, s, u, False)

            def split_heads(l):
                with pool.Fori(4 * l, 4 * l + 4) as i:
                    for p in range(2):
                        q, k = pair_tiles(l, i - 4 * l, p)
                        wait_alone(pool, qk_high, 4 * i + 2 * p + 2)
                        pool.tensor_tensor(qSl[:, p:p + 1, :], q, qSh[:, p:p + 1, :].bitcast(F32), ALU.subtract).then_inc(qs_ready, 1)
                        pool.tensor_tensor(kSl[:, p:p + 1, :], k, kSh[:, p:p + 1, :].bitcast(F32), ALU.subtract).then_inc(qs_ready, 1)

            for s in range(2):
                pool.wait_ge(raw_in[s], 16)
                for u in range(2):
                    split(0, s, u, True)
            split_loads(2, FOX_OUT + 2)
            split_heads(0)
            split_loads(FOX_OUT + 2, DSA_OUT + 1)
            split_heads(1)
            split_loads(DSA_OUT + 1, LOADS)

        @block.tensor
        def _(pe):
            def mm3(dst, wa, wb, xa, xb, start, stop, signal=None):
                mm = pe.matmul(dst, wa, xa, start=start, stop=False)
                if signal:
                    mm.then_inc(signal, 1)
                pe.matmul(dst, wa, xb, start=False, stop=False)
                return pe.matmul(dst, wb, xa, start=False, stop=stop)

            def unit_cols(load, u):
                n = (2 * load + u) % 4
                return (wh[:, n, :].rearrange("p (k c) -> p k c", k=4), wl[:, n, :].rearrange("p (k c) -> p k c", k=4))

            def first_loads(n, load, dsts, readies, more=lambda k: None):
                for k in range(FT):
                    u = k // 4
                    pe.wait_ge(h_ready, FT * n + k + 1)
                    more(k)
                    for e in range(2):
                        a, b = unit_cols(load + e, u)
                        if k % 4 == 0:
                            pe.wait_ge(w_split, 2 * (load + e) + u + 1)
                        for c in range(2):
                            cols = slice(c * P, (c + 1) * P)
                            mm = mm3(dsts[2 * e + c], a[:, k % 4, cols], b[:, k % 4, cols], hh[:, k, :], hl[:, k, :],
                                     k == 0, k == FT - 1, unit_used if (k, e, c) == (FT - 1, 1, 0) else None)
                            if (k, e, c) == (3, 0, 1) or (k == FT - 1 and c == 1):
                                mm.then_inc(unit_used, 1)
                            if k == FT - 1 and c == 0:
                                mm.then_inc(readies[e], 1)

            def proj_tile(load, load_e, c, dst, ready, middle=lambda: None):
                for u in range(2):
                    a, b = unit_cols(load, u)
                    if c == 0:
                        pe.wait_ge(w_split, 2 * load_e + u + 1)
                    cols = slice(c * P, (c + 1) * P)
                    for k in range(4):
                        mm = mm3(dst, a[:, k, cols], b[:, k, cols], hh[:, 4 * u + k, :], hl[:, 4 * u + k, :],
                                 start=(u == 0 and k == 0), stop=(u == 1 and k == 3))
                    if c == 1:
                        mm.then_inc(unit_used, 1)
                    if u == 0:
                        middle()
                if c == 0:
                    mm.then_inc(ready, 1)

            def rows_load(n, load, load_e, xs, first, last, order=range(FT), before=None):
                for m in order:
                    if before:
                        before(m)
                    for u in range(2):
                        if m == order[0]:
                            pe.wait_ge(w_split, 2 * load_e + u + 1)
                        s = (2 * load + u) % 4
                        xa, xb = xs(u)
                        mm = mm3(bank[m][:], wh[:, s, m * P:(m + 1) * P], wl[:, s, m * P:(m + 1) * P], xa, xb,
                                 start=(first and u == 0), stop=(last and u == 1))
                        if m == order[-1]:
                            mm.then_inc(unit_used, 1)
                    if last and m != order[-1]:
                        mm.then_inc(y_ready[n], 1)

            def ada(q):
                pe.wait_ge(ada_used, 8 * q + 8)
                for m in range(FT):
                    mm = pe.matmul(ADA[:, m:m + 1], ada_acc[:, m * P:(m + 1) * P], cst[:, C_ONE:C_ONE + 1], start=True, stop=True)
                mm.then_inc(ada_sum, 1)

            def norm(n):
                pe.wait_ge(sq_added, (FT - 1) * n + FT - 1)
                for t in range(TT):
                    mm = pe.matmul(ST[:, t:t + 1], nt[:, 0, t * P:(t + 1) * P], cst[:, C_ONE:C_ONE + 1], start=True, stop=True)
                mm.then_inc(ms_ready, 1)
                pe.wait_ge(nD, 5 * n + 5)
                for t in range(TT):
                    mm = pe.transpose(RB[:, t * P:(t + 1) * P], rbs[:, t * P:(t + 1) * P], ident)
                mm.then_inc(rms_ready, 1)

            def stat(l, te, t, rows=P):
                pe.wait_ge(hsq_ready[l], te + 1)
                if t > 0:
                    pe.wait_ge(hD[l], 4 * te - 3)
                for j in range(TT):
                    mm = pe.matmul(ST[:, 2 * j:2 * j + 2], sqb[0:rows, t % 2, j * P:(j + 1) * P], cst[0:rows, C_BLOCK:C_BLOCK + 2],
                                   start=True, stop=True)
                mm.then_inc(hms_ready[l], 1)

            def spread(l, te):
                pe.wait_ge(hrs_ready[l], te + 1)
                pe.wait_ge(normed[l], te)
                for j in range(TT):
                    mm = pe.transpose(RB[:, j * P:(j + 1) * P], rbs[:, j * P:(j + 1) * P], ident)
                mm.then_inc(hrb_ready[l], 1)

            def v_load(l, load, load_e, emptied):
                for u in range(2):
                    a, b = unit_cols(load, u)
                    pe.wait_ge(w_split, 2 * load_e + u + 1)
                    for t in range(TT):
                        if u == 0:
                            pe.wait_ge(taken[l], emptied(t))
                        tok = slice(t * P, (t + 1) * P)
                        for k in range(4):
                            kk = 4 * u + k
                            mm = mm3(bank[t][:, 0:256], hh[:, kk, tok], hl[:, kk, tok], a[:, k, :], b[:, k, :],
                                     start=(kk == 0), stop=(kk == 7))
                        if u == 1 and t < TT - 1:
                            mm.then_inc(v_ready[l], 1)
                    mm.then_inc(unit_used, 1)

            def attention(l):
                def scores(i, s):
                    h, t = divmod(s, TT)
                    n = (t + 1) * P
                    if t == 0:
                        pe.wait_ge(qs_ready, 4 * i + 2 * (h // 2) + 2)
                        pe.wait_ge(kb_ready, 4 * i + h + 1)
                    S = bank[s % 4]
                    tok = slice(t * P, (t + 1) * P)
                    mm3(S[:, 0:n], half(qSh, h)[:, h // 2, tok], half(qSl, h)[:, h // 2, tok],
                        half(kSh, h)[:, h // 2, 0:n], half(kSl, h)[:, h // 2, 0:n], True, False)
                    pe.matmul(S[:, 0:n], half(biasq, h)[:, tok], half(biaskh, h)[:, h % 2, 0:n], start=False, stop=False)
                    if l == 0:
                        mm = pe.matmul(S[:, t * P:n], ident_r[:], causal_r[:], start=False, stop=True)
                    else:
                        mm = pe.matmul(S[:, 0:n], ident_r[:], masked[:, t, 0:n], start=False, stop=True)
                    mm.then_inc(s_ready, 1)

                def wait_turned(i, s):
                    pe.wait_ge(pta_done if s % 2 else ptd_done, 8 * i + s // 2 + 1)

                def turn(i, s, first):
                    pe.wait_ge(p_ready, 16 * i + s + 1)
                    if s in (4, 12):
                        wait_turned(i, s - 1)
                    if s == 5 and not first:
                        pe.wait_ge(ol_done, 2 * i)
                    if s == 13:
                        pe.wait_ge(ol_done, 2 * i + 1)
                    for j in range(s % TT + 1):
                        mm = pe.transpose(turned_bank(s)[:, j * P:(j + 1) * P], probs[:, s % 4, j * P:(j + 1) * P], ident)
                    mm.then_inc(pt_ready, 1)

                def values(i, s, first):
                    h, t = divmod(s, TT)
                    wait_turned(i, s)
                    if t == 0 and (h >= 2 or not first):
                        pe.wait_ge(o_done, 4 * i + h - 1)
                    for j in range(t + 1):
                        vj = v0[:, j, ds(256 * i + HD * h, HD)] if l == 0 else v1[:, j, ds(HD * (i - 4), HD)]
                        mm = pe.matmul(bank[6 + h % 2][:, t * HD:(t + 1) * HD], probsT[:, s % 4, j * P:(j + 1) * P], vj,
                                       start=(j == 0), stop=(j == t))
                    mm.then_inc(pv_done, 1)

                def turn_pair(i, p):
                    pe.wait_ge(o_done, 4 * i + 2 * p + 2)
                    for t in range(TT):
                        mm = pe.transpose(pair_bank(p)[:, t * P:(t + 1) * P], oP[:, p, t, :], ident)
                    mm.then_inc(ot_ready, 1)

                def round_(i, first, last):
                    for s in range(16):
                        if s >= 2:
                            values(i, s - 2, first)
                        elif not first:
                            values(i - 1, s + 14, False)
                        turn(i, s, first)
                        if s < 13:
                            scores(i, s + 3)
                        elif not last:
                            scores(i + 1, s - 13)
                        if s == 3 and not first:
                            wait_turned(i, 2)
                            turn_pair(i - 1, 1)
                        if s == 11:
                            wait_turned(i, 10)
                            turn_pair(i, 0)

                if l == 0:
                    pe.wait_ge(ada_done, 7)
                for s in range(3):
                    scores(4 * l, s)
                round_(4 * l, True, False)
                with pe.Fori(4 * l + 1, 4 * l + 3) as i:
                    round_(i, False, False)
                i = 4 * l + 3
                round_(i, False, True)
                values(i, 14, False)
                values(i, 15, False)
                turn_pair(i, 1)

            def out_proj(l, load):
                pe.wait_ge(ol_done, 8 * l + 8)
                for j in range(4):
                    rows_load(2 * l, load + j, load + j, lambda u: (hh[:, 2 * j + u, :], hl[:, 2 * j + u, :]), j == 0, j == 3)

            def mlp_layer(l, up, dn):
                n = 2 * l + 1
                norm(n)

                def up_body(i):
                    pe.wait_ge(conv_done[l], 2 * i)
                    proj_tile(up, up + 2 * i, 0, bank[0][:], a_ready[l])
                    proj_tile(up, up + 2 * i, 1, bank[1][:], None)
                    pe.wait_ge(uf_done[l], 2 * i)
                    proj_tile(up + 1, up + 2 * i + 1, 0, bank[2][:], g_ready[l])
                    proj_tile(up + 1, up + 2 * i + 1, 1, bank[3][:], None)

                first_loads(n, up, [bank[b][:] for b in range(4)], (a_ready[l], g_ready[l]))
                if l == 0:
                    up_body(1)
                    ada(7)
                    with pe.Fori(1, 5) as j:
                        up_body(2 * j)
                        up_body(2 * j + 1)
                        ada(7 + j)
                    up_body(10)
                else:
                    with pe.Fori(1, 11) as i:
                        up_body(i)

                def hidden(k):
                    return (uh[:, ds(k, 1), :].rearrange("p a n -> p (a n)"), ul[:, ds(k, 1), :].rearrange("p a n -> p (a n)"))

                def before(m):
                    if m == 0:
                        pe.wait_ge(uf_done[l], UT)

                if l == 0:
                    pe.wait_ge(ada_done, 12)
                pe.wait_ge(u_done[l], UT - 1)
                rows_load(n, dn, dn, lambda u: (uh[:, u, :], ul[:, u, :]), True, False, order=[4, 5, 6, 7, 0, 1, 2, 3], before=before)
                with pe.Fori(0, 4) as i:
                    for s in range(2):
                        rows_load(n, dn + 1 + s, dn + 1 + s + 2 * i, lambda u: hidden(4 * i + 2 + 2 * s + u), False, False)
                pe.wait_ge(u_done[l], UT + 1)
                for j in (9, 10):
                    rows_load(n, dn + j, dn + j, lambda u: (uh[:, 2 * j + u, :], ul[:, 2 * j + u, :]), False, j == 10)

            for s_ in (u_done[0], u_done[1]):
                pe.sem_inc(s_, 1)

            pe.wait_ge(cst_in, 16)
            pe.wait_ge(c_in, 32)
            pe.transpose(MISC[:, 2 * P:2 * P + V_ROWS], vrows[0:V_ROWS, 2, :], cst[0:V_ROWS, C_ID:C_ID + V_ROWS]).then_inc(vecT_ready, 1)
            pe.wait_ge(x_in, 16 * TT)
            for m in range(FT):
                if m >= 4:
                    pe.wait_ge(x_done[0], m - 3)
                for t in range(TT):
                    mm = pe.transpose(bank[m % 4][:, t * P:(t + 1) * P], xtok[:, t, m * P:(m + 1) * P], ident)
                mm.then_inc(xT_ready, 1)
            ada(0)
            pe.wait_ge(vec_in, 16 * (8 + 6))
            for j, rows in ((0, V_ROWS), (1, V_ROWS), (3, G_ROWS)):
                mm = pe.transpose(MISC[:, j * P:j * P + rows], vrows[0:rows, j, :], cst[0:rows, C_ID:C_ID + rows])
            mm.then_inc(vecT_ready, 1)
            ada(1)

            norm(0)
            pe.wait_ge(sm_ready[0], 8)

            def gate_logits(k):
                mm = mm3(MISC[:], smh0[:, k, :], sml0[:, k, :], hh[:, k, :], hl[:, k, :], k == 0, k == FT - 1)
                if k == FT - 1:
                    mm.then_inc(f_ready, 1)

            first_loads(0, 0, [bank[b][:] for b in range(4)], (tile_ready[0], tile_ready[0]), gate_logits)
            stat(0, 0, 0)

            def beat(te, t):
                stat(0, te, t)
                spread(0, te - 1)

            def fox_tile(i, c_, middle=lambda: None):
                pe.wait_ge(taken[0], 4 * i + c_ - 3)
                proj_tile(c_ // 2, 2 * i + c_ // 2, c_ % 2, bank[c_][:], tile_ready[0], middle)
                beat(4 * i + c_ - 1, c_ + 3)

            pe.wait_ge(taken[0], 1)
            proj_tile(0, 2, 0, bank[0][:], tile_ready[0], lambda: beat(1, 1))
            beat(2, 2)
            pe.wait_ge(taken[0], 2)
            proj_tile(0, 2, 1, bank[1][:], tile_ready[0], lambda: beat(3, 3))
            beat(4, 4)
            fox_tile(1, 2)
            fox_tile(1, 3)
            ada(2)
            with pe.Fori(2, 4) as i:
                for c_ in range(4):
                    fox_tile(i, c_)
                ada(1 + i)
            beat(15, 15)
            for j in range(4):
                v_load(0, j % 2, 8 + j, lambda t: 4 * j + 13 + t)
                if j == 0:
                    spread(0, 15)
                if j % 2:
                    ada(5 + j // 2)
            pe.wait_ge(taken[0], 32)
            pe.wait_ge(normed[0], 16)
            attention(0)
            out_proj(0, FOX_OUT)
            mlp_layer(0, FOX_UP, FOX_DOWN)

            norm(2)
            first_loads(2, DSA_IDX, [bank[b][:] for b in (1, 2, 3, 0)], (tile_ready[1], tile_ready[1]))
            pe.wait_ge(sm_ready[1], 1)
            for k in range(FT):
                mm = mm3(bank[7][0:HD + IH, :], smh1[:, k, :], sml1[:, k, :], hh[:, k, :], hl[:, k, :], k == 0, k == FT - 1)
            mm.then_inc(kidx_ready, 1)
            pe.wait_ge(wT_ready, 1)
            for t in range(TT):
                mm = pe.transpose(MISC[:, IH * t:IH * t + IH], wT[HD:HD + IH, t * P:(t + 1) * P], cst[HD:HD + IH, C_ID + HD:C_ID + HD + IH])
            mm.then_inc(w_ready, 1)
            stat(1, 0, 0, HD)
            spread(1, 0)
            pe.wait_ge(taken[1], 5)
            pe.wait_ge(normed[1], 1)
            pe.wait_ge(w_taken, 1)
            for e in range(3 * IH):
                h, t = e // 3, 1 + e % 3
                n = (t + 1) * P
                if e >= 2:
                    pe.wait_ge(relu_done, e - 1)
                pe.matmul(bank[6 + e % 2][:, 0:n], half(qidx, h)[:, h // 2, t * P:(t + 1) * P], half(kidx, h)[:, 0:n],
                          start=True, stop=True).then_inc(is_ready, 1)
            for c_ in range(2):
                proj_tile(DSA_K, DSA_K, c_, bank[1 + c_][:], tile_ready[1])
            stat(1, 1, 1)
            with pe.Fori(0, 2) as i:
                for c_ in range(4):
                    pe.wait_ge(taken[1], 4 * i + c_ + 4)
                    proj_tile(DSA_Q + c_ // 2, DSA_Q + c_ // 2 + 2 * i, c_ % 2, bank[(3 + c_) % 4][:], tile_ready[1])
                    stat(1, 4 * i + c_ + 2, c_ + 2)
                    spread(1, 4 * i + c_ + 1)
            stat(1, 10, 10)
            spread(1, 9)
            v_load(1, DSA_V, DSA_V, lambda t: 15)
            spread(1, 10)
            pe.wait_ge(taken[1], 19)
            pe.wait_ge(normed[1], 11)
            pe.wait_ge(relu_done, 3 * IH)
            pe.wait_ge(mask_ready, 4)
            attention(1)
            out_proj(1, DSA_OUT)
            mlp_layer(1, DSA_UP, DSA_DOWN)

            for m in range(FT):
                pe.wait_ge(x_done[4], m + 1)
                if m >= 4:
                    pe.wait_ge(oT_done, m - 3)
                for t in range(TT):
                    mm = pe.transpose(bank[m % 4][:, t * P:(t + 1) * P], xT[:, m, t * P:(t + 1) * P], ident)
                mm.then_inc(oT_ready, 1)

        @block.scalar
        def _(act):
            one = cst[:, C_ONE:C_ONE + 1]

            def squares(n, m):
                act.wait_ge(x_done[n], m + 1)
                if m >= 3:
                    act.wait_ge(sq_added, (FT - 1) * n + m - 2)
                act.activation(nt[:, 0 if m == 0 else 1 + m % 2, :], xT[:, m, :], ACT.Square).then_inc(sq_ready, 1)

            def root(steps_d, steps_a, n_d, cols):
                act.wait_ge(steps_d, n_d)
                act.activation(rt[:, 0:cols], rv[:, 0:cols], ACT.Sqrt).then_inc(steps_a, 1)

            def modulate(n):
                root(nD, nA, 5 * n + 1, TT)
                act.wait_ge(mul_ready, n + 1)
                shift = 3 * n
                for k in range(FT):
                    act.wait_ge(t_ready, FT * n + k + 1)
                    args = dict(scale=mulA[:, n, k:k + 1], bias=mod[:, shift, k:k + 1])
                    act.activation(hh[:, k, :], nt[:, k % 2, :], ACT.Identity, **args)
                    if k >= 2:
                        act.wait_ge(h_ready, FT * n + k - 1)
                    act.activation(nt[:, 2 + k % 2, :], nt[:, k % 2, :], ACT.Identity, **args).then_inc(hf_ready, 1)

            def take(l, te, t, b, gain, sem_, count):
                act.wait_ge(sem_, count)
                if t >= 2:
                    act.wait_ge(hms_ready[l], te - 1)
                act.activation(sqb[:, t % 2, :], bank[b][:], ACT.Square).then_inc(hsq_ready[l], 1)
                if t >= 2:
                    act.wait_ge(normed[l], te - 1)
                act.activation(qg[:, t % 2, :], bank[b][:], ACT.Identity, scale=gain).then_inc(taken[l], 1)

            def attention(l):
                def probabilities(i, s):
                    n = (s % TT + 1) * P
                    act.wait_ge(max_done, 16 * i + s + 1)
                    act.activation(probs[:, s % 4, 0:n], bank[s % 4][:, 0:n], ACT.Exp, bias=nmax[:, s:s + 1],
                                   accum_out=rowsum[:, s:s + 1]).then_inc(p_ready, 1)

                def turned(i, s):
                    n = (s % TT + 1) * P
                    act.wait_ge(pt_ready, 16 * i + s + 1)
                    act.copy(probsT[:, s % 4, 0:n], turned_bank(s)[:, 0:n]).then_inc(pta_done, 1)

                def out_high(i, p):
                    act.wait_ge(ot_ready, 2 * i + p + 1)
                    act.copy(hh[:, ds(2 * (i - 4 * l) + p, 1), :], pair_bank(p)[:].rearrange("p (a n) -> p a n", a=1)).then_inc(oh_done, 1)

                def pair_high(g, p):
                    q, k = pair_tiles(l, g, p)
                    act.copy(qSh[:, p:p + 1, :], q).then_inc(qk_high, 1)
                    act.copy(kSh[:, p:p + 1, :], k).then_inc(qk_high, 1)

                def round_(i, first, last):
                    for s in range(16):
                        if s == 4 and not first:
                            out_high(i - 1, 1)
                        if s == 12:
                            out_high(i, 0)
                        if s % 2:
                            turned(i, s)
                        if s < 13:
                            probabilities(i, s + 3)
                        elif not last:
                            probabilities(i + 1, s - 13)
                        if s == 6 and not last:
                            pair_high(i - 4 * l + 1, 0)
                        if s == 14 and not last:
                            pair_high(i - 4 * l + 1, 1)

                act.wait_ge(normed[l], 16 if l == 0 else 11)
                pair_high(0, 0)
                pair_high(0, 1)
                for s in range(3):
                    probabilities(4 * l, s)
                round_(4 * l, True, False)
                with act.Fori(4 * l + 1, 4 * l + 3) as i:
                    round_(i, False, False)
                round_(4 * l + 3, False, True)
                out_high(4 * l + 3, 1)

            def mlp_layer(l, up):
                n = 2 * l + 1
                modulate(n)
                col = vec[:, l, :]

                def up_body(i):
                    for c_ in range(2):
                        if c_ == 0:
                            act.wait_ge(a_ready[l], i + 1)
                            act.wait_ge(u_done[l], 2 * i + 1)
                        else:
                            act.wait_ge(unit_used, 2 * (up + 2 * i) + 2)
                        tau = 2 * i + c_
                        act.activation(cv[:, c_, :], bank[c_][:], ACT.Identity, scale=col[:, ds(V_CONVW + 2 * UT + tau, 1)],
                                       bias=col[:, ds(V_CONVB + tau, 1)]).then_inc(tap2[l], 1)
                    for c_ in range(2):
                        act.wait_ge(conv_done[l], 2 * i + c_ + 1)
                        act.activation(cv[:, c_, :], cv[:, c_, :], ACT.Silu).then_inc(silu_done[l], 1)
                    for c_ in range(2):
                        act.wait_ge(uf_done[l], 2 * i + c_ + 1)
                        act.copy(uh[:, ds(2 * i + c_, 1), :], cv[:, c_:c_ + 1, :]).then_inc(uh_done[l], 1)

                with act.Fori(0, 11) as i:
                    up_body(i)

            act.wait_ge(vec_done, 1)
            act.activation(csil[:], vec[:, 2, V_C:V_ROWS], ACT.Silu).then_inc(csil_done, 1)
            for m in range(FT):
                act.wait_ge(xT_ready, m + 1)
                act.copy(xT[:, m, :], bank[m % 4][:]).then_inc(x_done[0], 1)
                squares(0, m)

            modulate(0)
            def fox_tile(i, c_, first):
                tau = 4 * i + c_
                sem_, count = (tile_ready[0], 2 * i + c_ // 2 + 1) if c_ % 2 == 0 else (unit_used, 2 * (2 * i + c_ // 2) + 2)
                take(0, tau, c_ if first else c_ + 4, c_, gains[:, ds(GAIN[0] + tau, 1)], sem_, count)
                if not (first and c_ == 0):
                    root(hD[0], hA[0], 4 * (tau - 1) + 1, 8)

            for c_ in range(4):
                fox_tile(0, c_, True)
            with act.Fori(1, 4) as i:
                for c_ in range(4):
                    fox_tile(i, c_, False)
            root(hD[0], hA[0], 4 * 15 + 1, 8)

            def take_v(l, je, load_e, dst, t):
                if t < TT - 1:
                    act.wait_ge(v_ready[l], 3 * je + t + 1)
                else:
                    act.wait_ge(unit_used, 2 * load_e + 2)
                act.copy(dst, bank[t][:, 0:256]).then_inc(taken[l], 1)

            for t in range(TT):
                take_v(0, 0, 8, v0[:, t, 0:256], t)
            act.wait_ge(f_ready, 1)
            act.activation(scr[:, 0, :], MISC[:], ACT.Identity, bias=vec[:, 3, G_BF:G_BF + 1]).then_inc(f_act, 1)
            act.wait_ge(f_act, 1)
            act.activation(scr[:, 1, :], scr[:, 0, :], ACT.Abs).then_inc(f_act, 1)
            act.wait_ge(f_act, 2)
            act.activation(scr[:, 2, :], scr[:, 1, :], ACT.Exp, scale=-1.0).then_inc(f_act, 1)
            act.wait_ge(f_act, 3)
            act.activation(scr[:, 3, :], scr[:, 2, :], ACT.Ln, bias=one).then_inc(f_act, 1)
            with act.Fori(1, 4) as j:
                for t in range(TT):
                    take_v(0, j, 8 + j, v0[:, t, ds(256 * j, 256)], t)
            attention(0)
            for m in range(FT):
                squares(1, m)
            mlp_layer(0, FOX_UP)
            for m in range(FT):
                squares(2, m)

            modulate(2)
            for j in range(2):
                for c_ in range(2):
                    if c_ == 0:
                        act.wait_ge(tile_ready[1], j + 1)
                    else:
                        act.wait_ge(unit_used, 2 * (DSA_IDX + j) + 2)
                    act.copy(qidx[:, 2 * j + c_, :], bank[(1 + 2 * j + c_) % 4][:]).then_inc(taken[1], 1)
            act.wait_ge(kidx_ready, 1)
            act.copy(wT[HD:HD + IH, :], bank[7][HD:HD + IH, :]).then_inc(wT_ready, 1)
            act.activation(sqb[0:HD, 0, :], bank[7][0:HD, :], ACT.Square).then_inc(hsq_ready[1], 1)
            act.activation(qg[0:HD, 0, :], bank[7][0:HD, :], ACT.Identity, scale=gains[0:HD, GAIN[1]:GAIN[1] + 1]).then_inc(taken[1], 1)
            root(hD[1], hA[1], 1, 8)
            for e in range(3 * IH):
                n = (2 + e % 3) * P
                act.wait_ge(is_ready, e + 1)
                if e >= 2:
                    act.wait_ge(weighed, e - 1)
                act.activation(scr[:, e % 2, 0:n], bank[6 + e % 2][:, 0:n], ACT.Relu).then_inc(relu_done, 1)
            take(1, 1, 1, 1, gains[:, GAIN[1] + 1:GAIN[1] + 2], tile_ready[1], 3)
            take(1, 2, 2, 2, gains[:, GAIN[1] + 2:GAIN[1] + 3], unit_used, 2 * DSA_K + 2)
            root(hD[1], hA[1], 5, 8)
            with act.Fori(0, 2) as i:
                for c_ in range(4):
                    tau = 4 * i + c_ + 3
                    sem_, count = (tile_ready[1], 2 * i + c_ // 2 + 4) if c_ % 2 == 0 else (unit_used, 2 * (DSA_Q + c_ // 2 + 2 * i) + 2)
                    take(1, tau, c_ + 3, (3 + c_) % 4, gains[:, ds(GAIN[1] + tau, 1)], sem_, count)
                    root(hD[1], hA[1], 4 * (tau - 1) + 1, 8)
            root(hD[1], hA[1], 4 * 10 + 1, 8)
            for t in range(TT):
                take_v(1, 0, DSA_V, v1[:, t, :], t)
            attention(1)
            for m in range(FT):
                squares(3, m)
            mlp_layer(1, DSA_UP)

        @block.vector
        def _(dve):
            def add_squares(n, m):
                dve.wait_ge(sq_ready, FT * n + m + 1)
                if m >= 2:
                    dve.wait_ge(sq_added, (FT - 1) * n + m - 1)
                dve.tensor_tensor(nt[:, 0, :], nt[:, 0, :], nt[:, 1 + m % 2, :], ALU.add).then_inc(sq_added, 1)

            def mean_square(ready, count, steps, cols, width):
                dve.wait_ge(ready, count)
                dve.tensor_scalar(rv[:, 0:cols], ST[:, 0:cols], 1.0 / width, EPS, ALU.mult, ALU.add).then_inc(steps, 1)

            def newton(steps_d, steps_a, d0, a0, cols, last):
                dve.wait_ge(steps_a, a0 + 1)
                dve.reciprocal(ry[:, 0:cols], rt[:, 0:cols]).then_inc(steps_d, 1)
                dve.wait_ge(steps_d, d0 + 2)
                dve.tensor_tensor(ra[:, 0:cols], ry[:, 0:cols], ry[:, 0:cols], ALU.mult).then_inc(steps_d, 1)
                dve.wait_ge(steps_d, d0 + 3)
                dve.scalar_tensor_tensor(out=rb2[:, 0:cols], in0=ra[:, 0:cols], scalar=-0.5, in1=rv[:, 0:cols],
                                         op0=ALU.mult, op1=ALU.mult).then_inc(steps_d, 1)
                dve.wait_ge(steps_d, d0 + 4)
                wide = [P, cols, L // cols]
                dve.scalar_tensor_tensor(out=rbs[:].rearrange("p (a b) -> p a b", a=cols),
                                         in0=rb2[:, 0:cols].unsqueeze(2).to_broadcast(wide), scalar=1.5,
                                         in1=ry[:, 0:cols].unsqueeze(2).to_broadcast(wide),
                                         op0=ALU.add, op1=ALU.mult).then_inc(last, 1)

            def modulate(n):
                l, scale = n // 2, 3 * n + 1
                gain = vec[:, l, V_GMIX:V_GFFN] if n % 2 == 0 else vec[:, l, V_GFFN:V_ROWS]
                dve.wait_ge(ada_done, scale + 1)
                dve.scalar_tensor_tensor(out=mulA[:, n, :], in0=mod[:, scale, :], scalar=1.0, in1=gain,
                                         op0=ALU.add, op1=ALU.mult).then_inc(mul_ready, 1)
                mean_square(ms_ready, n + 1, nD, TT, float(D))
                newton(nD, nA, 5 * n, n, TT, nD)
                dve.wait_ge(rms_ready, n + 1)
                for k in range(FT + 1):
                    if k < FT:
                        if k >= 2:
                            dve.wait_ge(hf_ready, FT * n + k - 1)
                        dve.tensor_tensor(nt[:, k % 2, :], xT[:, k, :], RB[:], ALU.mult).then_inc(t_ready, 1)
                    if k >= 1:
                        dve.wait_ge(hf_ready, FT * n + k)
                        dve.tensor_tensor(hl[:, k - 1, :], nt[:, 2 + (k - 1) % 2, :], hh[:, k - 1, :].bitcast(F32),
                                          ALU.subtract).then_inc(h_ready, 1)

            def residual(n, last_unit):
                gate = 6 * (n // 2) + (2 if n % 2 == 0 else 5)
                dve.wait_ge(ada_done, gate + 1)
                for m in range(FT):
                    if m < FT - 1:
                        dve.wait_ge(y_ready[n], m + 1)
                    else:
                        dve.wait_ge(unit_used, last_unit)
                    dve.scalar_tensor_tensor(out=xT[:, m, :], in0=bank[m][:], scalar=mod[:, gate, m:m + 1], in1=xT[:, m, :],
                                             op0=ALU.mult, op1=ALU.add).then_inc(x_done[n + 1], 1)
                    if n < 3 and m >= 2:
                        add_squares(n + 1, m - 1)
                if n < 3:
                    add_squares(n + 1, FT - 1)

            def ada_slice(q, k, start=False):
                if start:
                    src = v0[:, k % 4, :]
                    dve.wait_ge(ada_in[k % 4], 16 * (2 * q + k // 4 + 1))
                else:
                    src = ada_raw[:, k % 2, :]
                    dve.wait_ge(ada_in[k % 2], 16 * (4 * q + k // 2 - 3))
                if k == 0:
                    dve.tensor_scalar(ada_acc[:], src, csil[:, 0:1], None, ALU.mult).then_inc(ada_used, 1)
                else:
                    dve.wait_ge(ada_used, 8 * q + k)
                    dve.scalar_tensor_tensor(out=ada_acc[:], in0=src, scalar=csil[:, k:k + 1], in1=ada_acc[:],
                                             op0=ALU.mult, op1=ALU.add).then_inc(ada_used, 1)

            def ada_out(l, q, part):
                dve.wait_ge(ada_sum, q + 1)
                bias = vec[:, 2, V_BADA + 48 * l:V_BADA + 48 * l + 48].rearrange("p (q m) -> p q m", q=6)[:, ds(part, 1), :]
                dve.tensor_tensor(mod[:, ds(q, 1), :], ADA[:, 0:FT].rearrange("p (a m) -> p a m", a=1), bias, ALU.add).then_inc(ada_done, 1)

            def finish_tile(l, te, t, dst):
                dve.wait_ge(hrb_ready[l], te + 1)
                return dve.tensor_tensor(dst, qg[:, t % 2:t % 2 + 1, :], RB[:].rearrange("p (a n) -> p a n", a=1), ALU.mult).then_inc(normed[l], 1)

            def head_stats(l, te):
                mean_square(hms_ready[l], te + 1, hD[l], 8, float(HD))

            def head_newton(l, te):
                newton(hD[l], hA[l], 4 * te, te, 8, hrs_ready[l])

            def bias_rows(l):
                b = bias_step[l]
                dve.tensor_copy(cumh[:], cum[:]).then_inc(b, 1)
                dve.wait_ge(b, 1)
                dve.tensor_tensor(scr[:, 0, :], cum[:], cumh[:].bitcast(F32), ALU.subtract).then_inc(b, 1)
                dve.wait_ge(b, 2)
                dve.tensor_scalar(scr[:, 1, :], scr[:, 0, :], cst[:, C_ODD:C_ODD + 1], None, ALU.mult).then_inc(b, 1)
                dve.wait_ge(b, 3)
                dve.scalar_tensor_tensor(out=scr[:, 0, :], in0=cumh[:].bitcast(F32), scalar=cst[:, C_EVEN:C_EVEN + 1],
                                         in1=scr[:, 1, :], op0=ALU.mult, op1=ALU.add).then_inc(b, 1)
                dve.wait_ge(b, 4)
                for r in (0, 64):
                    dve.tensor_copy(biasq[r:r + 32, :], scr[r:r + 32, 0, :])
                    dve.tensor_scalar(biasq[r + 32:r + 64, :], cst[r + 32:r + 64, C_ONE:C_ONE + 1].to_broadcast([32, L]), 1.0, None, ALU.mult)
                    dve.memset(biask[r:r + 32, :], 1.0)
                    op = dve.tensor_scalar(biask[r + 32:r + 64, :], scr[r + 32:r + 64, 0, :], -1.0, None, ALU.mult)
                op.then_inc(b, 1)
                dve.wait_ge(b, 5)

            def attention(l):
                def bias_head(i, h):
                    dve.tensor_scalar(half(biaskh, h)[:, h % 2, :], half(biask, h), half(cst, h)[:, ds(C_HEAD + 4 * (i - 4 * l) + h, 1)], None,
                                      ALU.mult).then_inc(kb_ready, 1)

                def row_max(i, s):
                    n = (s % TT + 1) * P
                    dve.wait_ge(s_ready, 16 * i + s + 1)
                    dve.tensor_reduce(nmax[:, s:s + 1], bank[s % 4][:, 0:n], AX_X, ALU.max, negate=True).then_inc(max_done, 1)

                def turned(i, s):
                    n = (s % TT + 1) * P
                    dve.wait_ge(pt_ready, 16 * i + s + 1)
                    dve.tensor_copy(probsT[:, s % 4, 0:n], turned_bank(s)[:, 0:n]).then_inc(ptd_done, 1)

                def head_out(i, h):
                    dve.wait_ge(pv_done, 16 * i + 4 * h + 4)
                    dve.reciprocal(rrec[:, 4 * h:4 * h + 4], rowsum[:, 4 * h:4 * h + 4]).then_inc(rec_done, 1)
                    dve.wait_ge(rec_done, 4 * i + h + 1)
                    dve.tensor_tensor(oP[:, h // 2, :, HD * (h % 2):HD * (h % 2) + HD],
                                      bank[6 + h % 2][:, 0:4 * HD].rearrange("p (t d) -> p t d", t=TT),
                                      rrec[:, 4 * h:4 * h + 4].unsqueeze(2).to_broadcast([P, TT, HD]), ALU.mult).then_inc(o_done, 1)

                def out_low(i, p):
                    dve.wait_ge(oh_done, 2 * i + p + 1)
                    dve.tensor_tensor(hl[:, ds(2 * (i - 4 * l) + p, 1), :], pair_bank(p)[:].rearrange("p (a n) -> p a n", a=1),
                                      hh[:, ds(2 * (i - 4 * l) + p, 1), :].bitcast(F32), ALU.subtract).then_inc(ol_done, 1)

                def round_(i, first, last):
                    for s in range(16):
                        if s % 2 == 0:
                            turned(i, s)
                        if s == 4 and not first:
                            out_low(i - 1, 1)
                        if s == 12:
                            out_low(i, 0)
                        if s < 13:
                            row_max(i, s + 3)
                        elif not last:
                            row_max(i + 1, s - 13)
                        if s == 1 and not first:
                            head_out(i - 1, 3)
                        if s in (5, 9, 13):
                            head_out(i, (s - 5) // 4)
                        if s in (2, 6):
                            bias_head(i, 2 + s // 4)
                        if s == 10 and not last:
                            bias_head(i + 1, 0)
                        if s == 13 and not last:
                            bias_head(i + 1, 1)

                i = 4 * l
                bias_head(i, 0)
                bias_head(i, 1)
                for s in range(3):
                    row_max(i, s)
                round_(i, True, False)
                with dve.Fori(4 * l + 1, 4 * l + 3) as i:
                    round_(i, False, False)
                i = 4 * l + 3
                round_(i, False, True)
                head_out(i, 3)
                out_low(i, 1)

            def mlp_layer(l, up, last_unit):
                n = 2 * l + 1
                modulate(n)
                col = vec[:, l, :]

                def up_body(i, slices=lambda: None):
                    for c_ in range(2):
                        tau = 2 * i + c_
                        dve.wait_ge(tap2[l], tau + 1)
                        dve.scalar_tensor_tensor(out=cv[:, c_, 1:L], in0=bank[c_][:, 0:L - 1], scalar=col[:, ds(V_CONVW + UT + tau, 1)],
                                                 in1=cv[:, c_, 1:L], op0=ALU.mult, op1=ALU.add).then_inc(tap1[l], 1)
                        dve.wait_ge(tap1[l], tau + 1)
                        dve.scalar_tensor_tensor(out=cv[:, c_, 2:L], in0=bank[c_][:, 0:L - 2], scalar=col[:, ds(V_CONVW + tau, 1)],
                                                 in1=cv[:, c_, 2:L], op0=ALU.mult, op1=ALU.add).then_inc(conv_done[l], 1)
                    slices()
                    for c_ in range(2):
                        tau = 2 * i + c_
                        dve.wait_ge(silu_done[l], tau + 1)
                        if c_ == 0:
                            dve.wait_ge(g_ready[l], i + 1)
                        else:
                            dve.wait_ge(unit_used, 2 * (up + 2 * i + 1) + 2)
                        dve.tensor_tensor(cv[:, c_, :], cv[:, c_, :], bank[2 + c_][:], ALU.mult).then_inc(uf_done[l], 1)
                        dve.wait_ge(uh_done[l], tau + 1)
                        dve.tensor_tensor(ul[:, ds(tau, 1), :], cv[:, c_:c_ + 1, :], uh[:, ds(tau, 1), :].bitcast(F32),
                                          ALU.subtract).then_inc(u_done[l], 1)

                if l == 0:
                    with dve.Fori(0, 5) as j:
                        for e in range(2):
                            up_body(2 * j + e, lambda: [ada_slice(7 + j, k) for k in range(4 * e, 4 * e + 4)])
                        ada_out(1, 7 + j, 1 + j)
                    up_body(10)
                else:
                    with dve.Fori(0, 11) as i:
                        up_body(i)
                residual(n, last_unit)

            dve.wait_ge(cst_in, 16)
            dve.tensor_copy(ident_r[:], ident)
            dve.tensor_copy(causal_r[:], cst[:, C_CAUSAL:C_CAUSAL + P]).then_inc(cst_done, 1)
            dve.wait_ge(vecT_ready, 1)
            dve.tensor_copy(vec[:, 2, 0:V_ROWS], MISC[:, 2 * P:2 * P + V_ROWS]).then_inc(vec_done, 1)
            dve.wait_ge(csil_done, 1)
            for k in range(FT):
                ada_slice(0, k, start=True)
            ada_out(0, 0, 0)
            for m in range(1, FT):
                add_squares(0, m)
            dve.wait_ge(vecT_ready, 2)
            for j, rows in ((0, V_ROWS), (1, V_ROWS), (3, G_ROWS)):
                dve.tensor_copy(vec[:, j, 0:rows], MISC[:, j * P:j * P + rows]).then_inc(vec_done, 1)
            dve.wait_ge(vec_done, 4)

            def gain_cols(at, n, row, scale):
                return dve.tensor_scalar(gains[:, at:at + n], vec[:, 3, row:row + 1].to_broadcast([P, n]), scale, None, ALU.mult)
            gain_cols(GAIN[0], 8, G_FOXQ, HD ** -0.5)
            gain_cols(GAIN[0] + 8, 8, G_FOXK, 1.0)
            gain_cols(GAIN[1], 1, G_KIDX, 1.0)
            gain_cols(GAIN[1] + 1, 2, G_DSAK, 1.0)
            gain_cols(GAIN[1] + 3, 8, G_DSAQ, HD ** -0.5).then_inc(cst_done, 1)
            for k in range(FT):
                ada_slice(1, k, start=True)
            ada_out(0, 1, 1)
            dve.wait_ge(sm_in[0], 16)
            for r in range(8):
                dve.tensor_copy(smh0[:, :, r * NH:(r + 1) * NH], smr0[:]).then_inc(sm_hi[0], 1)
            dve.wait_ge(sm_hi[0], 8)
            for r in range(8):
                dve.tensor_tensor(sml0[:, :, r * NH:(r + 1) * NH], smr0[:], smh0[:, :, r * NH:(r + 1) * NH].bitcast(F32),
                                  ALU.subtract).then_inc(sm_ready[0], 1)

            modulate(0)
            def forget_gates():
                dve.wait_ge(f_act, 4)
                dve.tensor_scalar(scr[:, 0, :], scr[:, 0, :], 0.0, None, ALU.min).then_inc(f_dve, 1)
                dve.wait_ge(f_dve, 1)
                dve.tensor_tensor(scr[:, 1, :], scr[:, 0, :], scr[:, 3, :], ALU.subtract).then_inc(f_dve, 1)
                dve.memset(scr[:, 2, :], 1.0).then_inc(f_dve, 1)
                dve.wait_ge(f_dve, 3)
                dve.tensor_tensor_scan(cum[:], scr[:, 2, :], scr[:, 1, :], 0.0, ALU.mult, ALU.add).then_inc(f_dve, 1)
                dve.wait_ge(f_dve, 4)
                bias_rows(0)

            def fox_body(i, first):
                for c_ in range(4):
                    tau = 4 * i + c_
                    if not (first and c_ == 0):
                        head_stats(0, tau - 1)
                    if not (first and c_ < 2):
                        finish_tile(0, tau - 2, c_, qk[:, ds(tau - 2, 1), :])
                    if not (first and c_ == 0):
                        head_newton(0, tau - 1)
                    if not first:
                        ada_slice(1 + i, 2 * c_)
                        ada_slice(1 + i, 2 * c_ + 1)
                if not first:
                    ada_out(0, 1 + i, 1 + i)

            fox_body(0, True)
            with dve.Fori(1, 4) as i:
                fox_body(i, False)
            head_stats(0, 15)
            finish_tile(0, 14, 14, qk[:, 14:15, :])
            head_newton(0, 15)
            for i in range(2):
                for k in range(FT):
                    ada_slice(5 + i, k)
                    if (i, k) == (0, 3):
                        finish_tile(0, 15, 15, qk[:, 15:16, :])
                ada_out(i, 5 + i, 5 * (1 - i))
                if i == 0:
                    forget_gates()
            attention(0)
            residual(0, 2 * (FOX_OUT + 3) + 2)
            mlp_layer(0, FOX_UP, 2 * (FOX_DOWN + 10) + 2)

            modulate(2)
            dve.wait_ge(sm_in[1], 16)
            dve.tensor_copy(smh1[:], smr1[:]).then_inc(sm_hi[1], 1)
            dve.wait_ge(sm_hi[1], 1)
            dve.tensor_tensor(sml1[:], smr1[:], smh1[:].bitcast(F32), ALU.subtract).then_inc(sm_ready[1], 1)
            dve.wait_ge(alibi_in, 16)
            bias_rows(1)
            dve.wait_ge(w_ready, 1)
            dve.tensor_scalar(widx[:], MISC[:, 0:TT * IH], IH ** -0.5 * HD ** -0.5, None, ALU.mult).then_inc(w_taken, 1)
            dve.wait_ge(w_taken, 1)
            head_stats(1, 0)
            head_newton(1, 0)
            dve.wait_ge(hrb_ready[1], 1)
            for e in range(2):
                op = dve.tensor_tensor(kidx[e * HD:(e + 1) * HD, :], qg[0:HD, 0, :], RB[0:HD, :], ALU.mult)
            op.then_inc(normed[1], 1)
            for e in range(3 * IH):
                h, t = e // 3, 1 + e % 3
                n = (t + 1) * P
                w_col = widx[:, IH * t + h:IH * t + h + 1]
                dve.wait_ge(relu_done, e + 1)
                if h == 0:
                    dve.tensor_scalar(score[:, t - 1, 0:n], scr[:, e % 2, 0:n], w_col, 0.0, ALU.mult, ALU.add).then_inc(weighed, 1)
                else:
                    dve.wait_ge(weighed, e - 2)
                    dve.scalar_tensor_tensor(out=score[:, t - 1, 0:n], in0=scr[:, e % 2, 0:n], scalar=w_col,
                                             in1=score[:, t - 1, 0:n], op0=ALU.mult, op1=ALU.add).then_inc(weighed, 1)
            dve.wait_ge(weighed, 3 * IH)
            for t in range(1, TT):
                dve.tensor_tensor(score[:, t - 1, t * P:(t + 1) * P], score[:, t - 1, t * P:(t + 1) * P],
                                  cst[:, C_CAUSAL:C_CAUSAL + P], ALU.add).then_inc(tk, 1)

            def top_round(r):
                for t in range(3):
                    n = (t + 2) * P
                    dve.wait_ge(tk, 6 * r + 1 + t)
                    dve.max(top8[:, t, :], score[:, t, 0:n]).then_inc(tk, 1)
                for t in range(3):
                    n = (t + 2) * P
                    dve.wait_ge(tk, 6 * r + 4 + t)
                    dve.match_replace(score[:, t, 0:n], top8[:, t, :], score[:, t, 0:n], TAKEN).then_inc(tk, 1)

            for r in range(3):
                top_round(r)
            head_stats(1, 1)
            head_newton(1, 1)

            def key_heads(te, p):
                dve.wait_ge(hrb_ready[1], te + 1)
                for g in range(2):
                    src = slice(g * HD, (g + 1) * HD)
                    for e in range(2):
                        op = dve.tensor_tensor(qk[e * HD:(e + 1) * HD, 8 + 2 * p + g, :], qg[src, te % 2, :], RB[src, :], ALU.mult)
                op.then_inc(normed[1], 1)

            def dsa_slot(i, c_, first):
                tau = 4 * i + c_ + 3
                head_stats(1, tau - 1)
                if first and c_ < 2:
                    key_heads(tau - 2, tau - 3)
                else:
                    finish_tile(1, tau - 2, c_ + 1, qk[:, ds(tau - 5, 1), :])
                head_newton(1, tau - 1)
                for r in ((3,), (4, 5), (6,), (7, 8))[c_]:
                    top_round(6 * i + r)

            for c_ in range(4):
                dsa_slot(0, c_, True)
            with dve.Fori(1, 2) as i:
                for c_ in range(4):
                    dsa_slot(i, c_, False)
            head_stats(1, 10)
            finish_tile(1, 9, 9, qk[:, 6:7, :])
            head_newton(1, 10)
            finish_tile(1, 10, 10, qk[:, 7:8, :])
            top_round(15)
            dve.tensor_copy(masked[:, 0, 0:P], cst[:, C_CAUSAL:C_CAUSAL + P]).then_inc(mask_ready, 1)
            dve.wait_ge(tk, 3 + 6 * (TOPK // 8))
            for t in range(1, TT):
                n = (t + 1) * P
                dve.tensor_scalar(masked[:, t, 0:n], score[:, t - 1, 0:n], TAKEN, MASKED, ALU.not_equal, ALU.mult).then_inc(mask_ready, 1)
            attention(1)
            residual(2, 2 * (DSA_OUT + 3) + 2)
            mlp_layer(1, DSA_UP, 2 * (DSA_DOWN + 10) + 2)

            for m in range(FT):
                dve.wait_ge(oT_ready, m + 1)
                dve.tensor_copy(outs[:, :, m * P:(m + 1) * P], bank[m % 4][:].rearrange("p (t d) -> p t d", t=TT)).then_inc(oT_done, 1)


_INS = ["x", "c", "w_ada", "b_ada", "g_norm_mix", "g_norm_ffn", "fox_w_in", "fox_b_f", "fox_g_q", "fox_g_k",
        "fox_w_out", "dsa_w_in", "dsa_g_q", "dsa_g_k", "dsa_g_kidx", "dsa_w_out", "ffn_w_up", "ffn_conv_w",
        "ffn_conv_b", "ffn_w_down"]


def shape_constants():
    import numpy as np
    t = np.zeros((P, C_N), np.float32)
    p = np.arange(P)
    t[:, C_ID:C_ID + P] = np.eye(P)
    t[:, C_CAUSAL:C_CAUSAL + P] = np.where(p[None, :] > p[:, None], MASKED, 0.0)
    t[:, C_BLOCK] = p < HD
    t[:, C_BLOCK + 1] = p >= HD
    t[:, C_EVEN] = p % 32 < NH
    t[:, C_ODD] = p % 32 >= NH
    t[:, C_HEAD:C_HEAD + NH] = p[:, None] % NH == np.arange(NH)[None, :]
    t[:, C_ONE] = 1.0
    t[:, C_EPS] = EPS
    slopes = np.exp2(-8.0 * np.arange(1, NH + 1, dtype=np.float32) / np.float32(NH)).astype(np.float32)
    alibi = -slopes[p % NH][:, None] * np.arange(L, dtype=np.float32)[None, :]
    return t, alibi.astype(np.float32)


def kernel(**inputs):
    import numpy as _np
    import concourse.bacc as _bacc
    from concourse import mybir as _mybir
    from concourse.bass_utils import run_bass_kernel_spmd as _run

    nc = _bacc.Bacc("TRN2", target_bir_lowering=False, num_devices=1, dynamic_dma_scratch_size=2048)
    arrays, args = {}, []
    for name, a in [(n, inputs[n]) for n in _INS] + list(zip(("consts", "alibi"), shape_constants())):
        a = _np.ascontiguousarray(a)
        arrays[f"in_{name}_dram"] = a
        args.append(nc.dram_tensor(f"in_{name}_dram", a.shape, _mybir.dt.from_np(a.dtype), kind="ExternalInput").ap())
    args.append(nc.dram_tensor("out_dram", (1, L, D), _mybir.dt.float32, kind="ExternalOutput").ap())
    two_layers(nc, *args)
    r = _run(nc, [arrays], core_ids=[0])
    return r.results[0]["out_dram"]
```

```python
from contextlib import ExitStack

import concourse.bass as bass
from concourse import mybir

F32 = mybir.dt.float32
F32R = mybir.dt.float32r
ALU = mybir.AluOpType
ACT = mybir.ActivationFunctionType
AX_X = mybir.AxisListType.X
ds = bass.ds

P = 128
D = 1024
L = 512
FT = D // P
TT = L // P
HD = 64
NH = D // HD
NKV = 4
IH = 8
TOPK = L // 4
FF = 2816
UT = FF // P
EPS = 1e-6
MASKED = -3.0e38
TAKEN = -3.4028235e38

C_ID, C_CAUSAL, C_BLOCK, C_EVEN, C_ODD, C_HEAD, C_ONE, C_EPS, C_N = 0, 128, 256, 258, 259, 260, 276, 277, 278

FOX_IN, FOX_OUT, FOX_UP, FOX_DOWN = 0, 12, 16, 38
DSA_IDX, DSA_K, DSA_Q, DSA_V, DSA_OUT, DSA_UP, DSA_DOWN = 49, 51, 52, 56, 57, 61, 83
LOADS = 94
UNIT = 1024

V_CONVW, V_CONVB, V_GMIX, V_GFFN, V_ROWS = 0, 66, 88, 96, 104
V_BADA, V_C = 0, 96
G_FOXQ, G_FOXK, G_DSAQ, G_DSAK, G_KIDX, G_BF, G_ROWS = 0, 1, 2, 3, 4, 5, 6
GAIN = [0, 16]


def two_layers(nc, x, c, w_ada, b_ada, g_norm_mix, g_norm_ffn, fox_w_in, fox_b_f, fox_g_q, fox_g_k,
               fox_w_out, dsa_w_in, dsa_g_q, dsa_g_k, dsa_g_kidx, dsa_w_out, ffn_w_up, ffn_conv_w,
               ffn_conv_b, ffn_w_down, consts, alibi, out):
    ctx = ExitStack()
    with ctx:
        def sem(name):
            return ctx.enter_context(nc.semaphore(name))

        def sems(name, n):
            return [sem(f"{name}{i}") for i in range(n)]

        def sb(name, shape, dt=F32, stack=ctx):
            return stack.enter_context(nc.sbuf_tensor(name, shape, dt))

        xT = sb("xT", [P, FT, L])
        hh = sb("hh", [P, FT, L], F32R)
        hl = sb("hl", [P, FT, L], F32R)
        raw = sb("raw", [P, 2, 2 * UNIT])
        wh = sb("wh", [P, 4, UNIT], F32R)
        wl = sb("wl", [P, 4, UNIT], F32R)
        ada_raw = sb("ada_raw", [P, 2, D])
        ada_acc = sb("ada_acc", [P, D])
        nt = sb("nt", [P, 4, L])
        rbs = sb("rbs", [P, L])
        cst = sb("cst", [P, C_N])
        ident_r = sb("ident_r", [P, P], F32R)
        causal_r = sb("causal_r", [P, P], F32R)
        vec = sb("vec", [P, 4, P])
        csil = sb("csil", [P, FT])
        mod = sb("mod", [P, 12, FT])
        mulA = sb("mulA", [P, 4, FT])
        gains = sb("gains", [P, 32])
        rv = sb("rv", [P, 8])
        rt = sb("rt", [P, 8])
        ry = sb("ry", [P, 8])
        ra = sb("ra", [P, 8])
        rb2 = sb("rb2", [P, 8])
        nmax = sb("nmax", [P, 16])
        rowsum = sb("rowsum", [P, 16])
        rrec = sb("rrec", [P, 16])
        widx = sb("widx", [P, TT * IH])
        top8 = sb("top8", [P, 3, 8])
        ident = cst[:, C_ID:C_ID + P]

        with ExitStack() as before_att:
            qidx = sb("qidx", [P, IH, L], F32R, stack=before_att)
        with ExitStack() as att:
            qk = sb("qk", [P, 16, L], stack=att)
            probsT = sb("probsT", [P, 4, L], stack=att)
            oP = sb("oP", [P, 2, TT, P], stack=att)
            biasq = sb("biasq", [P, L], F32R, stack=att)
            biask = sb("biask", [P, L], stack=att)
            cum = sb("cum", [P, L], stack=att)
            cumh = sb("cumh", [P, L], F32R, stack=att)
            with ExitStack() as proj:
                sqb = sb("sqb", [P, 2, L], stack=proj)
                qg = sb("qg", [P, 2, L], stack=proj)
                smr0 = sb("smr0", [P, FT, 16], stack=proj)
                smh0 = sb("smh0", [P, FT, P], F32R, stack=proj)
                sml0 = sb("sml0", [P, FT, P], F32R, stack=proj)
            with ExitStack() as proj:
                sb("sqb_qg", [P, 4, L], stack=proj)
                smr1 = sb("smr1", [P, FT, HD + IH], stack=proj)
                smh1 = sb("smh1", [P, FT, HD + IH], F32R, stack=proj)
                sml1 = sb("sml1", [P, FT, HD + IH], F32R, stack=proj)
                wT = sb("wT", [P, L], stack=proj)
            with ExitStack() as heads:
                qA = sb("qA", [P, 2, L], F32R, stack=heads)
                kA = sb("kA", [P, 2, L], F32R, stack=heads)
                qB = sb("qB", [P, 2, L], F32R, stack=heads)
                kB = sb("kB", [P, 2, L], F32R, stack=heads)
            sb("below_values", [P, 5 * 1024], stack=att)
            with ExitStack() as fox:
                v0 = sb("v0", [P, TT, D], stack=fox)
            with ExitStack() as dsa:
                v1 = sb("v1", [P, TT, NKV * HD], stack=dsa)
                score = sb("score", [P, 3, L], stack=dsa)
                masked = sb("masked", [P, TT, L], F32R, stack=dsa)
        probs = nt
        scr = probsT
        kfull = oP[:, 0, :, :].rearrange("p t d -> p (t d)")
        kidx, kidl = masked[:, 0, :], masked[:, 1, :]
        with ExitStack() as mlp:
            uh = sb("uh", [P, UT, L], F32R, stack=mlp)
            ul = sb("ul", [P, UT, L], F32R, stack=mlp)
            cv = sb("cv", [P, 2, L], stack=mlp)
        with ExitStack() as ends:
            xtok = sb("xtok", [P, TT, D], stack=ends)
            vrows = sb("vrows", [P, 4, P], stack=ends)
        with ExitStack() as ends2:
            outs = sb("outs", [P, TT, D], stack=ends2)

        bank = [ctx.enter_context(nc.psum_tensor(f"bank{i}", [P, 512], F32)) for i in range(8)]
        ST, RB, MISC, ADA = bank[4], bank[5], bank[6], bank[7]

        cst_in, c_in, vec_in, x_in, alibi_in, out_done = (sem(n) for n in ("cst_in", "c_in", "vec_in", "x_in", "alibi_in", "out_done"))
        raw_in = sems("raw_in", 2)
        w_hi = sem("w_hi")
        w_split = sem("w_split")
        unit_used = sem("unit_used")
        ada_in = sems("ada_in", 4)
        ada_used = sem("ada_used")
        ada_sum = sem("ada_sum")
        ada_done = sem("ada_done")
        vecT_ready, vec_done, csil_done = sem("vecT_ready"), sem("vec_done"), sem("csil_done")
        cst_done, xT_ready = sem("cst_done"), sem("xT_ready")
        x_done = sems("x_done", 5)
        sq_ready = sem("sq_ready")
        sq_added = sem("sq_added")
        ms_ready = sem("ms_ready")
        nD = sem("nD")
        nA = sem("nA")
        rms_ready = sem("rms_ready")
        t_ready, hh_ready, hf_ready, h_ready = sem("t_ready"), sem("hh_ready"), sem("hf_ready"), sem("h_ready")
        mul_ready = sem("mul_ready")
        sm_in, sm_hi, sm_ready = sems("sm_in", 2), sems("sm_hi", 2), sems("sm_ready", 2)
        tile_ready = sems("tile_ready", 2)
        kidx_ready = sem("kidx_ready")
        taken = sems("taken", 2)
        hsq_ready = sems("hsq_ready", 2)
        hms_ready = sems("hms_ready", 2)
        hD, hA = sems("hD", 2), sems("hA", 2)
        hrs_ready = sems("hrs_ready", 2)
        hrb_ready = sems("hrb_ready", 2)
        normed = sems("normed", 2)
        v_ready = sems("v_ready", 2)
        f_ready, f_act, f_dve = sem("f_ready"), sem("f_act"), sem("f_dve")
        bias_step = sems("bias_step", 2)
        bias_ready = sems("bias_ready", 2)
        wT_ready, w_ready, w_taken = sem("wT_ready"), sem("w_ready"), sem("w_taken")
        idx_high, key_step, is_ready, relu_done, weighed, tk, mask_ready = (sem(n) for n in ("idx_high", "key_step", "is_ready", "relu_done", "weighed", "tk", "mask_ready"))
        s_high, s_low, s_rest = sem("s_high"), sem("s_low"), sem("s_rest")
        s_ready, max_done, p_ready = sem("s_ready"), sem("max_done"), sem("p_ready")
        pt_ready, ptd_done, pta_done = sem("pt_ready"), sem("ptd_done"), sem("pta_done")
        pv_done, rec_done, o_done = sem("pv_done"), sem("rec_done"), sem("o_done")
        ot_ready, oh_done, ol_done = sem("ot_ready"), sem("oh_done"), sem("ol_done")
        y_ready = sems("y_ready", 4)
        a_ready, g_ready = sems("a_ready", 2), sems("g_ready", 2)
        tap2, tap1, conv_done, silu_done = sems("tap2_", 2), sems("tap1_", 2), sems("conv_done", 2), sems("silu_done", 2)
        uf_done, uh_done, u_done = sems("uf_done", 2), sems("uh_done", 2), sems("u_done", 2)
        oT_ready, oT_done = sem("oT_ready"), sem("oT_done")
        waits_passed = sem("waits_passed")

        block = ctx.enter_context(nc.Block())

        def wait_alone(eng, semaphore, count):
            eng.wait_ge(semaphore, count)
            eng.sem_inc(waits_passed, 1)

        def half(tensor, h):
            return tensor[64 * (h % 2):64 * (h % 2) + 64]

        def other(tensor, h):
            return half(tensor, h + 1)

        def head_tiles(l, g, h):
            return half(qk, h)[:, ds(2 * g + h // 2, 1), :], half(qk, h)[:, ds(8 + (2 * g + h // 2 if l == 0 else g), 1), :]

        def part(tensor, h):
            return tensor[:, h % 2:h % 2 + 1, :]

        def conv_banks(e):
            return (bank[4], bank[5]) if e else (bank[0], bank[1])

        def ada_slot(k, start):
            if start:
                return v0[:, k % 4, :]
            return ada_raw[:, k % 4, :] if k % 4 < 2 else nt[:, 2 * (k % 4) - 4:2 * (k % 4) - 2, :].rearrange("p a n -> p (a n)")

        def turned_bank(s):
            return bank[4 + (s + (s >= 4) + (s >= 12)) % 2]

        def pair_bank(p):
            return bank[5 - p]

        @block.sync
        def _(sp):
            def load(n, slot, src, first=False):
                if not first:
                    sp.wait_ge(w_split, 2 * n - 2)
                dst = raw[:, slot, :]
                sp.dma_start(dst.rearrange("p (k c) -> p k c", k=src.shape[1]), src).then_inc(raw_in[slot], 16)

            def load_cols(n, slot, w, col, first=False):
                load(n, slot, w.rearrange("(k p) c -> p k c", p=P)[:, :, ds(col, 256)], first)

            def load_rows(n, slot, w, k):
                load(n, slot, w.rearrange("(k p) c -> p k c", p=P)[:, ds(k, 2), :])

            def ada_slices(layer, q, part, ks=range(FT), start=False, nt_free=0):
                for k in ks:
                    if k % 4 == 2 and nt_free:
                        sp.wait_ge(h_ready, nt_free)
                    if not (start and 8 * q + k < 4):
                        sp.wait_ge(ada_used, 8 * q + k - 3)
                    sp.dma_start(ada_slot(k, start), w_ada[layer, k * P:(k + 1) * P, ds(part * D, D)]).then_inc(ada_in[k % 4], 16)

            sp.dma_start(cst[:], consts).then_inc(cst_in, 16)
            sp.dma_start(vrows[V_BADA:V_C, 2, :], b_ada.rearrange("l (m p) -> (l m) p", p=P)).then_inc(c_in, 16)
            sp.dma_start(vrows[V_C:V_ROWS, 2, :], c.rearrange("a (m p) -> (a m) p", p=P)).then_inc(c_in, 16)
            for t in range(TT):
                sp.dma_start(xtok[:, t, :], x[0, t * P:(t + 1) * P, :]).then_inc(x_in, 16)
            ada_slices(0, 0, 0, start=True)
            load_cols(0, 0, fox_w_in[0], 0, first=True)
            for l in range(2):
                sp.dma_start(vrows[V_CONVW:V_CONVB, l, :], ffn_conv_w[l].rearrange("w (m p) -> (w m) p", p=P)).then_inc(vec_in, 16)
                sp.dma_start(vrows[V_CONVB:V_GMIX, l, :], ffn_conv_b[l].rearrange("(m p) -> m p", p=P)).then_inc(vec_in, 16)
                sp.dma_start(vrows[V_GMIX:V_GFFN, l, :], g_norm_mix[l].rearrange("(m p) -> m p", p=P)).then_inc(vec_in, 16)
                sp.dma_start(vrows[V_GFFN:V_ROWS, l, :], g_norm_ffn[l].rearrange("(m p) -> m p", p=P)).then_inc(vec_in, 16)
            for row, g, n in ((G_FOXQ, fox_g_q, 2), (G_FOXK, fox_g_k, 2), (G_DSAQ, dsa_g_q, 2), (G_DSAK, dsa_g_k, 2),
                              (G_KIDX, dsa_g_kidx, 2), (G_BF, fox_b_f, 8)):
                sp.dma_start(vrows[row:row + 1, 3, :].rearrange("a (e d) -> a e d", e=n),
                             g.unsqueeze(1).to_broadcast([1, n, P // n])).then_inc(vec_in, 16)
            sp.dma_start(smr0[:], fox_w_in[0].rearrange("(k p) c -> p k c", p=P)[:, :, 3 * D:3 * D + NH]).then_inc(sm_in[0], 16)
            ada_slices(0, 1, 1, start=True)
            load_cols(1, 1, fox_w_in[0], 256, first=True)
            for s in range(2):
                load_cols(2 + s, s, fox_w_in[0], 512 + 256 * s)
            ada_slices(0, 2, 2, range(4), nt_free=FT)
            load_cols(4, 0, fox_w_in[0], 1024)
            ada_slices(0, 2, 2, range(4, 8))
            load_cols(5, 1, fox_w_in[0], 1280)
            with sp.Fori(2, 4) as i:
                for s in range(2):
                    load_cols(2 * i + 2 + s, s, fox_w_in[0], 512 * i + 512 + 256 * s)
                    ada_slices(0, 1 + i, 1 + i, range(4 * s, 4 * s + 4))
            for i in range(2):
                for s in range(2):
                    if i == 0:
                        load_cols(10 + s, s, fox_w_in[0], 2560 + 256 * s)
                    else:
                        load_rows(FOX_OUT + s, s, fox_w_out[0], 2 * s)
                    ada_slices(i, 5 + i, 5 * (1 - i), range(4 * s, 4 * s + 4))
            for j in (2, 3):
                load_rows(FOX_OUT + j, j % 2, fox_w_out[0], 2 * j)

            def mlp_loads(l, up, down):
                def columns(i, between=lambda e: None):
                    load_cols(up + 2 * i, up % 2, ffn_w_up[l], 256 * i)
                    between(0)
                    load_cols(up + 2 * i + 1, (up + 1) % 2, ffn_w_up[l], FF + 256 * i)
                    between(2)
                if l == 0:
                    columns(0)
                    with sp.Fori(0, 5) as j:
                        for e in range(2):
                            columns(2 * j + e + 1, lambda k: ada_slices(1, 7 + j, 1 + j, range(4 * e + k, 4 * e + k + 2), nt_free=2 * FT))
                else:
                    with sp.Fori(0, 11) as i:
                        columns(i)
                load_rows(down, down % 2, ffn_w_down[l], 0)
                with sp.Fori(0, 5) as i:
                    for s in range(2):
                        load_rows(down + 1 + 2 * i + s, (down + 1 + s) % 2, ffn_w_down[l], 2 + 4 * i + 2 * s)

            mlp_loads(0, FOX_UP, FOX_DOWN)
            for j in range(2):
                load_cols(DSA_IDX + j, (DSA_IDX + j) % 2, dsa_w_in[0], 1536 + 256 * j)
            sp.wait_ge(x_done[2], FT)
            sp.dma_start(smr1[:], dsa_w_in[0].rearrange("(k p) c -> p k c", p=P)[:, :, 2048:2120]).then_inc(sm_in[1], 16)
            sp.dma_start(cum[:], alibi).then_inc(alibi_in, 16)
            load_cols(DSA_K, DSA_K % 2, dsa_w_in[0], 1024)
            for j in range(4):
                load_cols(DSA_Q + j, (DSA_Q + j) % 2, dsa_w_in[0], 256 * j)
            load_cols(DSA_V, DSA_V % 2, dsa_w_in[0], 1280)
            for j in range(4):
                load_rows(DSA_OUT + j, (DSA_OUT + j) % 2, dsa_w_out[0], 2 * j)
            mlp_loads(1, DSA_UP, DSA_DOWN)
            for e in range(2):
                sp.wait_ge(oT_done, 4 * e + 4)
                sp.dma_start(out[0].rearrange("(t p) d -> p t d", p=P)[:, :, 512 * e:512 * e + 512],
                             outs[:, :, 512 * e:512 * e + 512]).then_inc(out_done, 16)
            sp.wait_ge(out_done, 32)

        @block.gpsimd
        def _(pool):
            def split(i, s, u, first):
                n = 2 * s + u
                src = raw[:, s, u * UNIT:(u + 1) * UNIT]
                if not first:
                    wait_alone(pool, unit_used, 4 * i + n - 3)
                pool.tensor_scalar(wh[:, n, :], src, 1.0, 1.0, ALU.mult, ALU.mult).then_inc(w_hi, 1)
                pool.wait_ge(w_hi, 4 * i + n + 1)
                pool.tensor_tensor(wl[:, n, :], src, wh[:, n, :].bitcast(F32), ALU.subtract).then_inc(w_split, 1)

            def split_loads(first, end):
                with pool.Fori(first // 2, end // 2) as i:
                    for s in range(2):
                        pool.wait_ge(raw_in[s], 16 * i + 16)
                        for u in range(2):
                            split(i, s, u, False)

            def split_heads(l):
                with pool.Fori(4 * l, 4 * l + 4) as i:
                    for h in range(4):
                        k = head_tiles(l, i - 4 * l, h)[1]
                        n = 12 * i + 3 * h
                        wait_alone(pool, s_high, 8 * i + 2 * h + 1)
                        wait_alone(pool, s_low, n + 1)
                        pool.tensor_scalar(half(qB, h)[:, h % 2, :], half(qA, h)[:, h % 2, :].bitcast(F32), 1.0, 1.0, ALU.mult, ALU.mult).then_inc(s_low, 1)
                        wait_alone(pool, s_high, 8 * i + 2 * h + 2)
                        wait_alone(pool, s_low, n + 2)
                        pool.tensor_scalar(other(kA, h)[:, h % 2, :], half(kA, h)[:, h % 2, :].bitcast(F32), 1.0, 1.0, ALU.mult, ALU.mult).then_inc(s_low, 1)
                        wait_alone(pool, s_low, n + 3)
                        pool.tensor_tensor(part(half(kB, h), h), k, part(half(kA, h), h).bitcast(F32), ALU.subtract).then_inc(s_low, 1)
                pool.wait_ge(s_low, 48 * (l + 1) + 1)

            pool.sem_inc(s_low, 1)
            for s in range(2):
                pool.wait_ge(raw_in[s], 16)
                for u in range(2):
                    split(0, s, u, True)
            split_loads(2, FOX_OUT + 2)
            split_heads(0)
            split_loads(FOX_OUT + 2, DSA_OUT + 1)
            split_heads(1)
            split_loads(DSA_OUT + 1, LOADS)

        @block.tensor
        def _(pe):
            def mm3(dst, wa, wb, xa, xb, start, stop):
                pe.matmul(dst, wa, xa, start=start, stop=False)
                pe.matmul(dst, wa, xb, start=False, stop=False)
                return pe.matmul(dst, wb, xa, start=False, stop=stop)

            def unit_cols(load, u):
                n = (2 * load + u) % 4
                return (wh[:, n, :].rearrange("p (k c) -> p k c", k=4), wl[:, n, :].rearrange("p (k c) -> p k c", k=4))

            def first_loads(n, load, dsts, readies, more=lambda k: None):
                for k in range(FT):
                    u = k // 4
                    tiles = [(e, c) for e in range(2) for c in range(2)]
                    wa, wb = {}, {}
                    for e, c in tiles:
                        a, b = unit_cols(load + e, u)
                        wa[e, c], wb[e, c] = a[:, k % 4, c * P:(c + 1) * P], b[:, k % 4, c * P:(c + 1) * P]
                    pe.wait_ge(hh_ready, FT * n + k + 1)
                    for e, c in tiles:
                        if k % 4 == 0 and c == 0:
                            pe.wait_ge(w_split, 2 * (load + e) + u + 1)
                        mm = pe.matmul(dsts[2 * e + c], wa[e, c], hh[:, k, :], start=(k == 0), stop=False)
                    pe.wait_ge(h_ready, FT * n + k + 1)
                    more(k)
                    for e, c in tiles:
                        mm = pe.matmul(dsts[2 * e + c], wb[e, c], hh[:, k, :], start=False, stop=False)
                        if (k, e, c) == (FT - 1, 1, 0):
                            mm.then_inc(unit_used, 1)
                        mm = pe.matmul(dsts[2 * e + c], wa[e, c], hl[:, k, :], start=False, stop=(k == FT - 1))
                        if (k, e, c) == (3, 0, 1) or (k == FT - 1 and c == 1):
                            mm.then_inc(unit_used, 1)
                        if k == FT - 1 and c == 0:
                            mm.then_inc(readies[e], 1)

            def proj_tile(load, load_e, c, dst, ready, middle=lambda: None):
                for u in range(2):
                    a, b = unit_cols(load, u)
                    if c == 0:
                        pe.wait_ge(w_split, 2 * load_e + u + 1)
                    cols = slice(c * P, (c + 1) * P)
                    for k in range(4):
                        mm = mm3(dst, a[:, k, cols], b[:, k, cols], hh[:, 4 * u + k, :], hl[:, 4 * u + k, :],
                                 start=(u == 0 and k == 0), stop=(u == 1 and k == 3))
                    if c == 1:
                        mm.then_inc(unit_used, 1)
                    if u == 0:
                        middle()
                if c == 0:
                    mm.then_inc(ready, 1)

            def rows_load(n, load, load_e, xs, first, last, order=range(FT), before=None):
                for m in order:
                    if before:
                        before(m)
                    for u in range(2):
                        if m == order[0]:
                            pe.wait_ge(w_split, 2 * load_e + u + 1)
                        s = (2 * load + u) % 4
                        xa, xb = xs(u)
                        mm = mm3(bank[m][:], wh[:, s, m * P:(m + 1) * P], wl[:, s, m * P:(m + 1) * P], xa, xb,
                                 start=(first and u == 0), stop=(last and u == 1))
                        if m == order[-1]:
                            mm.then_inc(unit_used, 1)
                    if last and m != order[-1]:
                        mm.then_inc(y_ready[n], 1)

            def ada(q):
                pe.wait_ge(ada_used, 8 * q + 8)
                for m in range(FT):
                    mm = pe.matmul(ADA[:, m:m + 1], ada_acc[:, m * P:(m + 1) * P], cst[:, C_ONE:C_ONE + 1], start=True, stop=True)
                mm.then_inc(ada_sum, 1)

            def norm(n):
                pe.wait_ge(sq_added, (FT - 2) * n + FT - 2)
                pe.wait_ge(sq_ready, FT * n + FT)
                for t in range(TT):
                    pe.matmul(ST[:, t:t + 1], nt[:, 0, t * P:(t + 1) * P], cst[:, C_ONE:C_ONE + 1], start=True, stop=False)
                    mm = pe.matmul(ST[:, t:t + 1], nt[:, 1 + (FT - 1) % 2, t * P:(t + 1) * P], cst[:, C_ONE:C_ONE + 1], start=False, stop=True)
                mm.then_inc(ms_ready, 1)
                pe.wait_ge(nD, 5 * n + 5)
                for t in range(TT):
                    mm = pe.transpose(RB[:, t * P:(t + 1) * P], rbs[:, t * P:(t + 1) * P], ident)
                mm.then_inc(rms_ready, 1)

            def stat(l, te, t, rows=P):
                pe.wait_ge(hsq_ready[l], te + 1)
                if t > 0:
                    pe.wait_ge(hD[l], 4 * te - 3)
                for j in range(TT):
                    mm = pe.matmul(ST[:, 2 * j:2 * j + 2], sqb[0:rows, t % 2, j * P:(j + 1) * P], cst[0:rows, C_BLOCK:C_BLOCK + 2],
                                   start=True, stop=True)
                mm.then_inc(hms_ready[l], 1)

            def spread(l, te):
                pe.wait_ge(hrs_ready[l], te + 1)
                pe.wait_ge(normed[l], te)
                for j in range(TT):
                    mm = pe.transpose(RB[:, j * P:(j + 1) * P], rbs[:, j * P:(j + 1) * P], ident)
                mm.then_inc(hrb_ready[l], 1)

            def v_load(l, load, load_e, emptied, middle=lambda: None):
                for u in range(2):
                    a, b = unit_cols(load, u)
                    pe.wait_ge(w_split, 2 * load_e + u + 1)
                    for t in range(TT):
                        if u == 0:
                            pe.wait_ge(taken[l], emptied(t))
                        tok = slice(t * P, (t + 1) * P)
                        for k in range(4):
                            kk = 4 * u + k
                            mm = mm3(bank[t][:, 0:256], hh[:, kk, tok], hl[:, kk, tok], a[:, k, :], b[:, k, :],
                                     start=(kk == 0), stop=(kk == 7))
                        if u == 1 and t < TT - 1:
                            mm.then_inc(v_ready[l], 1)
                    mm.then_inc(unit_used, 1)
                    if u == 0:
                        middle()

            def attention(l):
                def scores(i, s):
                    h, t = divmod(s, TT)
                    n = (t + 1) * P
                    if t == 0:
                        pe.wait_ge(s_low, 12 * i + 3 * h + 4)
                        pe.wait_ge(s_rest, 8 * i + 2 * h + 2)
                    S = bank[s % 4]
                    tok = slice(t * P, (t + 1) * P)
                    pe.matmul(S[:, 0:n], qA[:, h % 2, tok], kA[:, h % 2, 0:n], start=True, stop=False)
                    pe.matmul(S[:, 0:n], qB[:, h % 2, tok], kB[:, h % 2, 0:n], start=False, stop=False)
                    if l == 0:
                        mm = pe.matmul(S[:, t * P:n], ident_r[:], causal_r[:], start=False, stop=True)
                    else:
                        mm = pe.matmul(S[:, 0:n], ident_r[:], masked[:, t, 0:n], start=False, stop=True)
                    mm.then_inc(s_ready, 1)

                def wait_turned(i, s):
                    pe.wait_ge(pta_done if s % 2 else ptd_done, 8 * i + s // 2 + 1)

                def turn(i, s, first):
                    pe.wait_ge(p_ready, 16 * i + s + 1)
                    if s in (4, 12):
                        wait_turned(i, s - 1)
                    if s == 5 and not first:
                        pe.wait_ge(ol_done, 2 * i)
                    if s == 13:
                        pe.wait_ge(ol_done, 2 * i + 1)
                    for j in range(s % TT + 1):
                        mm = pe.transpose(turned_bank(s)[:, j * P:(j + 1) * P], probs[:, s % 4, j * P:(j + 1) * P], ident)
                    mm.then_inc(pt_ready, 1)

                def values(i, s, first):
                    h, t = divmod(s, TT)
                    wait_turned(i, s)
                    if t == 0 and (h >= 2 or not first):
                        pe.wait_ge(o_done, 4 * i + h - 1)
                    for j in range(t + 1):
                        vj = v0[:, j, ds(256 * i + HD * h, HD)] if l == 0 else v1[:, j, ds(HD * (i - 4), HD)]
                        mm = pe.matmul(bank[6 + h % 2][:, t * HD:(t + 1) * HD], probsT[:, s % 4, j * P:(j + 1) * P], vj,
                                       start=(j == 0), stop=(j == t))
                    mm.then_inc(pv_done, 1)

                def turn_pair(i, p):
                    pe.wait_ge(o_done, 4 * i + 2 * p + 2)
                    for t in range(TT):
                        mm = pe.transpose(pair_bank(p)[:, t * P:(t + 1) * P], oP[:, p, t, :], ident)
                    mm.then_inc(ot_ready, 1)

                def round_(i, first, last):
                    for s in range(16):
                        if s >= 2:
                            values(i, s - 2, first)
                        elif not first:
                            values(i - 1, s + 14, False)
                        turn(i, s, first)
                        if s < 13:
                            scores(i, s + 3)
                        elif not last:
                            scores(i + 1, s - 13)
                        if s == 3 and not first:
                            wait_turned(i, 2)
                            turn_pair(i - 1, 1)
                        if s == 11:
                            wait_turned(i, 10)
                            turn_pair(i, 0)

                if l == 0:
                    pe.wait_ge(ada_done, 7)
                for s in range(3):
                    scores(4 * l, s)
                round_(4 * l, True, False)
                with pe.Fori(4 * l + 1, 4 * l + 3) as i:
                    round_(i, False, False)
                i = 4 * l + 3
                round_(i, False, True)
                values(i, 14, False)
                values(i, 15, False)
                turn_pair(i, 1)

            def out_proj(l, load):
                def before(m):
                    if m == 4:
                        pe.wait_ge(ol_done, 8 * l + 8)
                for j in range(4):
                    rows_load(2 * l, load + j, load + j, lambda u: (hh[:, 2 * j + u, :], hl[:, 2 * j + u, :]), j == 0, j == 3,
                              order=[0, 1, 2, 3, 5, 6, 7, 4] if j == 0 else range(FT), before=before if j == 0 else None)

            def mlp_layer(l, up, dn):
                n = 2 * l + 1
                norm(n)

                def up_body(i, e):
                    proj_tile(up, up + 2 * i, 0, conv_banks(e)[0][:], a_ready[l])
                    proj_tile(up, up + 2 * i, 1, conv_banks(e)[1][:], None)
                    pe.wait_ge(uf_done[l], 2 * i)
                    proj_tile(up + 1, up + 2 * i + 1, 0, bank[2][:], g_ready[l])
                    proj_tile(up + 1, up + 2 * i + 1, 1, bank[3][:], None)

                first_loads(n, up, [bank[b][:] for b in range(4)], (a_ready[l], g_ready[l]))
                up_body(1, 1)
                if l == 0:
                    ada(7)
                with pe.Fori(1, 5) as j:
                    for e in range(2):
                        pe.wait_ge(conv_done[l], 4 * j + 2 * e - 2)
                        up_body(2 * j + e, e)
                    if l == 0:
                        ada(7 + j)
                pe.wait_ge(conv_done[l], 18)
                up_body(10, 0)

                def hidden(k):
                    return (uh[:, ds(k, 1), :].rearrange("p a n -> p (a n)"), ul[:, ds(k, 1), :].rearrange("p a n -> p (a n)"))

                def before(m):
                    if m == 4:
                        pe.wait_ge(conv_done[l], UT - 2)
                    if m == 0:
                        pe.wait_ge(uf_done[l], UT)

                if l == 0:
                    pe.wait_ge(ada_done, 12)
                pe.wait_ge(u_done[l], UT - 1)
                rows_load(n, dn, dn, lambda u: (uh[:, u, :], ul[:, u, :]), True, False, order=[4, 5, 6, 7, 0, 1, 2, 3], before=before)
                with pe.Fori(0, 4) as i:
                    for s in range(2):
                        rows_load(n, dn + 1 + s, dn + 1 + s + 2 * i, lambda u: hidden(4 * i + 2 + 2 * s + u), False, False)
                pe.wait_ge(u_done[l], UT + 1)
                for j in (9, 10):
                    rows_load(n, dn + j, dn + j, lambda u: (uh[:, 2 * j + u, :], ul[:, 2 * j + u, :]), False, j == 10)

            for s_ in (u_done[0], u_done[1]):
                pe.sem_inc(s_, 1)

            pe.wait_ge(cst_in, 16)
            pe.wait_ge(c_in, 32)
            pe.transpose(MISC[:, 2 * P:2 * P + V_ROWS], vrows[0:V_ROWS, 2, :], cst[0:V_ROWS, C_ID:C_ID + V_ROWS]).then_inc(vecT_ready, 1)
            pe.wait_ge(x_in, 16 * TT)
            for m in range(FT):
                if m >= 4:
                    pe.wait_ge(x_done[0], m - 3)
                for t in range(TT):
                    mm = pe.transpose(bank[m % 4][:, t * P:(t + 1) * P], xtok[:, t, m * P:(m + 1) * P], ident)
                mm.then_inc(xT_ready, 1)
            ada(0)
            pe.wait_ge(vec_in, 16 * (8 + 6))
            for j, rows in ((0, V_ROWS), (1, V_ROWS), (3, G_ROWS)):
                mm = pe.transpose(MISC[:, j * P:j * P + rows], vrows[0:rows, j, :], cst[0:rows, C_ID:C_ID + rows])
            mm.then_inc(vecT_ready, 1)
            ada(1)

            norm(0)
            pe.wait_ge(sm_ready[0], 8)

            def gate_logits(k):
                mm = mm3(MISC[:], smh0[:, k, :], sml0[:, k, :], hh[:, k, :], hl[:, k, :], k == 0, k == FT - 1)
                if k == FT - 1:
                    mm.then_inc(f_ready, 1)

            first_loads(0, 0, [bank[b][:] for b in range(4)], (tile_ready[0], tile_ready[0]), gate_logits)
            stat(0, 0, 0)

            def beat(te, t):
                stat(0, te, t)
                spread(0, te - 1)

            def fox_tile(i, c_, middle=lambda: None):
                pe.wait_ge(taken[0], 4 * i + c_ - 3)
                proj_tile(c_ // 2, 2 * i + c_ // 2, c_ % 2, bank[c_][:], tile_ready[0], middle)
                beat(4 * i + c_ - 1, c_ + 3)

            pe.wait_ge(taken[0], 1)
            proj_tile(0, 2, 0, bank[0][:], tile_ready[0], lambda: beat(1, 1))
            beat(2, 2)
            pe.wait_ge(taken[0], 2)
            proj_tile(0, 2, 1, bank[1][:], tile_ready[0], lambda: beat(3, 3))
            beat(4, 4)
            fox_tile(1, 2)
            fox_tile(1, 3)
            ada(2)
            with pe.Fori(2, 4) as i:
                for c_ in range(4):
                    fox_tile(i, c_)
                ada(1 + i)
            for j in range(4):
                v_load(0, j % 2, 8 + j, lambda t: 4 * j + 13 + t, (lambda: beat(15, 15)) if j == 0 else (lambda: None))
                if j == 0:
                    spread(0, 15)
                if j % 2:
                    ada(5 + j // 2)
            pe.wait_ge(taken[0], 32)
            pe.wait_ge(normed[0], 16)
            attention(0)
            out_proj(0, FOX_OUT)
            mlp_layer(0, FOX_UP, FOX_DOWN)

            norm(2)
            first_loads(2, DSA_IDX, [bank[b][:] for b in (1, 2, 3, 0)], (tile_ready[1], tile_ready[1]))
            pe.wait_ge(sm_ready[1], 1)
            for k in range(FT):
                mm = mm3(bank[7][0:HD + IH, :], smh1[:, k, :], sml1[:, k, :], hh[:, k, :], hl[:, k, :], k == 0, k == FT - 1)
            mm.then_inc(kidx_ready, 1)
            pe.wait_ge(wT_ready, 1)
            for t in range(TT):
                mm = pe.transpose(MISC[:, IH * t:IH * t + IH], wT[HD:HD + IH, t * P:(t + 1) * P], cst[HD:HD + IH, C_ID + HD:C_ID + HD + IH])
            mm.then_inc(w_ready, 1)
            stat(1, 0, 0, HD)
            spread(1, 0)
            pe.wait_ge(taken[1], 5)
            pe.wait_ge(normed[1], 1)
            pe.wait_ge(w_taken, 1)
            for e in range(3 * IH):
                h, t = e // 3, 1 + e % 3
                n = (t + 1) * P
                if e >= 4:
                    pe.wait_ge(relu_done, e - 3)
                tok = slice(t * P, (t + 1) * P)
                pe.matmul(bank[4 + e % 4][:, 0:n], qidx[:, h, tok], kidx[:, 0:n], start=True, stop=False)
                pe.matmul(bank[4 + e % 4][:, 0:n], qidx[:, h, tok], kidl[:, 0:n], start=False, stop=True).then_inc(is_ready, 1)
            for c_ in range(2):
                proj_tile(DSA_K, DSA_K, c_, bank[1 + c_][:], tile_ready[1])
            stat(1, 1, 1)
            with pe.Fori(0, 2) as i:
                for c_ in range(4):
                    pe.wait_ge(taken[1], 4 * i + c_ + 4)
                    proj_tile(DSA_Q + c_ // 2, DSA_Q + c_ // 2 + 2 * i, c_ % 2, bank[(3 + c_) % 4][:], tile_ready[1])
                    stat(1, 4 * i + c_ + 2, c_ + 2)
                    spread(1, 4 * i + c_ + 1)
            def last_beat():
                stat(1, 10, 10)
                spread(1, 9)
            v_load(1, DSA_V, DSA_V, lambda t: (13, 14, 15, 12)[t], last_beat)
            spread(1, 10)
            pe.wait_ge(taken[1], 19)
            pe.wait_ge(normed[1], 11)
            pe.wait_ge(relu_done, 3 * IH)
            pe.wait_ge(mask_ready, 4)
            attention(1)
            out_proj(1, DSA_OUT)
            mlp_layer(1, DSA_UP, DSA_DOWN)

            for m in range(FT):
                pe.wait_ge(x_done[4], m + 1)
                if m >= 4:
                    pe.wait_ge(oT_done, m - 3)
                for t in range(TT):
                    mm = pe.transpose(bank[m % 4][:, t * P:(t + 1) * P], xT[:, m, t * P:(t + 1) * P], ident)
                mm.then_inc(oT_ready, 1)

        @block.scalar
        def _(act):
            one = cst[:, C_ONE:C_ONE + 1]

            def squares(n, m):
                act.wait_ge(x_done[n], m + 1)
                if m >= 3:
                    act.wait_ge(sq_added, (FT - 2) * n + m - 2)
                act.activation(nt[:, 0 if m == 0 else 1 + m % 2, :], xT[:, m, :], ACT.Square).then_inc(sq_ready, 1)

            def root(steps_d, steps_a, n_d, cols):
                act.wait_ge(steps_d, n_d)
                act.activation(rt[:, 0:cols], rv[:, 0:cols], ACT.Sqrt).then_inc(steps_a, 1)

            def modulate(n):
                root(nD, nA, 5 * n + 1, TT)
                act.wait_ge(mul_ready, n + 1)
                shift = 3 * n
                for k in range(FT):
                    act.wait_ge(t_ready, FT * n + k + 1)
                    act.activation(hh[:, k, :], nt[:, k % 2, :], ACT.Identity, scale=mulA[:, n, k:k + 1],
                                   bias=mod[:, shift, k:k + 1]).then_inc(hh_ready, 1)

            def take(l, te, t, b, gain, sem_, count):
                act.wait_ge(sem_, count)
                if t >= 2:
                    act.wait_ge(hms_ready[l], te - 1)
                act.activation(sqb[:, t % 2, :], bank[b][:], ACT.Square).then_inc(hsq_ready[l], 1)
                if t >= 2:
                    act.wait_ge(normed[l], te - 1)
                act.activation(qg[:, t % 2, :], bank[b][:], ACT.Identity, scale=gain).then_inc(taken[l], 1)

            def attention(l):
                def probabilities(i, s):
                    n = (s % TT + 1) * P
                    act.wait_ge(max_done, 16 * i + s + 1)
                    act.activation(probs[:, s % 4, 0:n], bank[s % 4][:, 0:n], ACT.Exp, bias=nmax[:, s:s + 1],
                                   accum_out=rowsum[:, s:s + 1]).then_inc(p_ready, 1)

                def turned(i, s):
                    n = (s % TT + 1) * P
                    act.wait_ge(pt_ready, 16 * i + s + 1)
                    act.copy(probsT[:, s % 4, 0:n], turned_bank(s)[:, 0:n]).then_inc(pta_done, 1)

                def out_high(i, p):
                    act.wait_ge(ot_ready, 2 * i + p + 1)
                    act.copy(hh[:, ds(2 * (i - 4 * l) + p, 1), :], pair_bank(p)[:].rearrange("p (a n) -> p a n", a=1)).then_inc(oh_done, 1)

                def q_high(g, h):
                    act.copy(part(half(qA, h), h), head_tiles(l, g, h)[0]).then_inc(s_high, 1)

                def k_high(g, h):
                    act.copy(part(half(kA, h), h), head_tiles(l, g, h)[1]).then_inc(s_high, 1)

                def round_(i, first, last):
                    for s in range(16):
                        if s == 4 and not first:
                            out_high(i - 1, 1)
                        if s == 12:
                            out_high(i, 0)
                        if s % 2:
                            turned(i, s)
                        if s < 13:
                            probabilities(i, s + 3)
                        elif not last:
                            probabilities(i + 1, s - 13)
                        if s % 2 == 0 and (s < 8 or not last):
                            g, h = (i - 4 * l, 2 + s // 4) if s < 8 else (i - 4 * l + 1, s // 4 - 2)
                            if s % 4 == 0:
                                q_high(g, h)
                            else:
                                k_high(g, h)

                act.wait_ge(normed[l], 16 if l == 0 else 11)
                for h in range(2):
                    q_high(0, h)
                    k_high(0, h)
                for s in range(3):
                    probabilities(4 * l, s)
                round_(4 * l, True, False)
                with act.Fori(4 * l + 1, 4 * l + 3) as i:
                    round_(i, False, False)
                round_(4 * l + 3, False, True)
                out_high(4 * l + 3, 1)

            def mlp_layer(l, up):
                n = 2 * l + 1
                modulate(n)
                col = vec[:, l, :]

                def up_body(i, e):
                    for c_ in range(2):
                        if c_ == 0:
                            act.wait_ge(a_ready[l], i + 1)
                            act.wait_ge(u_done[l], 2 * i + 1)
                        else:
                            act.wait_ge(unit_used, 2 * (up + 2 * i) + 2)
                        tau = 2 * i + c_
                        act.activation(cv[:, c_, :], conv_banks(e)[c_][:], ACT.Identity, scale=col[:, ds(V_CONVW + 2 * UT + tau, 1)],
                                       bias=col[:, ds(V_CONVB + tau, 1)]).then_inc(tap2[l], 1)
                    for c_ in range(2):
                        act.wait_ge(conv_done[l], 2 * i + c_ + 1)
                        act.activation(cv[:, c_, :], cv[:, c_, :], ACT.Silu).then_inc(silu_done[l], 1)
                    for c_ in range(2):
                        act.wait_ge(uf_done[l], 2 * i + c_ + 1)
                        act.copy(uh[:, ds(2 * i + c_, 1), :], cv[:, c_:c_ + 1, :]).then_inc(uh_done[l], 1)

                with act.Fori(0, 5) as j:
                    for e in range(2):
                        up_body(2 * j + e, e)
                up_body(10, 0)

            act.wait_ge(vec_done, 1)
            act.activation(csil[:], vec[:, 2, V_C:V_ROWS], ACT.Silu).then_inc(csil_done, 1)
            for m in range(FT):
                act.wait_ge(xT_ready, m + 1)
                act.copy(xT[:, m, :], bank[m % 4][:]).then_inc(x_done[0], 1)
                squares(0, m)

            modulate(0)
            def fox_tile(i, c_, first):
                tau = 4 * i + c_
                sem_, count = (tile_ready[0], 2 * i + c_ // 2 + 1) if c_ % 2 == 0 else (unit_used, 2 * (2 * i + c_ // 2) + 2)
                take(0, tau, c_ if first else c_ + 4, c_, gains[:, ds(GAIN[0] + tau, 1)], sem_, count)
                if not (first and c_ == 0):
                    root(hD[0], hA[0], 4 * (tau - 1) + 1, 8)

            for c_ in range(4):
                fox_tile(0, c_, True)
            with act.Fori(1, 4) as i:
                for c_ in range(4):
                    fox_tile(i, c_, False)
            root(hD[0], hA[0], 4 * 15 + 1, 8)

            def take_v(l, je, load_e, dst, t):
                if t < TT - 1:
                    act.wait_ge(v_ready[l], 3 * je + t + 1)
                else:
                    act.wait_ge(unit_used, 2 * load_e + 2)
                act.copy(dst, bank[t][:, 0:256]).then_inc(taken[l], 1)

            for t in range(TT):
                take_v(0, 0, 8, v0[:, t, 0:256], t)
            act.wait_ge(f_ready, 1)
            act.activation(scr[:, 0, :], MISC[:], ACT.Identity, bias=vec[:, 3, G_BF:G_BF + 1]).then_inc(f_act, 1)
            act.wait_ge(f_act, 1)
            act.activation(scr[:, 1, :], scr[:, 0, :], ACT.Abs).then_inc(f_act, 1)
            act.wait_ge(f_act, 2)
            act.activation(scr[:, 2, :], scr[:, 1, :], ACT.Exp, scale=-1.0).then_inc(f_act, 1)
            act.wait_ge(f_act, 3)
            act.activation(scr[:, 3, :], scr[:, 2, :], ACT.Ln, bias=one).then_inc(f_act, 1)
            with act.Fori(1, 4) as j:
                for t in range(TT):
                    take_v(0, j, 8 + j, v0[:, t, ds(256 * j, 256)], t)
            attention(0)
            for m in range(FT):
                squares(1, m)
            mlp_layer(0, FOX_UP)
            for m in range(FT):
                squares(2, m)

            modulate(2)
            for j in range(2):
                for c_ in range(2):
                    if c_ == 0:
                        act.wait_ge(tile_ready[1], j + 1)
                    else:
                        act.wait_ge(unit_used, 2 * (DSA_IDX + j) + 2)
                    for h in (4 * j + 2 * c_, 4 * j + 2 * c_ + 1):
                        act.copy(half(qidx, h)[:, h, :], half(bank[(1 + 2 * j + c_) % 4], h)).then_inc(idx_high, 1)
            act.wait_ge(kidx_ready, 1)
            act.copy(wT[HD:HD + IH, :], bank[7][HD:HD + IH, :]).then_inc(wT_ready, 1)
            act.activation(sqb[0:HD, 0, :], bank[7][0:HD, :], ACT.Square).then_inc(hsq_ready[1], 1)
            act.activation(qg[0:HD, 0, :], bank[7][0:HD, :], ACT.Identity, scale=gains[0:HD, GAIN[1]:GAIN[1] + 1]).then_inc(taken[1], 1)
            root(hD[1], hA[1], 1, 8)
            for e in range(3 * IH):
                n = (2 + e % 3) * P
                act.wait_ge(is_ready, e + 1)
                if e >= 4:
                    act.wait_ge(weighed, e - 3)
                act.activation(scr[:, e % 4, 0:n], bank[4 + e % 4][:, 0:n], ACT.Relu).then_inc(relu_done, 1)
            take(1, 1, 1, 1, gains[:, GAIN[1] + 1:GAIN[1] + 2], tile_ready[1], 3)
            take(1, 2, 2, 2, gains[:, GAIN[1] + 2:GAIN[1] + 3], unit_used, 2 * DSA_K + 2)
            root(hD[1], hA[1], 5, 8)
            with act.Fori(0, 2) as i:
                for c_ in range(4):
                    tau = 4 * i + c_ + 3
                    sem_, count = (tile_ready[1], 2 * i + c_ // 2 + 4) if c_ % 2 == 0 else (unit_used, 2 * (DSA_Q + c_ // 2 + 2 * i) + 2)
                    take(1, tau, c_ + 3, (3 + c_) % 4, gains[:, ds(GAIN[1] + tau, 1)], sem_, count)
                    root(hD[1], hA[1], 4 * (tau - 1) + 1, 8)
            root(hD[1], hA[1], 4 * 10 + 1, 8)
            for t in range(TT):
                take_v(1, 0, DSA_V, v1[:, t, :], t)
            attention(1)
            for m in range(FT):
                squares(3, m)
            mlp_layer(1, DSA_UP)

        @block.vector
        def _(dve):
            def add_squares(n, m):
                dve.wait_ge(sq_ready, FT * n + m + 1)
                if m >= 2:
                    dve.wait_ge(sq_added, (FT - 2) * n + m - 1)
                dve.tensor_tensor(nt[:, 0, :], nt[:, 0, :], nt[:, 1 + m % 2, :], ALU.add).then_inc(sq_added, 1)

            def mean_square(ready, count, steps, cols, width):
                dve.wait_ge(ready, count)
                dve.tensor_scalar(rv[:, 0:cols], ST[:, 0:cols], 1.0 / width, EPS, ALU.mult, ALU.add).then_inc(steps, 1)

            def newton(steps_d, steps_a, d0, a0, cols, last):
                dve.wait_ge(steps_a, a0 + 1)
                dve.reciprocal(ry[:, 0:cols], rt[:, 0:cols]).then_inc(steps_d, 1)
                dve.wait_ge(steps_d, d0 + 2)
                dve.tensor_tensor(ra[:, 0:cols], ry[:, 0:cols], ry[:, 0:cols], ALU.mult).then_inc(steps_d, 1)
                dve.wait_ge(steps_d, d0 + 3)
                dve.scalar_tensor_tensor(out=rb2[:, 0:cols], in0=ra[:, 0:cols], scalar=-0.5, in1=rv[:, 0:cols],
                                         op0=ALU.mult, op1=ALU.mult).then_inc(steps_d, 1)
                dve.wait_ge(steps_d, d0 + 4)
                wide = [P, cols, L // cols]
                dve.scalar_tensor_tensor(out=rbs[:].rearrange("p (a b) -> p a b", a=cols),
                                         in0=rb2[:, 0:cols].unsqueeze(2).to_broadcast(wide), scalar=1.5,
                                         in1=ry[:, 0:cols].unsqueeze(2).to_broadcast(wide),
                                         op0=ALU.add, op1=ALU.mult).then_inc(last, 1)

            def modulate(n):
                l, scale = n // 2, 3 * n + 1
                gain = vec[:, l, V_GMIX:V_GFFN] if n % 2 == 0 else vec[:, l, V_GFFN:V_ROWS]
                dve.wait_ge(ada_done, scale + 1)
                dve.scalar_tensor_tensor(out=mulA[:, n, :], in0=mod[:, scale, :], scalar=1.0, in1=gain,
                                         op0=ALU.add, op1=ALU.mult).then_inc(mul_ready, 1)
                mean_square(ms_ready, n + 1, nD, TT, float(D))
                newton(nD, nA, 5 * n, n, TT, nD)
                dve.wait_ge(rms_ready, n + 1)
                shift = 3 * n
                for k in range(FT + 1):
                    if k < FT:
                        if k >= 2:
                            dve.wait_ge(hh_ready, FT * n + k - 1)
                        dve.tensor_tensor(nt[:, k % 2, :], xT[:, k, :], RB[:], ALU.mult).then_inc(t_ready, 1)
                        dve.wait_ge(t_ready, FT * n + k + 1)
                        if k >= 2:
                            dve.wait_ge(h_ready, FT * n + k - 1)
                        dve.tensor_scalar(nt[:, 2 + k % 2, :], nt[:, k % 2, :], mulA[:, n, k:k + 1], mod[:, shift, k:k + 1],
                                          ALU.mult, ALU.add).then_inc(hf_ready, 1)
                    if k >= 1:
                        dve.wait_ge(hh_ready, FT * n + k)
                        dve.wait_ge(hf_ready, FT * n + k)
                        dve.tensor_tensor(hl[:, k - 1, :], nt[:, 2 + (k - 1) % 2, :], hh[:, k - 1, :].bitcast(F32),
                                          ALU.subtract).then_inc(h_ready, 1)

            def residual(n, last_unit):
                gate = 6 * (n // 2) + (2 if n % 2 == 0 else 5)
                dve.wait_ge(ada_done, gate + 1)
                for m in range(FT):
                    if m < FT - 1:
                        dve.wait_ge(y_ready[n], m + 1)
                    else:
                        dve.wait_ge(unit_used, last_unit)
                    dve.scalar_tensor_tensor(out=xT[:, m, :], in0=bank[m][:], scalar=mod[:, gate, m:m + 1], in1=xT[:, m, :],
                                             op0=ALU.mult, op1=ALU.add).then_inc(x_done[n + 1], 1)
                    if n < 3 and m >= 2:
                        add_squares(n + 1, m - 1)

            def ada_slice(q, k, start=False):
                src = ada_slot(k, start)
                dve.wait_ge(ada_in[k % 4], 16 * (2 * q + k // 4 + 1))
                if k == 0:
                    dve.tensor_scalar(ada_acc[:], src, csil[:, 0:1], None, ALU.mult).then_inc(ada_used, 1)
                else:
                    dve.wait_ge(ada_used, 8 * q + k)
                    dve.scalar_tensor_tensor(out=ada_acc[:], in0=src, scalar=csil[:, k:k + 1], in1=ada_acc[:],
                                             op0=ALU.mult, op1=ALU.add).then_inc(ada_used, 1)

            def ada_out(l, q, part):
                dve.wait_ge(ada_sum, q + 1)
                bias = vec[:, 2, V_BADA + 48 * l:V_BADA + 48 * l + 48].rearrange("p (q m) -> p q m", q=6)[:, ds(part, 1), :]
                dve.tensor_tensor(mod[:, ds(q, 1), :], ADA[:, 0:FT].rearrange("p (a m) -> p a m", a=1), bias, ALU.add).then_inc(ada_done, 1)

            def finish_tile(l, te, t, dst):
                dve.wait_ge(hrb_ready[l], te + 1)
                return dve.tensor_tensor(dst, qg[:, t % 2:t % 2 + 1, :], RB[:].rearrange("p (a n) -> p a n", a=1), ALU.mult).then_inc(normed[l], 1)

            def head_stats(l, te):
                mean_square(hms_ready[l], te + 1, hD[l], 8, float(HD))

            def head_newton(l, te):
                newton(hD[l], hA[l], 4 * te, te, 8, hrs_ready[l])

            def bias_rows(l):
                b = bias_step[l]
                dve.tensor_copy(cumh[:], cum[:]).then_inc(b, 1)
                dve.wait_ge(b, 1)
                dve.tensor_tensor(scr[:, 0, :], cum[:], cumh[:].bitcast(F32), ALU.subtract).then_inc(b, 1)
                dve.wait_ge(b, 2)
                dve.tensor_scalar(scr[:, 1, :], scr[:, 0, :], cst[:, C_ODD:C_ODD + 1], None, ALU.mult).then_inc(b, 1)
                dve.wait_ge(b, 3)
                dve.scalar_tensor_tensor(out=scr[:, 0, :], in0=cumh[:].bitcast(F32), scalar=cst[:, C_EVEN:C_EVEN + 1],
                                         in1=scr[:, 1, :], op0=ALU.mult, op1=ALU.add).then_inc(b, 1)
                dve.wait_ge(b, 4)
                for r in (0, 64):
                    dve.tensor_copy(biasq[r:r + 32, :], scr[r:r + 32, 0, :])
                    dve.tensor_scalar(biasq[r + 32:r + 64, :], cst[r + 32:r + 64, C_ONE:C_ONE + 1].to_broadcast([32, L]), 1.0, None, ALU.mult)
                    dve.memset(biask[r:r + 32, :], 1.0)
                    op = dve.tensor_scalar(biask[r + 32:r + 64, :], scr[r + 32:r + 64, 0, :], -1.0, None, ALU.mult)
                op.then_inc(b, 1)
                dve.wait_ge(b, 5)

            def attention(l):
                def head_rest(i, h):
                    q = head_tiles(l, i - 4 * l, h)[0]
                    dve.wait_ge(s_high, 8 * i + 2 * h + 1)
                    dve.tensor_tensor(part(other(qA, h), h), q, part(half(qA, h), h).bitcast(F32), ALU.subtract).then_inc(s_rest, 1)
                    dve.tensor_scalar(other(kB, h)[:, h % 2, :], other(biask, h), other(cst, h)[:, ds(C_HEAD + 4 * (i - 4 * l) + h, 1)], None,
                                      ALU.mult).then_inc(s_rest, 1)

                def row_max(i, s):
                    n = (s % TT + 1) * P
                    dve.wait_ge(s_ready, 16 * i + s + 1)
                    dve.tensor_reduce(nmax[:, s:s + 1], bank[s % 4][:, 0:n], AX_X, ALU.max, negate=True).then_inc(max_done, 1)

                def turned(i, s):
                    n = (s % TT + 1) * P
                    dve.wait_ge(pt_ready, 16 * i + s + 1)
                    dve.tensor_copy(probsT[:, s % 4, 0:n], turned_bank(s)[:, 0:n]).then_inc(ptd_done, 1)

                def head_out(i, h):
                    dve.wait_ge(pv_done, 16 * i + 4 * h + 4)
                    dve.reciprocal(rrec[:, 4 * h:4 * h + 4], rowsum[:, 4 * h:4 * h + 4]).then_inc(rec_done, 1)
                    dve.wait_ge(rec_done, 4 * i + h + 1)
                    dve.tensor_tensor(oP[:, h // 2, :, HD * (h % 2):HD * (h % 2) + HD],
                                      bank[6 + h % 2][:, 0:4 * HD].rearrange("p (t d) -> p t d", t=TT),
                                      rrec[:, 4 * h:4 * h + 4].unsqueeze(2).to_broadcast([P, TT, HD]), ALU.mult).then_inc(o_done, 1)

                def out_low(i, p):
                    dve.wait_ge(oh_done, 2 * i + p + 1)
                    dve.tensor_tensor(hl[:, ds(2 * (i - 4 * l) + p, 1), :], pair_bank(p)[:].rearrange("p (a n) -> p a n", a=1),
                                      hh[:, ds(2 * (i - 4 * l) + p, 1), :].bitcast(F32), ALU.subtract).then_inc(ol_done, 1)

                def round_(i, first, last):
                    for s in range(16):
                        if s % 2 == 0:
                            turned(i, s)
                        if s == 4 and not first:
                            out_low(i - 1, 1)
                        if s == 12:
                            out_low(i, 0)
                        if s < 13:
                            row_max(i, s + 3)
                        elif not last:
                            row_max(i + 1, s - 13)
                        if s == 1 and not first:
                            head_out(i - 1, 3)
                        if s in (5, 9, 13):
                            head_out(i, (s - 5) // 4)
                        if s in (2, 6):
                            head_rest(i, 2 + s // 4)
                        if s in (10, 14) and not last:
                            head_rest(i + 1, s // 4 - 2)

                i = 4 * l
                dve.wait_ge(normed[l], 16 if l == 0 else 11)
                for h in range(2):
                    dve.tensor_copy(other(qB, h)[:, h, :], other(biasq, h))
                    head_rest(i, h)
                for s in range(3):
                    row_max(i, s)
                round_(i, True, False)
                with dve.Fori(4 * l + 1, 4 * l + 3) as i:
                    round_(i, False, False)
                i = 4 * l + 3
                round_(i, False, True)
                head_out(i, 3)
                out_low(i, 1)

            def mlp_layer(l, up, last_unit):
                n = 2 * l + 1
                modulate(n)
                col = vec[:, l, :]

                def up_body(i, e, slices=lambda: None):
                    for c_ in range(2):
                        tau = 2 * i + c_
                        dve.wait_ge(tap2[l], tau + 1)
                        dve.scalar_tensor_tensor(out=cv[:, c_, 1:L], in0=conv_banks(e)[c_][:, 0:L - 1], scalar=col[:, ds(V_CONVW + UT + tau, 1)],
                                                 in1=cv[:, c_, 1:L], op0=ALU.mult, op1=ALU.add).then_inc(tap1[l], 1)
                        dve.wait_ge(tap1[l], tau + 1)
                        dve.scalar_tensor_tensor(out=cv[:, c_, 2:L], in0=conv_banks(e)[c_][:, 0:L - 2], scalar=col[:, ds(V_CONVW + tau, 1)],
                                                 in1=cv[:, c_, 2:L], op0=ALU.mult, op1=ALU.add).then_inc(conv_done[l], 1)
                    slices()
                    for c_ in range(2):
                        tau = 2 * i + c_
                        dve.wait_ge(silu_done[l], tau + 1)
                        if c_ == 0:
                            dve.wait_ge(g_ready[l], i + 1)
                        else:
                            dve.wait_ge(unit_used, 2 * (up + 2 * i + 1) + 2)
                        dve.tensor_tensor(cv[:, c_, :], cv[:, c_, :], bank[2 + c_][:], ALU.mult).then_inc(uf_done[l], 1)
                        dve.wait_ge(uh_done[l], tau + 1)
                        dve.tensor_tensor(ul[:, ds(tau, 1), :], cv[:, c_:c_ + 1, :], uh[:, ds(tau, 1), :].bitcast(F32),
                                          ALU.subtract).then_inc(u_done[l], 1)

                with dve.Fori(0, 5) as j:
                    for e in range(2):
                        if l == 0:
                            up_body(2 * j + e, e, lambda: [ada_slice(7 + j, k) for k in range(4 * e, 4 * e + 4)])
                        else:
                            up_body(2 * j + e, e)
                    if l == 0:
                        ada_out(1, 7 + j, 1 + j)
                up_body(10, 0)
                residual(n, last_unit)

            dve.wait_ge(cst_in, 16)
            dve.tensor_copy(ident_r[:], ident)
            dve.tensor_copy(causal_r[:], cst[:, C_CAUSAL:C_CAUSAL + P]).then_inc(cst_done, 1)
            dve.wait_ge(vecT_ready, 1)
            dve.tensor_copy(vec[:, 2, 0:V_ROWS], MISC[:, 2 * P:2 * P + V_ROWS]).then_inc(vec_done, 1)
            dve.wait_ge(csil_done, 1)
            for k in range(FT):
                ada_slice(0, k, start=True)
            ada_out(0, 0, 0)
            for m in range(1, FT - 1):
                add_squares(0, m)
            dve.wait_ge(vecT_ready, 2)
            for j, rows in ((0, V_ROWS), (1, V_ROWS), (3, G_ROWS)):
                dve.tensor_copy(vec[:, j, 0:rows], MISC[:, j * P:j * P + rows]).then_inc(vec_done, 1)
            dve.wait_ge(vec_done, 4)

            def gain_cols(at, n, row, scale):
                return dve.tensor_scalar(gains[:, at:at + n], vec[:, 3, row:row + 1].to_broadcast([P, n]), scale, None, ALU.mult)
            gain_cols(GAIN[0], 8, G_FOXQ, HD ** -0.5)
            gain_cols(GAIN[0] + 8, 8, G_FOXK, 1.0)
            gain_cols(GAIN[1], 1, G_KIDX, 1.0)
            gain_cols(GAIN[1] + 1, 2, G_DSAK, 1.0)
            gain_cols(GAIN[1] + 3, 8, G_DSAQ, HD ** -0.5).then_inc(cst_done, 1)
            for k in range(FT):
                ada_slice(1, k, start=True)
            ada_out(0, 1, 1)
            dve.wait_ge(sm_in[0], 16)
            for r in range(8):
                dve.tensor_copy(smh0[:, :, r * NH:(r + 1) * NH], smr0[:]).then_inc(sm_hi[0], 1)
            dve.wait_ge(sm_hi[0], 8)
            for r in range(8):
                dve.tensor_tensor(sml0[:, :, r * NH:(r + 1) * NH], smr0[:], smh0[:, :, r * NH:(r + 1) * NH].bitcast(F32),
                                  ALU.subtract).then_inc(sm_ready[0], 1)

            modulate(0)
            def forget_gates():
                dve.wait_ge(f_act, 4)
                dve.tensor_scalar(scr[:, 0, :], scr[:, 0, :], 0.0, None, ALU.min).then_inc(f_dve, 1)
                dve.wait_ge(f_dve, 1)
                dve.tensor_tensor(scr[:, 1, :], scr[:, 0, :], scr[:, 3, :], ALU.subtract).then_inc(f_dve, 1)
                dve.memset(scr[:, 2, :], 1.0).then_inc(f_dve, 1)
                dve.wait_ge(f_dve, 3)
                dve.tensor_tensor_scan(cum[:], scr[:, 2, :], scr[:, 1, :], 0.0, ALU.mult, ALU.add).then_inc(f_dve, 1)
                dve.wait_ge(f_dve, 4)
                bias_rows(0)

            def fox_body(i, slices, first=False):
                for c_ in range(4):
                    tau = 4 * i + c_
                    if not (first and c_ == 0):
                        head_stats(0, tau - 1)
                    if not (first and c_ < 2):
                        finish_tile(0, tau - 2, c_, qk[:, ds(tau - 2, 1), :])
                    if not (first and c_ == 0):
                        head_newton(0, tau - 1)
                    for k in slices[c_]:
                        ada_slice(1 + i, k)
                if not first:
                    ada_out(0, 1 + i, 1 + i)

            for k in range(4):
                ada_slice(2, k)
            fox_body(0, ((), (), (), ()), first=True)
            fox_body(1, ((4, 5), (6, 7), (), ()))
            with dve.Fori(2, 4) as i:
                fox_body(i, ((0, 1, 2), (3, 4, 5), (6, 7), ()))
            head_stats(0, 15)
            finish_tile(0, 14, 14, qk[:, 14:15, :])
            head_newton(0, 15)
            for i in range(2):
                for k in range(FT):
                    ada_slice(5 + i, k)
                    if (i, k) == (0, 3):
                        finish_tile(0, 15, 15, qk[:, 15:16, :])
                ada_out(i, 5 + i, 5 * (1 - i))
                if i == 0:
                    forget_gates()
            attention(0)
            residual(0, 2 * (FOX_OUT + 3) + 2)
            mlp_layer(0, FOX_UP, 2 * (FOX_DOWN + 10) + 2)

            modulate(2)
            dve.wait_ge(sm_in[1], 16)
            dve.tensor_copy(smh1[:], smr1[:]).then_inc(sm_hi[1], 1)
            dve.wait_ge(sm_hi[1], 1)
            dve.tensor_tensor(sml1[:], smr1[:], smh1[:].bitcast(F32), ALU.subtract).then_inc(sm_ready[1], 1)
            dve.wait_ge(alibi_in, 16)
            bias_rows(1)
            for h in range(IH):
                dve.wait_ge(idx_high, h + 1)
                op = dve.tensor_tensor(other(qidx, h)[:, h, :], half(bank[(1 + h // 2) % 4], h), half(qidx, h)[:, h, :].bitcast(F32), ALU.subtract)
                if h % 2:
                    op.then_inc(taken[1], 1)
            dve.wait_ge(w_ready, 1)
            dve.tensor_scalar(widx[:], MISC[:, 0:TT * IH], IH ** -0.5 * HD ** -0.5, None, ALU.mult).then_inc(w_taken, 1)
            dve.wait_ge(w_taken, 1)
            head_stats(1, 0)
            head_newton(1, 0)
            dve.wait_ge(hrb_ready[1], 1)
            for e in range(2):
                op = dve.tensor_tensor(kfull[e * HD:(e + 1) * HD, :], qg[0:HD, 0, :], RB[0:HD, :], ALU.mult)
            op.then_inc(key_step, 1)
            dve.wait_ge(key_step, 1)
            dve.tensor_copy(kidx, kfull).then_inc(key_step, 1)
            dve.wait_ge(key_step, 2)
            dve.tensor_tensor(kidl, kfull, kidx.bitcast(F32), ALU.subtract).then_inc(normed[1], 1)
            for e in range(3 * IH):
                h, t = e // 3, 1 + e % 3
                n = (t + 1) * P
                w_col = widx[:, IH * t + h:IH * t + h + 1]
                dve.wait_ge(relu_done, e + 1)
                if h == 0:
                    dve.tensor_scalar(score[:, t - 1, 0:n], scr[:, e % 4, 0:n], w_col, 0.0, ALU.mult, ALU.add).then_inc(weighed, 1)
                else:
                    dve.wait_ge(weighed, e - 2)
                    dve.scalar_tensor_tensor(out=score[:, t - 1, 0:n], in0=scr[:, e % 4, 0:n], scalar=w_col,
                                             in1=score[:, t - 1, 0:n], op0=ALU.mult, op1=ALU.add).then_inc(weighed, 1)
            dve.wait_ge(weighed, 3 * IH)
            for t in range(1, TT):
                dve.tensor_tensor(score[:, t - 1, t * P:(t + 1) * P], score[:, t - 1, t * P:(t + 1) * P],
                                  cst[:, C_CAUSAL:C_CAUSAL + P], ALU.add).then_inc(tk, 1)

            def top_round(r):
                for t in range(3):
                    n = (t + 2) * P
                    dve.wait_ge(tk, 6 * r + 1 + t)
                    dve.max(top8[:, t, :], score[:, t, 0:n]).then_inc(tk, 1)
                for t in range(3):
                    n = (t + 2) * P
                    dve.wait_ge(tk, 6 * r + 4 + t)
                    dve.match_replace(score[:, t, 0:n], top8[:, t, :], score[:, t, 0:n], TAKEN).then_inc(tk, 1)

            for r in range(3):
                top_round(r)
            head_stats(1, 1)
            head_newton(1, 1)

            def key_heads(te, p):
                dve.wait_ge(hrb_ready[1], te + 1)
                for g in range(2):
                    src = slice(g * HD, (g + 1) * HD)
                    for e in range(2):
                        op = dve.tensor_tensor(qk[e * HD:(e + 1) * HD, 8 + 2 * p + g, :], qg[src, te % 2, :], RB[src, :], ALU.mult)
                op.then_inc(normed[1], 1)

            def dsa_slot(i, c_, first):
                tau = 4 * i + c_ + 3
                head_stats(1, tau - 1)
                if first and c_ < 2:
                    key_heads(tau - 2, tau - 3)
                else:
                    finish_tile(1, tau - 2, c_ + 1, qk[:, ds(tau - 5, 1), :])
                head_newton(1, tau - 1)
                for r in ((3,), (4, 5), (6, 7), (8,))[c_]:
                    top_round(6 * i + r)

            for c_ in range(4):
                dsa_slot(0, c_, True)
            with dve.Fori(1, 2) as i:
                for c_ in range(4):
                    dsa_slot(i, c_, False)
            head_stats(1, 10)
            finish_tile(1, 9, 9, qk[:, 6:7, :])
            head_newton(1, 10)
            finish_tile(1, 10, 10, qk[:, 7:8, :])
            top_round(15)
            dve.tensor_copy(masked[:, 0, 0:P], cst[:, C_CAUSAL:C_CAUSAL + P]).then_inc(mask_ready, 1)
            dve.wait_ge(tk, 3 + 6 * (TOPK // 8))
            for t in range(1, TT):
                n = (t + 1) * P
                dve.tensor_scalar(masked[:, t, 0:n], score[:, t - 1, 0:n], TAKEN, MASKED, ALU.not_equal, ALU.mult).then_inc(mask_ready, 1)
            attention(1)
            residual(2, 2 * (DSA_OUT + 3) + 2)
            mlp_layer(1, DSA_UP, 2 * (DSA_DOWN + 10) + 2)

            for m in range(FT):
                dve.wait_ge(oT_ready, m + 1)
                dve.tensor_copy(outs[:, :, m * P:(m + 1) * P], bank[m % 4][:].rearrange("p (t d) -> p t d", t=TT)).then_inc(oT_done, 1)


_INS = ["x", "c", "w_ada", "b_ada", "g_norm_mix", "g_norm_ffn", "fox_w_in", "fox_b_f", "fox_g_q", "fox_g_k",
        "fox_w_out", "dsa_w_in", "dsa_g_q", "dsa_g_k", "dsa_g_kidx", "dsa_w_out", "ffn_w_up", "ffn_conv_w",
        "ffn_conv_b", "ffn_w_down"]


def shape_constants():
    import numpy as np
    t = np.zeros((P, C_N), np.float32)
    p = np.arange(P)
    t[:, C_ID:C_ID + P] = np.eye(P)
    t[:, C_CAUSAL:C_CAUSAL + P] = np.where(p[None, :] > p[:, None], MASKED, 0.0)
    t[:, C_BLOCK] = p < HD
    t[:, C_BLOCK + 1] = p >= HD
    t[:, C_EVEN] = p % 32 < NH
    t[:, C_ODD] = p % 32 >= NH
    t[:, C_HEAD:C_HEAD + NH] = p[:, None] % NH == np.arange(NH)[None, :]
    t[:, C_ONE] = 1.0
    t[:, C_EPS] = EPS
    slopes = np.exp2(-8.0 * np.arange(1, NH + 1, dtype=np.float32) / np.float32(NH)).astype(np.float32)
    alibi = -slopes[p % NH][:, None] * np.arange(L, dtype=np.float32)[None, :]
    return t, alibi.astype(np.float32)


def kernel(**inputs):
    import numpy as _np
    import concourse.bacc as _bacc
    from concourse import mybir as _mybir
    from concourse.bass_utils import run_bass_kernel_spmd as _run

    nc = _bacc.Bacc("TRN2", target_bir_lowering=False, num_devices=1, dynamic_dma_scratch_size=2048)
    arrays, args = {}, []
    for name, a in [(n, inputs[n]) for n in _INS] + list(zip(("consts", "alibi"), shape_constants())):
        a = _np.ascontiguousarray(a)
        arrays[f"in_{name}_dram"] = a
        args.append(nc.dram_tensor(f"in_{name}_dram", a.shape, _mybir.dt.from_np(a.dtype), kind="ExternalInput").ap())
    args.append(nc.dram_tensor("out_dram", (1, L, D), _mybir.dt.float32, kind="ExternalOutput").ap())
    two_layers(nc, *args)
    r = _run(nc, [arrays], core_ids=[0])
    return r.results[0]["out_dram"]
```
